# Optimizing a Trainium2 kernel written in Bass

```python
import math
import jax
import jax.numpy as jnp
from jax import lax
import numpy as np
import jax, jax.numpy as jnp

D_MODEL = 1024
BATCH = 1
SEQ = 256
DEPTH = 2

CHUNK = 64
Q_BLOCK = 128
LN_EPS = 1e-5
DEEPNORM_ALPHA = (2 * DEPTH) ** 0.25
DEEPNORM_BETA = (8 * DEPTH) ** -0.25

D_FF = 2816
FFN_RES = 0.5

H_A = 8
HD_A = 64
ROT_A = HD_A // 4
ROPE_THETA = 500000.0
A_W = H_A * 2 * HD_A

H_B = 16
P_B = 64
D_INNER = H_B * P_B
G_B = 2
N_B = 128
CONV_B = 4
CONV_DIM = D_INNER + 2 * G_B * N_B

H_C = 16
HD_C = 64
C_W = H_C * HD_C

N_BRANCH = 3
BR_W = 1024

_SEGMENTS = (A_W, A_W, A_W, D_INNER, CONV_DIM, H_B, C_W, C_W, C_W, N_BRANCH * D_MODEL)
SPLIT_POINTS = tuple(int(v) for v in np.cumsum(_SEGMENTS)[:-1])
N_IN = int(sum(_SEGMENTS))


def _layernorm(x, g, b):
    xf = x.astype(jnp.float32)
    mu = jnp.mean(xf, -1, keepdims=True)
    xc = xf - mu
    var = jnp.mean(xc * xc, -1, keepdims=True)
    y = xc * lax.rsqrt(var + LN_EPS) * g.astype(jnp.float32) + b.astype(jnp.float32)
    return y.astype(x.dtype)

def _rmsnorm(x, g):
    xf = x.astype(jnp.float32)
    y = xf * lax.rsqrt(jnp.mean(xf * xf, -1, keepdims=True) + LN_EPS)
    return (y * g.astype(jnp.float32)).astype(x.dtype)

def _swiglu(x, w_in, w_out):
    gate, up = jnp.split(x @ w_in, 2, axis=-1)
    return (jax.nn.silu(gate) * up) @ w_out

def _rotary_tables(s):
    half = ROT_A // 2
    inv_freq = ROPE_THETA ** (-jnp.arange(half, dtype=jnp.float32) * 2.0 / ROT_A)
    ang = jnp.arange(s, dtype=jnp.float32)[:, None] * inv_freq[None, :]
    return jnp.cos(ang), jnp.sin(ang)

def _apply_partial_rope(x, cos, sin):
    half = ROT_A // 2
    c = cos.reshape(cos.shape[0], 1, 1, half).astype(x.dtype)
    sn = sin.reshape(sin.shape[0], 1, 1, half).astype(x.dtype)
    x1 = x[..., :half]
    x2 = x[..., half:ROT_A]
    return jnp.concatenate([x1 * c - x2 * sn, x2 * c + x1 * sn, x[..., ROT_A:]], axis=-1)

def _diff_attention(qa, ka, va, lam, subln_g, layer):
    b, s, _ = qa.shape
    nb = s // Q_BLOCK
    cos, sin = _rotary_tables(s)
    q = _apply_partial_rope(qa.reshape(b, s, H_A, 2, HD_A), cos, sin)
    k = _apply_partial_rope(ka.reshape(b, s, H_A, 2, HD_A), cos, sin)
    v = va.reshape(b, s, H_A, 2 * HD_A)
    lam_init = 0.8 - 0.6 * math.exp(-0.3 * layer)
    lf = lam.astype(jnp.float32)
    lam_full = jnp.exp(jnp.sum(lf[0] * lf[1])) - jnp.exp(jnp.sum(lf[2] * lf[3])) + lam_init
    kpos = jnp.arange(s)
    kchunk = kpos // CHUNK
    qpos = kpos.reshape(nb, Q_BLOCK)
    qb = jnp.moveaxis(q.reshape(b, nb, Q_BLOCK, H_A, 2, HD_A), 1, 0)
    scale = HD_A ** -0.5

    def block(args):
        qblk, qp = args
        sc = jnp.einsum('bqhmd,bkhmd->bhmqk', qblk, k).astype(jnp.float32) * scale
        allowed = kchunk[None, :] <= (qp // CHUNK)[:, None]
        p = jax.nn.softmax(jnp.where(allowed, sc, -jnp.inf), axis=-1)
        w = p[:, :, 0] - lam_full * p[:, :, 1]
        return jnp.einsum('bhqk,bkhe->bqhe', w.astype(v.dtype), v)

    out = lax.map(block, (qb, qpos))
    out = jnp.moveaxis(out, 0, 1).reshape(b, s, H_A, 2 * HD_A)
    out = _rmsnorm(out, subln_g) * (1.0 - lam_init)
    return out.reshape(b, s, A_W)

def _stick_breaking(qc, kc, vc):
    b, s, _ = qc.shape
    nb = s // Q_BLOCK
    k = kc.reshape(b, s, H_C, HD_C)
    v = vc.reshape(b, s, H_C, HD_C)
    qb = jnp.moveaxis(qc.reshape(b, nb, Q_BLOCK, H_C, HD_C), 1, 0)
    kpos = jnp.arange(s)
    qpos = kpos.reshape(nb, Q_BLOCK)
    scale = HD_C ** -0.5

    def block(args):
        qblk, qp = args
        z = jnp.einsum('bqhd,bkhd->bhqk', qblk, k).astype(jnp.float32) * scale
        strict = kpos[None, :] < qp[:, None]
        log_stay = jnp.where(strict, jax.nn.log_sigmoid(-z), 0.0)
        after = lax.cumsum(log_stay, axis=3, reverse=True) - log_stay
        a = jnp.where(strict, jnp.exp(jax.nn.log_sigmoid(z) + after), 0.0)
        return jnp.einsum('bhqk,bkhd->bqhd', a.astype(v.dtype), v)

    out = lax.map(block, (qb, qpos))
    return jnp.moveaxis(out, 0, 1).reshape(b, s, C_W)

def _ssd(x, dt, a_neg, bm, cm):
    b, s = x.shape[:2]
    nc = s // CHUNK
    hg = H_B // G_B
    xr = x.reshape(b, nc, CHUNK, G_B, hg, P_B)
    dtr = dt.reshape(b, nc, CHUNK, G_B, hg)
    br = bm.reshape(b, nc, CHUNK, G_B, N_B)
    cr = cm.reshape(b, nc, CHUNK, G_B, N_B)
    acum = jnp.cumsum(dtr * a_neg.reshape(G_B, hg), axis=2)
    xdt = xr * dtr[..., None]
    causal = jnp.tril(jnp.ones((CHUNK, CHUNK), dtype=bool))[None, None, :, :, None, None]
    seg = acum[:, :, :, None] - acum[:, :, None, :]
    decay = jnp.exp(jnp.where(causal, seg, -jnp.inf))
    cb = jnp.einsum('bctgn,bcsgn->bctsg', cr, br)
    y_diag = jnp.einsum('bctsgh,bcsghp->bctghp', cb[..., None] * decay, xdt)
    decay_to_end = jnp.exp(acum[:, :, -1:] - acum)
    states = jnp.einsum('bclgn,bclghp->bcghpn', br, xdt * decay_to_end[..., None])
    chunk_decay = jnp.exp(acum[:, :, -1])

    def step(h_prev, inp):
        st, dc = inp
        return h_prev * dc[..., None, None] + st, h_prev

    h0 = jnp.zeros((b, G_B, hg, P_B, N_B), jnp.float32)
    _, h_in = lax.scan(step, h0, (jnp.moveaxis(states, 1, 0), jnp.moveaxis(chunk_decay, 1, 0)))
    h_in = jnp.moveaxis(h_in, 0, 1)
    y_off = jnp.einsum('bclgn,bcghpn->bclghp', cr, h_in) * jnp.exp(acum)[..., None]
    return (y_diag + y_off).reshape(b, s, H_B, P_B)

def _mamba2(zb, xbc, dtb, conv_w, conv_b, dt_bias, a_log, d_skip, norm_g):
    b, s, _ = zb.shape
    xbc = lax.conv_general_dilated(
        xbc, conv_w[:, None, :], window_strides=(1,), padding=[(CONV_B - 1, 0)],
        dimension_numbers=('NWC', 'WIO', 'NWC'), feature_group_count=CONV_DIM) + conv_b
    xbc = jax.nn.silu(xbc).astype(jnp.float32)
    xs, bm, cm = jnp.split(xbc, [D_INNER, D_INNER + G_B * N_B], axis=-1)
    dt = jax.nn.softplus(dtb.astype(jnp.float32) + dt_bias.astype(jnp.float32))
    a_neg = -jnp.exp(a_log.astype(jnp.float32))
    xh = xs.reshape(b, s, H_B, P_B)
    y = _ssd(xh, dt, a_neg, bm.reshape(b, s, G_B, N_B), cm.reshape(b, s, G_B, N_B))
    y = y + d_skip.astype(jnp.float32)[:, None] * xh
    y = y.reshape(b, s, D_INNER) * jax.nn.silu(zb.astype(jnp.float32))
    y = _rmsnorm(y.reshape(b, s, G_B, D_INNER // G_B), norm_g.reshape(G_B, D_INNER // G_B))
    return y.reshape(b, s, D_INNER).astype(zb.dtype)

def _hybrid_mixer(h, layer, w_in, gate_bias, diff_lambda, diff_subln_g, conv_w, conv_b,
                  dt_bias, a_log, d_skip, norm_g, w_branch, w_out):
    b, s, _ = h.shape
    qa, ka, va, zb, xbc, dtb, qc, kc, vc, gpre = jnp.split(h @ w_in, SPLIT_POINTS, axis=-1)
    o_a = _diff_attention(qa, ka, va, diff_lambda, diff_subln_g, layer)
    o_b = _mamba2(zb, xbc, dtb, conv_w, conv_b, dt_bias, a_log, d_skip, norm_g)
    o_c = _stick_breaking(qc, kc, vc)
    branches = jnp.stack([o_a, o_b.astype(h.dtype), o_c], axis=2)
    proj = jnp.einsum('bsrc,rcd->bsrd', branches, w_branch)
    gates = jax.nn.sigmoid(gpre.reshape(b, s, N_BRANCH, D_MODEL) + gate_bias)
    merged = jnp.einsum('bsrd,bsrd->bsd', gates, proj)
    return merged @ w_out

def first_inputs(seed: int = 0) -> dict:
    key = jax.random.key(seed)
    ks = jax.random.split(key, 24)
    f32 = jnp.float32
    L = DEPTH

    def nrm(k, shape, scale):
        return jax.random.normal(k, shape, f32) * scale

    dt0 = jnp.exp(jax.random.uniform(ks[11], (L, H_B), f32, math.log(1e-3), math.log(1e-1)))
    return {
        'x': nrm(ks[0], (BATCH, SEQ, D_MODEL), 1.0),
        'ffn1_w_in': nrm(ks[1], (L, D_MODEL, 2 * D_FF), DEEPNORM_BETA * D_MODEL ** -0.5),
        'ffn1_w_out': nrm(ks[2], (L, D_FF, D_MODEL), DEEPNORM_BETA * D_FF ** -0.5),
        'ln1_g': 1.0 + nrm(ks[3], (L, D_MODEL), 0.02),
        'ln1_b': nrm(ks[4], (L, D_MODEL), 0.02),
        'w_mix_in': nrm(ks[5], (L, D_MODEL, N_IN), D_MODEL ** -0.5),
        'gate_bias': nrm(ks[6], (L, N_BRANCH, D_MODEL), 0.02),
        'diff_lambda': nrm(ks[7], (L, 4, HD_A), 0.1),
        'diff_subln_g': 1.0 + nrm(ks[8], (L, 2 * HD_A), 0.02),
        'ssm_conv_w': nrm(ks[9], (L, CONV_B, CONV_DIM), CONV_B ** -0.5),
        'ssm_conv_b': nrm(ks[10], (L, CONV_DIM), 0.02),
        'ssm_dt_bias': dt0 + jnp.log(-jnp.expm1(-dt0)),
        'ssm_A_log': jnp.log(jax.random.uniform(ks[12], (L, H_B), f32, 1.0, 16.0)),
        'ssm_D': 1.0 + nrm(ks[13], (L, H_B), 0.02),
        'ssm_norm_g': 1.0 + nrm(ks[14], (L, D_INNER), 0.02),
        'w_branch': nrm(ks[15], (L, N_BRANCH, BR_W, D_MODEL), DEEPNORM_BETA * BR_W ** -0.5),
        'w_mix_out': nrm(ks[16], (L, D_MODEL, D_MODEL), DEEPNORM_BETA * D_MODEL ** -0.5),
        'ln2_g': 1.0 + nrm(ks[17], (L, D_MODEL), 0.02),
        'ln2_b': nrm(ks[18], (L, D_MODEL), 0.02),
        'ffn2_w_in': nrm(ks[19], (L, D_MODEL, 2 * D_FF), DEEPNORM_BETA * D_MODEL ** -0.5),
        'ffn2_w_out': nrm(ks[20], (L, D_FF, D_MODEL), DEEPNORM_BETA * D_FF ** -0.5),
        'ln3_g': 1.0 + nrm(ks[21], (L, D_MODEL), 0.02),
        'ln3_b': nrm(ks[22], (L, D_MODEL), 0.02),
    }

def first_block(x, ffn1_w_in, ffn1_w_out, ln1_g, ln1_b, w_mix_in, gate_bias, diff_lambda,
              diff_subln_g, ssm_conv_w, ssm_conv_b, ssm_dt_bias, ssm_A_log, ssm_D, ssm_norm_g,
              w_branch, w_mix_out, ln2_g, ln2_b, ffn2_w_in, ffn2_w_out, ln3_g, ln3_b):
    for l in range(DEPTH):
        x = _layernorm(DEEPNORM_ALPHA * x + FFN_RES * _swiglu(x, ffn1_w_in[l], ffn1_w_out[l]),
                       ln1_g[l], ln1_b[l])
        mix = _hybrid_mixer(x, l, w_mix_in[l], gate_bias[l], diff_lambda[l], diff_subln_g[l],
                            ssm_conv_w[l], ssm_conv_b[l], ssm_dt_bias[l], ssm_A_log[l], ssm_D[l],
                            ssm_norm_g[l], w_branch[l], w_mix_out[l])
        x = _layernorm(DEEPNORM_ALPHA * x + mix, ln2_g[l], ln2_b[l])
        x = _layernorm(DEEPNORM_ALPHA * x + FFN_RES * _swiglu(x, ffn2_w_in[l], ffn2_w_out[l]),
                       ln3_g[l], ln3_b[l])
    return x


DEPTH_2 = 1

D_MIX = D_MODEL
HEAD_DIM = 64
GDN_HEADS = (D_MIX // 2) // HEAD_DIM
GDN_WIDTH = GDN_HEADS * HEAD_DIM
CONV_K = 4
SWA_Q_HEADS = (D_MIX // 2) // HEAD_DIM
SWA_KV_HEADS = 2
SWA_GROUP = SWA_Q_HEADS // SWA_KV_HEADS
SWA_Q_WIDTH = SWA_Q_HEADS * HEAD_DIM
SWA_KV_WIDTH = SWA_KV_HEADS * HEAD_DIM
WINDOW = 128
BLOCK = 128
ROPE_THETA_2 = 10000.0
N_GROUPS = 4
EXPERTS_PER_GROUP = 8
N_EXPERTS = N_GROUPS * EXPERTS_PER_GROUP
TOP_K = 2
D_EXPERT = D_MODEL // 4
EPS = 1e-6
IN_WIDTHS = (GDN_WIDTH, GDN_WIDTH, GDN_WIDTH, GDN_WIDTH, GDN_HEADS, GDN_HEADS,
             SWA_Q_WIDTH, SWA_KV_WIDTH, SWA_KV_WIDTH)
IN_WIDTH = sum(IN_WIDTHS)
MIX_OUT_WIDTH = GDN_WIDTH + SWA_Q_WIDTH


def rms_norm(x, gain):
    xf = x.astype(jnp.float32)
    y = xf * lax.rsqrt(jnp.mean(xf * xf, axis=-1, keepdims=True) + EPS)
    return (y * gain.astype(jnp.float32)).astype(x.dtype)

def l2_norm(x):
    return x * lax.rsqrt(jnp.sum(x * x, axis=-1, keepdims=True) + EPS)

def modulate(x, shift, scale):
    return x * (1 + scale[:, None, :]) + shift[:, None, :]

def causal_conv_silu(x, w):
    seq = x.shape[1]
    xp = jnp.pad(x, ((0, 0), (CONV_K - 1, 0), (0, 0)))
    y = xp[:, 0:seq] * w[0]
    for j in range(1, CONV_K):
        y = y + xp[:, j:j + seq] * w[j]
    return jax.nn.silu(y)

def rope(x, positions):
    half = x.shape[-1] // 2
    inv_freq = jnp.power(jnp.float32(ROPE_THETA_2), -jnp.arange(half, dtype=jnp.float32) / half)
    ang = positions.astype(jnp.float32)[..., None] * inv_freq
    cos = jnp.cos(ang)[:, :, None, :]
    sin = jnp.sin(ang)[:, :, None, :]
    xf = x.astype(jnp.float32)
    x1, x2 = xf[..., :half], xf[..., half:]
    out = jnp.concatenate([x1 * cos - x2 * sin, x1 * sin + x2 * cos], axis=-1)
    return out.astype(x.dtype)

def chunked_gated_delta_rule(q, k, v, g, beta):
    bsz, seq, heads, dh = q.shape
    n_chunks = seq // CHUNK

    def to_chunks(t):
        return t.reshape(bsz, n_chunks, CHUNK, heads, -1).transpose(0, 3, 1, 2, 4)

    q, k, v = to_chunks(q), to_chunks(k), to_chunks(v)
    g = g.reshape(bsz, n_chunks, CHUNK, heads).transpose(0, 3, 1, 2)
    beta = beta.reshape(bsz, n_chunks, CHUNK, heads).transpose(0, 3, 1, 2)
    G = jnp.cumsum(g, axis=-1)

    idx = jnp.arange(CHUNK)
    lower_incl = idx[:, None] >= idx[None, :]
    strict = idx[:, None] > idx[None, :]
    diff = G[..., :, None] - G[..., None, :]
    decay = jnp.where(lower_incl, jnp.exp(jnp.where(lower_incl, diff, 0.0)), 0.0)

    kb = k * beta[..., None]
    vb = v * beta[..., None]
    m = jnp.where(strict, jnp.einsum('bhncd,bhnsd->bhncs', kb, k) * decay, 0.0)
    eye = jnp.eye(CHUNK, dtype=jnp.float32)
    a_mat = eye + m
    t_mat = lax.linalg.triangular_solve(a_mat, jnp.broadcast_to(eye, a_mat.shape),
                                        left_side=True, lower=True)
    u = jnp.einsum('bhncs,bhnse->bhnce', t_mat, vb)
    w = jnp.einsum('bhncs,bhnsd->bhncd', t_mat, kb * jnp.exp(G)[..., None])
    qg = q * jnp.exp(G)[..., None]
    attn = jnp.einsum('bhncd,bhnsd->bhncs', q, k) * decay
    g_last = G[..., -1]
    k_dec = k * jnp.exp(g_last[..., None] - G)[..., None]

    xs = tuple(jnp.moveaxis(t, 2, 0) for t in (u, w, qg, attn, k_dec, g_last))

    def step(state, inp):
        u_n, w_n, qg_n, attn_n, kdec_n, gl_n = inp
        v_new = u_n - jnp.einsum('bhcd,bhde->bhce', w_n, state)
        o_n = (jnp.einsum('bhcd,bhde->bhce', qg_n, state)
               + jnp.einsum('bhcs,bhse->bhce', attn_n, v_new))
        state = (state * jnp.exp(gl_n)[..., None, None]
                 + jnp.einsum('bhcd,bhce->bhde', kdec_n, v_new))
        return state, o_n

    s0 = jnp.zeros((bsz, heads, dh, v.shape[-1]), jnp.float32)
    _, o = lax.scan(step, s0, xs)
    return o.transpose(1, 0, 3, 2, 4).reshape(bsz, seq, heads, -1)

def gated_deltanet(q_in, k_in, v_in, z, a, b, conv_w, a_log, dt_bias, out_norm):
    bsz, seq, _ = q_in.shape
    qkv = causal_conv_silu(jnp.concatenate([q_in, k_in, v_in], axis=-1), conv_w)
    q, k, v = jnp.split(qkv.astype(jnp.float32), 3, axis=-1)
    q = l2_norm(q.reshape(bsz, seq, GDN_HEADS, HEAD_DIM)) * (HEAD_DIM ** -0.5)
    k = l2_norm(k.reshape(bsz, seq, GDN_HEADS, HEAD_DIM))
    v = v.reshape(bsz, seq, GDN_HEADS, HEAD_DIM)
    g = -jnp.exp(a_log.astype(jnp.float32)) * jax.nn.softplus(
        a.astype(jnp.float32) + dt_bias.astype(jnp.float32))
    beta = jax.nn.sigmoid(b.astype(jnp.float32))
    o = chunked_gated_delta_rule(q, k, v, g, beta)
    zf = z.astype(jnp.float32).reshape(bsz, seq, GDN_HEADS, HEAD_DIM)
    o = rms_norm(o, out_norm) * jax.nn.silu(zf)
    return o.reshape(bsz, seq, GDN_WIDTH).astype(q_in.dtype)

def sliding_window_attention(q, k, v, q_norm, k_norm, sinks, positions):
    bsz, seq, _ = q.shape
    n_blk = seq // BLOCK
    q = rope(rms_norm(q.reshape(bsz, seq, SWA_Q_HEADS, HEAD_DIM), q_norm), positions)
    k = rope(rms_norm(k.reshape(bsz, seq, SWA_KV_HEADS, HEAD_DIM), k_norm), positions)
    v = v.reshape(bsz, seq, SWA_KV_HEADS, HEAD_DIM)

    qb = q.reshape(bsz, n_blk, BLOCK, SWA_KV_HEADS, SWA_GROUP, HEAD_DIM)

    def band(t):
        tb = t.reshape(bsz, n_blk, BLOCK, SWA_KV_HEADS, HEAD_DIM)
        prev = jnp.pad(tb[:, :-1], ((0, 0), (1, 0), (0, 0), (0, 0), (0, 0)))
        return jnp.concatenate([prev, tb], axis=2)

    k_band, v_band = band(k), band(v)
    scores = jnp.einsum('bnqhgd,bnkhd->bnhgqk', qb, k_band).astype(jnp.float32) * (HEAD_DIM ** -0.5)

    qi = jnp.arange(BLOCK)[:, None]
    kj = jnp.arange(2 * BLOCK)[None, :]
    rel = qi + BLOCK - kj
    in_window = (rel >= 0) & (rel < WINDOW)
    has_prev = jnp.arange(n_blk)[:, None, None] > 0
    valid = in_window[None] & (has_prev | (kj >= BLOCK)[None])
    scores = jnp.where(valid[None, :, None, None], scores, -jnp.inf)

    sink = sinks.astype(jnp.float32).reshape(SWA_KV_HEADS, SWA_GROUP)[None, None, :, :, None]
    mx = jnp.maximum(scores.max(axis=-1), sink)
    p = jnp.exp(scores - mx[..., None])
    denom = p.sum(axis=-1) + jnp.exp(sink - mx)
    p = p / denom[..., None]
    out = jnp.einsum('bnhgqk,bnkhd->bnqhgd', p, v_band.astype(jnp.float32))
    return out.reshape(bsz, seq, SWA_Q_WIDTH).astype(q.dtype)

def hierarchical_moe(h, w_group, b_group, w_router, b_router, w_gate, w_up, w_down):
    bsz, seq, d = h.shape
    t = h.reshape(-1, d)
    group_prob = jax.nn.softmax((t @ w_group + b_group).astype(jnp.float32), axis=-1)
    p_group, g_idx = lax.top_k(group_prob, 1)
    expert_logits = (t @ w_router + b_router).astype(jnp.float32).reshape(
        -1, N_GROUPS, EXPERTS_PER_GROUP)
    g_onehot = jax.nn.one_hot(g_idx[:, 0], N_GROUPS, dtype=jnp.float32)
    in_group = jnp.einsum('tg,tge->te', g_onehot, expert_logits)
    p_exp = jax.nn.softmax(in_group, axis=-1)
    w_top, e_idx = lax.top_k(p_exp, TOP_K)
    w_top = w_top / jnp.sum(w_top, axis=-1, keepdims=True) * p_group
    expert_ids = g_idx * EXPERTS_PER_GROUP + e_idx
    combine = jnp.sum(jax.nn.one_hot(expert_ids, N_EXPERTS, dtype=jnp.float32)
                      * w_top[..., None], axis=1)
    out = jnp.zeros(t.shape, jnp.float32)
    for e in range(N_EXPERTS):
        hid = jax.nn.silu(t @ w_gate[e]) * (t @ w_up[e])
        out = out + combine[:, e:e + 1] * (hid @ w_down[e]).astype(jnp.float32)
    return out.astype(h.dtype).reshape(bsz, seq, d)

def second_inputs(seed: int = 0) -> dict:
    key = jax.random.key(seed)
    ks = jax.random.split(key, 24)
    f32 = jnp.float32
    nrm = lambda k, shape: jax.random.normal(k, shape, f32)
    dt = jnp.exp(jax.random.uniform(ks[6], (DEPTH_2, GDN_HEADS), f32,
                                    jnp.log(jnp.float32(1e-3)), jnp.log(jnp.float32(1e-1))))
    return {
        "x": nrm(ks[0], (BATCH, SEQ, D_MODEL)),
        "c": nrm(ks[1], (BATCH, D_MODEL)),
        "positions": jnp.broadcast_to(jnp.arange(SEQ, dtype=jnp.int32), (BATCH, SEQ)),
        "w_ada": nrm(ks[2], (DEPTH_2, D_MODEL, 6 * D_MODEL)) * (0.5 * D_MODEL ** -0.5),
        "b_ada": 0.01 * nrm(ks[3], (DEPTH_2, 6 * D_MODEL)),
        "norm_mix": 1.0 + 0.1 * nrm(ks[4], (DEPTH_2, D_MODEL)),
        "w_in": nrm(ks[5], (DEPTH_2, D_MODEL, IN_WIDTH)) * D_MODEL ** -0.5,
        "conv_w": nrm(ks[7], (DEPTH_2, CONV_K, 3 * GDN_WIDTH)) * CONV_K ** -0.5,
        "a_log": jnp.log(jax.random.uniform(ks[8], (DEPTH_2, GDN_HEADS), f32, 1.0, 16.0)),
        "dt_bias": jnp.log(jnp.expm1(dt)),
        "gdn_out_norm": 1.0 + 0.1 * nrm(ks[9], (DEPTH_2, HEAD_DIM)),
        "q_norm": 1.0 + 0.1 * nrm(ks[10], (DEPTH_2, HEAD_DIM)),
        "k_norm": 1.0 + 0.1 * nrm(ks[11], (DEPTH_2, HEAD_DIM)),
        "sinks": nrm(ks[12], (DEPTH_2, SWA_Q_HEADS)),
        "w_out": nrm(ks[13], (DEPTH_2, MIX_OUT_WIDTH, D_MODEL)) * MIX_OUT_WIDTH ** -0.5,
        "norm_ffn": 1.0 + 0.1 * nrm(ks[14], (DEPTH_2, D_MODEL)),
        "w_group": nrm(ks[15], (DEPTH_2, D_MODEL, N_GROUPS)) * D_MODEL ** -0.5,
        "b_group": 0.01 * nrm(ks[16], (DEPTH_2, N_GROUPS)),
        "w_router": nrm(ks[17], (DEPTH_2, D_MODEL, N_EXPERTS)) * D_MODEL ** -0.5,
        "b_router": 0.01 * nrm(ks[18], (DEPTH_2, N_EXPERTS)),
        "w_gate": nrm(ks[19], (DEPTH_2, N_EXPERTS, D_MODEL, D_EXPERT)) * D_MODEL ** -0.5,
        "w_up": nrm(ks[20], (DEPTH_2, N_EXPERTS, D_MODEL, D_EXPERT)) * D_MODEL ** -0.5,
        "w_down": nrm(ks[21], (DEPTH_2, N_EXPERTS, D_EXPERT, D_MODEL)) * D_EXPERT ** -0.5,
    }

def second_block(x, c, positions, w_ada, b_ada, norm_mix, w_in, conv_w, a_log, dt_bias,
              gdn_out_norm, q_norm, k_norm, sinks, w_out, norm_ffn, w_group, b_group,
              w_router, b_router, w_gate, w_up, w_down):
    split_points = tuple(int(s) for s in np.cumsum(IN_WIDTHS)[:-1])
    c_act = jax.nn.silu(c)
    for l in range(DEPTH_2):
        mod = c_act @ w_ada[l] + b_ada[l]
        shift1, scale1, gate1, shift2, scale2, gate2 = jnp.split(mod, 6, axis=-1)

        h = modulate(rms_norm(x, norm_mix[l]), shift1, scale1)
        proj = h @ w_in[l]
        (g_q, g_k, g_v, g_z, g_a, g_b, s_q, s_k, s_v) = jnp.split(proj, split_points, axis=-1)
        gdn_out = gated_deltanet(g_q, g_k, g_v, g_z, g_a, g_b, conv_w[l], a_log[l],
                                 dt_bias[l], gdn_out_norm[l])
        swa_out = sliding_window_attention(s_q, s_k, s_v, q_norm[l], k_norm[l],
                                           sinks[l], positions)
        mixed = jnp.concatenate([gdn_out, swa_out], axis=-1) @ w_out[l]
        x = x + gate1[:, None, :] * mixed

        h2 = modulate(rms_norm(x, norm_ffn[l]), shift2, scale2)
        ffn = hierarchical_moe(h2, w_group[l], b_group[l], w_router[l], b_router[l],
                               w_gate[l], w_up[l], w_down[l])
        x = x + gate2[:, None, :] * ffn
    return x


def setup_inputs(seed=0):
    out = dict(first_inputs(seed))
    for name, value in second_inputs(seed + 1).items():
        if name != "x":
            out[name + "_2"] = value
    return out


def reference(
    x, ffn1_w_in, ffn1_w_out, ln1_g, ln1_b, w_mix_in, gate_bias, diff_lambda, diff_subln_g,
    ssm_conv_w, ssm_conv_b, ssm_dt_bias, ssm_A_log, ssm_D, ssm_norm_g, w_branch, w_mix_out,
    ln2_g, ln2_b, ffn2_w_in, ffn2_w_out, ln3_g, ln3_b, c_2, positions_2, w_ada_2, b_ada_2,
    norm_mix_2, w_in_2, conv_w_2, a_log_2, dt_bias_2, gdn_out_norm_2, q_norm_2, k_norm_2,
    sinks_2, w_out_2, norm_ffn_2, w_group_2, b_group_2, w_router_2, b_router_2, w_gate_2,
    w_up_2, w_down_2,
):
    x = first_block(
        x, ffn1_w_in, ffn1_w_out, ln1_g, ln1_b, w_mix_in, gate_bias, diff_lambda, diff_subln_g,
        ssm_conv_w, ssm_conv_b, ssm_dt_bias, ssm_A_log, ssm_D, ssm_norm_g, w_branch, w_mix_out,
        ln2_g, ln2_b, ffn2_w_in, ffn2_w_out, ln3_g, ln3_b,
    )
    return second_block(
        x, c_2, positions_2, w_ada_2, b_ada_2, norm_mix_2, w_in_2, conv_w_2, a_log_2, dt_bias_2,
        gdn_out_norm_2, q_norm_2, k_norm_2, sinks_2, w_out_2, norm_ffn_2, w_group_2, b_group_2,
        w_router_2, b_router_2, w_gate_2, w_up_2, w_down_2,
    )


_drawn_inputs = setup_inputs


def setup_inputs(seed=0):
    import zlib

    import numpy as np

    out = dict(_drawn_inputs(seed))
    spreads = {}
    factors = {'gate_bias': 8.0,
     'diff_lambda': 3.077,
     'diff_subln_g': 8.0,
     'ssm_conv_b': 7.289,
     'ssm_D': 8.0,
     'ssm_norm_g': 8.0,
     'b_ada_2': 4.749,
     'gdn_out_norm_2': 3.968,
     'q_norm_2': 8.0,
     'k_norm_2': 8.0,
     'sinks_2': 64.0,
     'b_group_2': 24.557,
     'b_router_2': 27.769}
    for name, (base, spread) in spreads.items():
        noise = np.random.default_rng([zlib.crc32(name.encode()), seed]).standard_normal(out[name].shape)
        drawn = base * np.exp(spread * noise) if base else spread * noise
        out[name] = jnp.asarray(drawn.astype(out[name].dtype))
    for name, factor in factors.items():
        out[name] = (out[name] * factor).astype(out[name].dtype)
    return out
```

```python
from contextlib import ExitStack

import numpy as np

import concourse.bass as bass
from concourse import mybir

F32 = mybir.dt.float32
I32 = mybir.dt.int32
ACT = mybir.ActivationFunctionType
ALU = mybir.AluOpType
AX = mybir.AxisListType

P = 128
TT = 2
TOK = P * TT
D = 1024
KT = D // P
LAYERS = 2
FF = 2816
UF = 256
UNITS = FF // UF
ALPHA = (2 * LAYERS) ** 0.25
FFN_RES = 0.5
LN_EPS = 1e-5
RMS_EPS = 1e-6
NEG = -1e30

HA, HDA, ROT_A = 8, 64, 16
HB, PB, GB, NB, CONV = 16, 64, 2, 128, 4
CONV_DIM = HB * PB + 2 * GB * NB
CT = CONV_DIM // P
HC, HDC = 16, 64
C_QA, C_KA, C_VA, C_Z, C_XBC = 0, 1024, 2048, 3072, 4096
C_DT = C_XBC + CONV_DIM
C_QC = C_DT + HB
C_KC, C_VC, C_G = C_QC + 1024, C_QC + 2048, C_QC + 3072

H2, HD2, KV2 = 8, 64, 2
G2W = H2 * HD2
EXPERTS, GROUPS, PER_GROUP = 32, 4, 8
ROUTE = GROUPS + EXPERTS
W2 = dict(qkv=0, z=3 * G2W, ab=4 * G2W, sq=4 * G2W + 2 * H2, skv=5 * G2W + 2 * H2)
LEVELS = 7

Q_FFN1 = 0
Q_A = Q_FFN1 + UNITS
Q_OA = Q_A + 6
Q_C = Q_OA + 4
Q_OC = Q_C + 6
Q_B = Q_OC + 4
Q_OB = Q_B + 6
Q_MO = Q_OB + 4
Q_FFN2 = Q_MO + 2
Q_LAYER = Q_FFN2 + UNITS
assert Q_LAYER % 2 == 0
Q_ADA = 0
Q_P2 = Q_ADA + 12
Q_W2 = Q_P2 + 7
Q_MOE = Q_W2 + 2
D_LAYER = 2 * UNITS

CONSTS = {}


def shape_constants():
    p = np.arange(P)[:, None]
    j = np.arange(P)[None, :]
    parts = [
        ("ident", p == j),
        ("ones", np.ones((P, P))),
        ("upto", p <= j),
        ("from_", p >= j),
        ("chunk_add", np.where(j // 64 <= p // 64, 0, NEG)),
        ("stick_add", np.concatenate([np.where(p < j, 0, NEG), 0 * (p + j), np.where(p < j, 0, NEG)], 1)),
        ("causal_add", np.where(j <= p, 0, NEG)),
        ("window_add", np.where(j > p, 0, NEG)),
    ]
    for b in [1 << n for n in range(LEVELS)]:
        parts.append((f"level{b}", ((j // b) % 2 == 1) & (p // b == j // b - 1)))
    half = ROT_A // 2
    inv = np.float32(500000.0) ** (-np.arange(half, dtype=np.float32) * np.float32(2.0) / np.float32(ROT_A))
    ang = np.arange(TOK, dtype=np.float32)[:, None] * inv[None, :].astype(np.float32)
    for name, f in (("cos_a", np.cos), ("sin_a", np.sin)):
        t = f(ang.astype(np.float32)).astype(np.float32).reshape(TT, P, half)
        parts.append((name, t.transpose(1, 0, 2).reshape(P, TT * half)))
    h2 = HD2 // 2
    inv2 = np.power(np.float32(10000.0), -np.arange(h2, dtype=np.float32) / np.float32(h2))
    parts.append(("inv_freq", np.broadcast_to(inv2.astype(np.float32), (P, h2))))
    li = [0.8 - 0.6 * np.exp(-0.3 * l) for l in range(LAYERS)]
    parts.append(("lam_init", np.broadcast_to(np.array(li, np.float32), (P, LAYERS))))
    parts.append(("one_minus_lam", np.broadcast_to(1.0 - np.array(li), (P, LAYERS))))
    parts.append(("minus_half", np.full((P, 64), -0.5)))
    at, cols = 0, []
    for name, a in parts:
        a = np.asarray(a, np.float32)
        CONSTS[name] = (at, a.shape[1])
        at += a.shape[1]
        cols.append(a)
    return np.ascontiguousarray(np.concatenate(cols, 1))


SHAPE_CONSTANTS = shape_constants()


def build(nc, A, out, stop=99):
    ctx = ExitStack()

    def sb(name, shape, dt=F32):
        return ctx.enter_context(nc.sbuf_tensor(name, shape, dt))

    def sem(name):
        return ctx.enter_context(nc.semaphore(name))

    consts = sb("consts", [P, SHAPE_CONSTANTS.shape[1]])
    wide = [sb(f"wide{s}", [P, KT, 512]) for s in range(2)]
    down = [sb(f"down{s}", [P, 2, D]) for s in range(2)]
    x = sb("x", [P, TT, D])
    xT = sb("xT", [P, KT, TOK])
    ln_par = sb("ln_par", [P, 2, D])
    sil = sb("sil", [P, TT, UF])
    hid = sb("hid", [P, TT, UF])
    hidT = sb("hidT", [P, TT, 2, P])
    small = sb("small", [P, 256])
    zrow = sb("zrow", [1, 512])
    br = sb("br", [P, TT, D])
    brT = sb("brT", [P, KT, TOK])
    merged = sb("merged", [P, TT, D])
    m1 = sb("m1", [P, 6144])
    m2 = sb("m2", [P, 6144])
    m3 = sb("m3", [P, 2048])
    m4 = sb("m4", [P, 3072])
    vecs = sb("vecs", [P, 1536])
    gate_row = sb("gate_row", [1, 3 * D])
    ps = ctx.enter_context(nc.psum_tensor("ps", [P, 8, 512], F32))

    def const(name, rows=P):
        at, n = CONSTS[name]
        return consts[0:rows, at:at + n]

    ident = const("ident")

    def view(t, at, *dims):
        n = int(np.prod(dims))
        names = " ".join(f"d{i}" for i in range(len(dims)))
        return t[:, at:at + n].rearrange(f"p ({names}) -> p {names}", **{f"d{i}": d for i, d in enumerate(dims)})

    def bc(ap, shape):
        return ap.to_broadcast(shape) if not isinstance(shape, int) else ap.to_broadcast([shape])

    wide_full = [sem(f"wide_full{s}") for s in range(2)]
    down_full = [sem(f"down_full{s}") for s in range(2)]
    blk = sem("block_done")
    dn = sem("down_done")
    BLK0, DN0 = 3, 2
    phase_left = sem("phase_left")

    pow_asked, pow_done = sem("pow_asked"), sem("pow_done")
    POW_LAYER = 5
    feat_turned = sem("to_features")
    TURN_LAYER = 7

    def power(l, nth):
        return l * POW_LAYER + (nth + 1)

    def turn(l, nth, kp):
        return l * (4 * TURN_LAYER) + (4 * (nth + 1) + kp + 1)

    class Block:

        def __init__(self, l, i, c):
            self.number = l * Q_LAYER + i * 2 + c
            self.slot = c % 2
            self.landed = (l * (Q_LAYER // 2) + i + c // 2 + 1) * 32
            self.may_load = self.number * 2 + (BLK0 - 2)
            self.tile = wide[self.slot]

        def done(self, t):
            return self.number * 2 + (BLK0 + t + 1)

    class Down:
        def __init__(self, l, i, c):
            self.number = l * D_LAYER + i * 2 + c
            self.slot = c % 2
            self.landed = (l * (D_LAYER // 2) + i + c // 2 + 1) * 16
            self.may_load = self.number + (DN0 - 1)
            self.done = self.number + (DN0 + 1)
            self.tile = down[self.slot]

    def pairs(eng, n, body):
        with eng.Fori(0, n // 2) as i:
            body(i, 0)
            body(i, 1)
        if n % 2:
            body(0, n - 1)

    carried = sem("waits_carried")

    def carry(eng):
        eng.sem_inc(carried, 1)

    def leave(eng, phase):
        eng.drain()
        eng.sem_inc(phase_left, 1)
        eng.wait_ge(phase_left, phase * 4 + 4)
        carry(eng)

    def load_halves(sp, b, lo, hi, dst):
        sp.wait_ge(blk, b.may_load)
        sp.dma_start(dst[0], lo).then_inc(wide_full[b.slot], 16)
        sp.dma_start(dst[1], hi).then_inc(wide_full[b.slot], 16)

    def load_columns(sp, b, w, col, n=512):
        v = w.rearrange("(k p) n -> p k n", p=P)[:, :, bass.ds(col, n)]
        load_halves(sp, b, v[:, 0:4, :], v[:, 4:8, :], (b.tile[:, 0:4, 0:n], b.tile[:, 4:8, 0:n]))

    def layer_of(ap, l):
        names = " ".join("abcd"[:len(ap.shape) - 1])
        return ap[bass.ds(l, 1)].rearrange(f"z {names} -> (z {names.split()[0]}) {' '.join(names.split()[1:])}")

    def products(pe, bank, stat, b, n=512, more=False):
        for k in range(KT):
            last = pe.matmul(bank[:, 0:n], stat(k), b.tile[:, k, 0:n], start=(k == 0), stop=(k == KT - 1 and not more))
        return last

    class ToFeatures:

        def __init__(self, src, dst, nth):
            self.src, self.dst, self.nth = src, dst, nth

        def pe(self, pe, l):
            for kp in range(4):
                for kk in range(2):
                    for t in range(TT):
                        k = 2 * kp + kk
                        at = kk * TOK + t * P
                        ins = pe.transpose(ps[:, kp, at:at + P], self.src[:, t, k * P:(k + 1) * P], ident)
                ins.then_inc(feat_turned, 1)

        def copy(self, eng, op, l, which):
            for kp in which:
                eng.wait_ge(feat_turned, turn(l, self.nth, kp))
                op(self.dst[:, 2 * kp:2 * kp + 2, :], view_bank(kp, 2, TOK))

        def act(self, act, l):
            self.copy(act, nc.scalar.copy, l, (0, 2))

        def dve(self, dve, l):
            self.copy(dve, nc.vector.tensor_copy, l, (1, 3))

    def view_bank(b, *dims):
        names = " ".join(f"d{i}" for i in range(len(dims)))
        n = int(np.prod(dims))
        return ps[:, b, 0:n].rearrange(f"p ({names}) -> p {names}", **{f"d{i}": d for i, d in enumerate(dims)})

    sil_done = sem("sil_done")
    hid_done = sem("hid_done")
    hid_turned = sem("hid_turned")
    hidT_done = sem("hidT_done")
    HALVES_LAYER = 4 * UNITS

    class Gated:

        def __init__(self, units, q, d, gate_up, down_rows, weight=None):
            self.units, self.q, self.d = units, q, d
            self.gate_up, self.down_rows, self.weight = gate_up, down_rows, weight

        def sp(self, sp, l):
            def unit(i, c):
                b, d = Block(l, i, self.q + c), Down(l, i, self.d + c)
                lo, hi = self.gate_up(l, i * 2 + c)
                load_halves(sp, b, lo, hi, (b.tile[:, :, 0:UF], b.tile[:, :, UF:2 * UF]))
                sp.wait_ge(dn, d.may_load)
                sp.dma_start(d.tile[:], self.down_rows(l, i * 2 + c)).then_inc(down_full[d.slot], 16)
            pairs(sp, self.units, unit)

        def pe(self, pe, l):
            for bank in range(4):
                pe.matmul(ps[:, bank, :], zrow[0:1, 0:P], zrow[0:1, :], start=True, stop=False, skip_group_check=True)

            def unit(i, c):
                b, d = Block(l, i, self.q + c), Down(l, i, self.d + c)
                n = l * HALVES_LAYER + i * 4 + (2 * self.d + c * 2)
                pe.wait_ge(wide_full[b.slot], b.landed)
                for t in range(TT):
                    pe.wait_ge(hid_done, n + t + 1)
                    products(pe, ps[:, 4 + t, :], lambda k: xT[:, k, t * P:(t + 1) * P], b).then_inc(blk, 1)
                for t in range(TT):
                    pe.wait_ge(hid_done, n + t + 3)
                    pe.wait_ge(hidT_done, n + t + 1)
                    for k in range(2):
                        ins = pe.transpose(ps[:, 6 + t, k * P:(k + 1) * P], hid[:, t, k * P:(k + 1) * P], ident)
                    ins.then_inc(hid_turned, 1)
                    if t == 0:
                        pe.wait_ge(down_full[d.slot], d.landed)
                    pe.wait_ge(hidT_done, n + t + 3)
                    for half in range(2):
                        for k in range(2):
                            ins = pe.matmul(ps[:, 2 * t + half, :], hidT[:, t, k, :], d.tile[:, k, half * 512:(half + 1) * 512],
                                            start=False, stop=False, skip_group_check=True)
                    if t == 1:
                        ins.then_inc(dn, 1)
            pairs(pe, self.units, unit)

        def act(self, act, l):
            def unit(i, c):
                b, d = Block(l, i, self.q + c), Down(l, i, self.d + c)
                n = l * HALVES_LAYER + i * 4 + (2 * self.d + c * 2)
                for t in range(TT):
                    act.wait_ge(blk, b.done(t))
                    nc.scalar.activation(sil[:, t, :], ps[:, 4 + t, 0:UF], ACT.Silu).then_inc(sil_done, 1)
                for t in range(TT):
                    act.wait_ge(hid_turned, n + t + 3)
                    act.wait_ge(dn, d.done - 1)
                    nc.scalar.copy(hidT[:, t], ps[:, 6 + t, 0:UF].rearrange("p (k n) -> p k n", k=2)).then_inc(hidT_done, 1)
            pairs(act, self.units, unit)

        def dve(self, dve, l):
            def unit(i, c):
                n = l * HALVES_LAYER + i * 4 + (2 * self.d + c * 2)
                for t in range(TT):
                    dve.wait_ge(sil_done, n + t + 1)
                    dve.wait_ge(hid_turned, n + t + 1)
                    if self.weight is None:
                        nc.vector.tensor_tensor(hid[:, t, :], sil[:, t, :], ps[:, 4 + t, UF:2 * UF], ALU.mult).then_inc(hid_done, 1)
                    else:
                        nc.vector.scalar_tensor_tensor(out=hid[:, t, :], in0=sil[:, t, :], scalar=self.weight(t, i * 2 + c),
                                                       in1=ps[:, 4 + t, UF:2 * UF], op0=ALU.mult, op1=ALU.mult).then_inc(hid_done, 1)
            pairs(dve, self.units, unit)

    norm_par = sem("norm_par")
    normed = sem("normed")

    class Norm:

        def __init__(self, nth, power, turn, r, g, b):
            self.nth, self.power, self.r, self.g, self.b = nth, power, r, g, b
            self.toT = ToFeatures(x, xT, turn)

        def load(self, pool, l):
            pool.dma_start(ln_par[:, 0, :], self.g[bass.ds(l, 1), :].partition_broadcast(P)).then_inc(norm_par, 16)
            pool.dma_start(ln_par[:, 1, :], self.b[bass.ds(l, 1), :].partition_broadcast(P)).then_inc(norm_par, 16)

        def dve(self, dve, l):
            st, mv = view(small, 0, TT, 2, 6), view(small, 24, TT, 2)
            for t in range(TT):
                nc.vector.tensor_scalar(x[:, t, :], x[:, t, :], ALPHA, None, ALU.mult)
            dve.drain()
            for t in range(TT):
                acc = ps[:, 2 * t:2 * t + 2, :].rearrange("p a b -> p (a b)")
                nc.vector.scalar_tensor_tensor(out=x[:, t, :], in0=acc, scalar=self.r, in1=x[:, t, :], op0=ALU.mult, op1=ALU.add)
            dve.drain()
            for t in range(TT):
                for h in range(2):
                    nc.vector.bn_stats(st[:, t, h, :], x[:, t, h * 512:(h + 1) * 512])
            dve.drain()
            for t in range(TT):
                nc.vector.bn_aggr(mv[:, t, :], st[:, t].rearrange("p a b -> p (a b)"))
            dve.drain()
            nc.vector.tensor_scalar(small[:, 30:32], mv[:, :, 1], LN_EPS, None, ALU.add).then_inc(pow_asked, 1)
            dve.wait_ge(pow_done, power(l, self.power))
            dve.wait_ge(norm_par, l * 96 + (self.nth + 1) * 32)
            for t in range(TT):
                nc.vector.tensor_scalar(x[:, t, :], x[:, t, :], mv[:, t, 0:1], small[:, 32 + t:33 + t], ALU.subtract, ALU.mult)
            dve.drain()
            nc.vector.tensor_tensor(x[:], x[:], bc(ln_par[:, 0:1, :], [P, TT, D]), ALU.mult)
            dve.drain()
            nc.vector.tensor_tensor(x[:], x[:], bc(ln_par[:, 1:2, :], [P, TT, D]), ALU.add).then_inc(normed, 1)
            self.toT.dve(dve, l)

        def pool(self, pool, l):
            pool.wait_ge(pow_asked, power(l, self.power))
            nc.gpsimd.tensor_tensor(small[:, 32:34], small[:, 30:32], const("minus_half")[:, 0:2], ALU.pow).then_inc(pow_done, 1)

        def pe(self, pe, l):
            pe.wait_ge(normed, l * 3 + (self.nth + 1))
            self.toT.pe(pe, l)

        def act(self, act, l):
            self.toT.act(act, l)

    class Project:

        def __init__(self, name, q, groups, stat=xT, first=0):
            self.q, self.groups, self.stat, self.first = q, groups, stat, first
            self.copied = [sem(f"{name}_copied{e}") for e in range(2)]
            self.total = sum(g[0] for g in groups)

        def start(self, act, dve):
            if act is not None:
                act.sem_inc(self.copied[0], 2)
            if dve is not None:
                dve.sem_inc(self.copied[1], 2)

        def each(self, eng, body):
            at = 0
            for g in self.groups:
                if g[0] >= 4:
                    with eng.Fori(0, g[0] // 2) as i:
                        for c in range(2):
                            body(g, i, at + c, c)
                else:
                    for c in range(g[0]):
                        body(g, 0, at + c, c)
                at += g[0]

        def sp(self, sp, l):
            def block(g, i, c, cl):
                load_columns(sp, Block(l, i, self.q + c), g[3](l), i * 1024 + (g[4] + cl * 512), g[2])
            self.each(sp, block)

        def pe(self, pe, l):
            def block(g, i, c, cl):
                b = Block(l, i, self.q + c)
                n = (l - self.first) * self.total + i * 2 + c
                pe.wait_ge(wide_full[b.slot], b.landed)
                for part in range(2):
                    pe.wait_ge(self.copied[part], n + 1)
                    bank = ps[:, 2 * (c % 2) + part, :]
                    if g[1] == "tok":
                        last = products(pe, bank, lambda k: self.stat[:, k, part * P:(part + 1) * P], b, g[2])
                    else:
                        for f in range(2):
                            at = (2 * part + f) * P
                            for k in range(KT):
                                last = pe.matmul(bank[:, f * TOK:(f + 1) * TOK], b.tile[:, k, at:at + P], self.stat[:, k, :],
                                                 start=(k == 0), stop=(k == KT - 1))
                    last.then_inc(blk, 1)
            self.each(pe, block)

        def copy(self, eng, op, l, part):
            def block(g, i, c, cl):
                b = Block(l, i, self.q + c)
                eng.wait_ge(blk, b.done(part))
                bank = 2 * (c % 2) + part
                dst = g[5](part, i, cl)
                src = ps[:, bank:bank + 1, 0:g[2]] if g[1] == "tok" else view_bank(bank, 2, TOK)
                op(dst, src).then_inc(self.copied[part], 1)
            self.each(eng, block)

        def act(self, act, l):
            self.copy(act, nc.scalar.copy, l, 0)

        def dve(self, dve, l):
            self.copy(dve, nc.vector.tensor_copy, l, 1)

    w_mix = lambda l: layer_of(A["w_mix_in"], l)

    qkv_a = view(m1, 0, 3, TT, D)
    proj_a = Project("a_proj", Q_A, [(6, "tok", 512, w_mix, C_QA,
                                      lambda part, i, c: qkv_a[:, bass.ds(i, 1), part, c * 512:(c + 1) * 512])])

    class DiffAttention:
        par = sem("a_par")
        lam_sum, lam_exp = sem("a_lam_sum"), sem("a_lam_exp")
        roped = sem("a_roped")
        staged, turned, qT_done, kT_done = sem("a_staged"), sem("a_turned"), sem("a_qT"), sem("a_kT")
        scored, masked, exped, mixed = sem("a_scored"), sem("a_masked"), sem("a_exped"), sem("a_mixed")
        w_turned, wT_done, out_done = sem("a_w_turned"), sem("a_wT"), sem("a_out")
        ready = sem("a_ready")
        stage = view(m4, 0, 3, TT, P)
        qT, kT = view(m4, 768, 2, TOK)[0:HDA], view(m4, 1280, 2, TOK)[0:HDA]
        sm = m2[:, 0:768]
        w = m2[:, 768:1152]
        wT = view(m2, 1152, 3, P)
        st = m2[:, 1536:1600]
        subln = vecs[:, 0:2 * HDA]
        lam4 = view(vecs, 128, 4, HDA)
        toT = ToFeatures(br, brT, 1)

        def load(self, pool, l):
            pool.dma_start(self.subln, A["diff_subln_g"][bass.ds(l, 1), :].partition_broadcast(P)).then_inc(self.par, 16)
            pool.dma_start(vecs[:, 128:384], A["diff_lambda"].rearrange("l a d -> l (a d)")[bass.ds(l, 1), :].partition_broadcast(P)).then_inc(self.par, 16)

        def pool(self, pool, l):
            pool.wait_ge(self.roped, l + 1)
            carry(pool)
            with pool.Fori(0, HA) as h:
                n = l * HA + h
                pool.wait_ge(self.out_done, n + 1)
                for j in range(3):
                    ins = nc.gpsimd.tensor_copy(self.stage[:, j], qkv_a[:, j, :, bass.ds(h * P, P)])
                ins.then_inc(self.staged, 1)
            pool.wait_ge(pow_asked, power(l, 1))
            nc.gpsimd.tensor_tensor(self.st[:, 32:48], self.st[:, 16:32], const("minus_half")[:, 0:16], ALU.pow).then_inc(pow_done, 1)

        def pe(self, pe, l):
            with pe.Fori(0, HA) as h:
                n = l * HA + h
                pe.wait_ge(self.staged, n + 1)
                carry(pe)
                for j in range(2):
                    for m in range(2):
                        for t in range(TT):
                            ins = pe.transpose(ps[0:HDA, j, m * TOK + t * P:m * TOK + (t + 1) * P],
                                               self.stage[:, j, t, m * HDA:(m + 1) * HDA], ident)
                    ins.then_inc(self.turned, 1)
                pe.wait_ge(self.qT_done, n + 1)
                pe.wait_ge(self.kT_done, n + 1)
                for t in range(TT):
                    keys = (t + 1) * P
                    for m in range(2):
                        ins = pe.matmul(ps[:, 2 + t, m * keys:(m + 1) * keys], self.qT[:, m, t * P:(t + 1) * P],
                                        self.kT[:, m, 0:keys], start=True, stop=True)
                ins.then_inc(self.scored, 1)
                pe.wait_ge(self.mixed, n + 1)
                for b in range(3):
                    ins = pe.transpose(ps[:, 4, b * P:(b + 1) * P], self.w[:, b * P:(b + 1) * P], ident)
                ins.then_inc(self.w_turned, 1)
                pe.wait_ge(self.wT_done, n + 1)
                pe.matmul(ps[:, 5, 0:P], self.wT[:, 0, :], self.stage[:, 2, 0, :], start=True, stop=True)
                pe.matmul(ps[:, 5, P:2 * P], self.wT[:, 1, :], self.stage[:, 2, 0, :], start=True, stop=False)
                pe.matmul(ps[:, 5, P:2 * P], self.wT[:, 2, :], self.stage[:, 2, 1, :], start=False, stop=True).then_inc(self.out_done, 1)
            pe.wait_ge(self.ready, l + 1)
            self.toT.pe(pe, l)

        def act(self, act, l):
            act.wait_ge(self.lam_sum, l + 1)
            nc.scalar.activation(self.st[:, 52:54], self.st[:, 50:52], ACT.Exp).then_inc(self.lam_exp, 1)
            with act.Fori(0, HA) as h:
                n = l * HA + h
                act.wait_ge(self.turned, n * 2 + 1)
                nc.scalar.mul(self.qT, ps[0:HDA, 0, :].rearrange("p (m n) -> p m n", m=2), HDA ** -0.5).then_inc(self.qT_done, 1)
                act.wait_ge(self.masked, n + 1)
                at = 0
                for t in range(TT):
                    keys = (t + 1) * P
                    for m in range(2):
                        c = 2 * t + m
                        ins = nc.scalar.activation(self.sm[:, at:at + keys], self.sm[:, at:at + keys], ACT.Exp,
                                                   bias=self.st[:, c:c + 1], accum_out=self.st[:, 4 + c:5 + c])
                        at += keys
                ins.then_inc(self.exped, 1)
                act.wait_ge(self.w_turned, n + 1)
                nc.scalar.copy(self.wT, view_bank(4, 3, P)).then_inc(self.wT_done, 1)
            self.toT.act(act, l)

        def dve(self, dve, l):
            V, st = nc.vector, self.st
            dve.wait_ge(self.par, l * 32 + 32)
            pr = view(m3, 0, 2, HDA)
            V.tensor_tensor(pr, self.lam4[:, 0:4:2, :], self.lam4[:, 1:4:2, :], ALU.mult)
            dve.drain()
            V.tensor_reduce(st[:, 50:52], pr, AX.X, ALU.add).then_inc(self.lam_sum, 1)
            V.tensor_copy(st[:, 56:57], const("lam_init")[:, bass.ds(l, 1)])
            V.tensor_copy(st[:, 57:58], const("one_minus_lam")[:, bass.ds(l, 1)])
            dve.drain()
            V.tensor_scalar(self.subln, self.subln, st[:, 57:58], None, ALU.mult)
            dve.wait_ge(self.lam_exp, l + 1)
            V.tensor_tensor(st[:, 54:55], st[:, 53:54], st[:, 52:53], ALU.subtract)
            dve.drain()
            V.tensor_tensor(st[:, 55:56], st[:, 54:55], st[:, 56:57], ALU.subtract)
            half = ROT_A // 2
            for t in range(TT):
                maps = qkv_a[:, 0:2, t, :].rearrange("p j (m d) -> p j m d", d=HDA)
                a, b = maps[:, :, :, 0:half], maps[:, :, :, half:ROT_A]
                cos, sin = (bc(const(c)[:, t * half:(t + 1) * half].unsqueeze(1).unsqueeze(1), [P, 2, 16, half]) for c in ("cos_a", "sin_a"))
                ac, bs, bcs, as_ = (view(m3, 256 + 256 * (4 * t + i), 2, 16, half) if 4 * t + i < 7 else view(m2, 4096, 2, 16, half) for i in range(4))
                V.tensor_tensor(ac, a, cos, ALU.mult)
                V.tensor_tensor(bs, b, sin, ALU.mult)
                V.tensor_tensor(bcs, b, cos, ALU.mult)
                V.tensor_tensor(as_, a, sin, ALU.mult)
                dve.drain()
                V.tensor_tensor(a, ac, bs, ALU.subtract)
                V.tensor_tensor(b, bcs, as_, ALU.add)
            dve.drain()
            dve.sem_inc(self.roped, 1)
            mask = const("chunk_add")
            s0 = self.sm[:, 0:256].rearrange("p (m k) -> p m k", m=2)
            s1 = self.sm[:, 256:768].rearrange("p (m k) -> p m k", m=2)
            with dve.Fori(0, HA) as h:
                n = l * HA + h
                dve.wait_ge(self.turned, n * 2 + 2)
                V.tensor_copy(self.kT, ps[0:HDA, 1, :].rearrange("p (m n) -> p m n", m=2)).then_inc(self.kT_done, 1)
                dve.wait_ge(self.scored, n + 1)
                V.tensor_tensor(s0, view_bank(2, 2, P), bc(mask.unsqueeze(1), [P, 2, P]), ALU.add)
                V.tensor_copy(s1[:, :, 0:P], view_bank(3, 2, TOK)[:, :, 0:P])
                V.tensor_tensor(s1[:, :, P:TOK], view_bank(3, 2, TOK)[:, :, P:TOK], bc(mask.unsqueeze(1), [P, 2, P]), ALU.add)
                dve.drain()
                V.tensor_reduce(st[:, 0:2], s0, AX.X, ALU.max, negate=True)
                V.tensor_reduce(st[:, 2:4], s1, AX.X, ALU.max, negate=True).then_inc(self.masked, 1)
                dve.wait_ge(self.exped, n + 1)
                V.reciprocal(st[:, 8:12], st[:, 4:8])
                dve.drain()
                V.tensor_scalar(st[:, 12:16], st[:, 8:12], st[:, 55:56], None, ALU.mult)
                V.tensor_scalar(self.w[:, 0:P], s0[:, 0, :], st[:, 8:9], None, ALU.mult)
                V.tensor_scalar(self.w[:, P:3 * P], s1[:, 0, :], st[:, 10:11], None, ALU.mult)
                dve.drain()
                V.scalar_tensor_tensor(out=self.w[:, 0:P], in0=s0[:, 1, :], scalar=st[:, 13:14], in1=self.w[:, 0:P], op0=ALU.mult, op1=ALU.add)
                V.scalar_tensor_tensor(out=self.w[:, P:3 * P], in0=s1[:, 1, :], scalar=st[:, 15:16], in1=self.w[:, P:3 * P],
                                       op0=ALU.mult, op1=ALU.add).then_inc(self.mixed, 1)
                dve.wait_ge(self.out_done, n + 2)
                V.tensor_copy(br[:, :, bass.ds(h * P, P)], view_bank(5, TT, P))
            dve.drain()
            heads = br[:].rearrange("p t (h e) -> p (t h) e", e=P)
            sq = view(m3, 0, TT * HA, P)
            V.tensor_tensor(sq, heads, heads, ALU.mult)
            dve.drain()
            V.tensor_reduce(st[:, 0:16], sq, AX.X, ALU.add)
            dve.drain()
            V.tensor_scalar(st[:, 16:32], st[:, 0:16], 1.0 / P, LN_EPS, ALU.mult, ALU.add).then_inc(pow_asked, 1)
            dve.wait_ge(pow_done, power(l, 1))
            V.tensor_tensor(heads, heads, bc(st[:, 32:48].unsqueeze(2), [P, TT * HA, P]), ALU.mult)
            dve.drain()
            V.tensor_tensor(heads, heads, bc(self.subln.unsqueeze(1), [P, TT * HA, P]), ALU.mult).then_inc(self.ready, 1)
            self.toT.dve(dve, l)

    gate_done, half_added = sem("branch_gate"), sem("branch_added")

    class Merge:

        def __init__(self, nth, q, r):
            self.nth, self.q, self.r = nth, q, r
            self.gates = view(m4, 0, TT, 512)
            self.part = view(m4, 1024, TT, 512)

        def sp(self, sp, l):
            for c in range(2):
                w = A["w_branch"][bass.ds(l, 1), self.r].rearrange("z k n -> (z k) n")
                load_columns(sp, Block(l, 0, self.q + 2 * c), w, c * 512)
                load_columns(sp, Block(l, 0, self.q + 2 * c + 1), w_mix(l), C_G + self.r * D + c * 512)

        def pe(self, pe, l):
            for c in range(2):
                for g in range(2):
                    b = Block(l, 0, self.q + 2 * c + g)
                    pe.wait_ge(wide_full[b.slot], b.landed)
                    if c == 1 and g == 0:
                        pe.wait_ge(half_added, l * 6 + (self.nth * 2 + 1))
                    for t in range(TT):
                        bank = ps[:, 4 + 2 * g + t, :]
                        if g == 0:
                            products(pe, bank, lambda k: brT[:, k, t * P:(t + 1) * P], b).then_inc(blk, 1)
                        else:
                            at = self.r * D + c * 512
                            pe.matmul(bank, const("ones", 1), gate_row[0:1, at:at + 512], start=True, stop=False)
                            for k in range(KT):
                                ins = pe.matmul(bank, xT[:, k, t * P:(t + 1) * P], b.tile[:, k, :], start=False, stop=(k == KT - 1))
                            ins.then_inc(blk, 1)

        def act(self, act, l):
            for c in range(2):
                if c == 1:
                    act.wait_ge(half_added, l * 6 + (self.nth * 2 + 1))
                for t in range(TT):
                    act.wait_ge(blk, Block(l, 0, self.q + 2 * c + 1).done(t))
                    nc.scalar.activation(self.gates[:, t, :], ps[:, 6 + t, :], ACT.Sigmoid).then_inc(gate_done, 1)

        def dve(self, dve, l):
            for c in range(2):
                cols = slice(c * 512, (c + 1) * 512)
                for t in range(TT):
                    dve.wait_ge(blk, Block(l, 0, self.q + 2 * c).done(t))
                    dve.wait_ge(gate_done, l * 12 + (self.nth * 4 + 2 * c + t + 1))
                    dst = merged[:, t, cols] if self.r == 0 else self.part[:, t, :]
                    ins = nc.vector.tensor_tensor(dst, self.gates[:, t, :], ps[:, 4 + t, :], ALU.mult)
                if self.r:
                    dve.drain()
                    ins = nc.vector.tensor_tensor(merged[:, :, cols], merged[:, :, cols], self.part, ALU.add)
                ins.then_inc(half_added, 1)

    qk_c = view(m1, 0, 16, TOK)
    v_c = view(m1, 4096, TT, D)
    proj_c = Project("c_proj", Q_C, [
        (4, "feat", 512, w_mix, C_QC, lambda part, i, c: qk_c[:, bass.ds(i * 8 + (c * 4 + part * 2), 2), :]),
        (2, "tok", 512, w_mix, C_VC, lambda part, i, c: v_c[:, part:part + 1, c * 512:(c + 1) * 512])])

    class StickBreaking:
        staged, scored, absed, logged = sem("c_staged"), sem("c_scored"), sem("c_abs"), sem("c_log")
        stay, summed, shifted, weighed = sem("c_stay"), sem("c_summed"), sem("c_shifted"), sem("c_weighed")
        out_done, ready = sem("c_out"), sem("c_ready")
        qk = view(m4, 0, 2, TOK)
        v = view(m4, 512, TT, P)
        z = view(m2, 0, 2, 384)
        ab = view(m2, 768, 2, 384)
        lg = view(m2, 1536, 2, 384)
        sp_ = view(m2, 2304, 2, 384)
        a = view(m2, 3072, 2, 384)
        toT = ToFeatures(br, brT, 2)

        def pool(self, pool, l):
            with pool.Fori(0, HC // 2) as h:
                n = l * (HC // 2) + h
                pool.wait_ge(self.out_done, n + 1)
                nc.gpsimd.tensor_copy(self.qk[:, 0:1, :], qk_c[:, bass.ds(h, 1), :])
                nc.gpsimd.tensor_copy(self.qk[:, 1:2, :], qk_c[:, bass.ds(h + 8, 1), :])
                nc.gpsimd.tensor_copy(self.v, v_c[:, :, bass.ds(h * P, P)]).then_inc(self.staged, 1)

        def pe(self, pe, l):
            with pe.Fori(0, HC // 2) as h:
                n = l * (HC // 2) + h
                pe.wait_ge(self.staged, n + 1)
                for e in range(2):
                    rows = slice(e * HDC, (e + 1) * HDC)
                    pe.matmul(ps[:, e, 0:TOK], self.qk[rows, 1, 0:P], self.qk[rows, 0, :], start=True, stop=True)
                    ins = pe.matmul(ps[:, e, TOK:384], self.qk[rows, 1, P:TOK], self.qk[rows, 0, P:TOK], start=True, stop=True)
                ins.then_inc(self.scored, 1)
                pe.wait_ge(self.stay, n + 1)
                for e in range(2):
                    pe.matmul(ps[:, 2 + e, 0:384], const("from_"), self.sp_[:, e, :], start=True, stop=False)
                    ins = pe.matmul(ps[:, 2 + e, P:TOK], const("ones"), self.sp_[:, e, TOK:384], start=False, stop=True)
                ins.then_inc(self.summed, 1)
                pe.wait_ge(self.weighed, n + 1)
                for e in range(2):
                    cols = slice(e * HDC, (e + 1) * HDC)
                    pe.matmul(ps[:, 4, e * HDC:(e + 1) * HDC], self.a[:, e, 0:P], self.v[:, 0, cols], start=True, stop=True)
                    pe.matmul(ps[:, 4, P + e * HDC:P + (e + 1) * HDC], self.a[:, e, P:TOK], self.v[:, 0, cols], start=True, stop=False)
                    ins = pe.matmul(ps[:, 4, P + e * HDC:P + (e + 1) * HDC], self.a[:, e, TOK:384], self.v[:, 1, cols], start=False, stop=True)
                ins.then_inc(self.out_done, 1)
            pe.wait_ge(self.ready, l + 1)
            self.toT.pe(pe, l)

        def act(self, act, l):
            with act.Fori(0, HC // 2) as h:
                n = l * (HC // 2) + h
                act.wait_ge(self.absed, n + 1)
                nc.scalar.activation(self.lg, self.ab, ACT.Exp, scale=-1.0)
                act.drain()
                nc.scalar.activation(self.lg, self.lg, ACT.Ln, bias=1.0).then_inc(self.logged, 1)
                act.wait_ge(self.shifted, n + 1)
                nc.scalar.activation(self.a, self.a, ACT.Exp).then_inc(self.weighed, 1)
                act.wait_ge(self.out_done, n + 2)
                nc.scalar.copy(br[:, :, bass.ds(h * P, P)], view_bank(4, TT, P))
            act.drain()
            act.sem_inc(self.ready, 1)
            self.toT.act(act, l)

        def dve(self, dve, l):
            V = nc.vector
            with dve.Fori(0, HC // 2) as h:
                n = l * (HC // 2) + h
                dve.wait_ge(self.scored, n + 1)
                V.scalar_tensor_tensor(out=self.z, in0=ps[:, 0:2, 0:384], scalar=HDC ** -0.5,
                                       in1=bc(const("stick_add").unsqueeze(1), [P, 2, 384]), op0=ALU.mult, op1=ALU.add)
                dve.drain()
                V.scalar_tensor_tensor(out=self.ab, in0=self.z, scalar=-1.0, in1=self.z, op0=ALU.mult, op1=ALU.max).then_inc(self.absed, 1)
                dve.wait_ge(self.logged, n + 1)
                V.scalar_tensor_tensor(out=self.sp_, in0=self.z, scalar=0.0, in1=self.lg, op0=ALU.max, op1=ALU.add).then_inc(self.stay, 1)
                dve.wait_ge(self.summed, n + 1)
                V.tensor_tensor(self.a, self.z, ps[:, 2:4, 0:384], ALU.subtract).then_inc(self.shifted, 1)
            self.toT.dve(dve, l)

    z_b = view(m1, 0, TT, D)
    xbc = view(m1, 2048, CT, TOK + CONV - 1)
    dt_raw = view(m1, 2048 + CT * (TOK + CONV - 1), TT, HB)
    proj_b = Project("b_proj", Q_B, [
        (2, "tok", 512, w_mix, C_Z, lambda part, i, c: z_b[:, part:part + 1, c * 512:(c + 1) * 512]),
        (3, "feat", 512, w_mix, C_XBC, lambda part, i, c: xbc[:, c * 4 + part * 2:c * 4 + part * 2 + 2, CONV - 1:]),
        (1, "tok", HB, w_mix, C_DT, lambda part, i, c: dt_raw[:, part:part + 1, :])])

    def convolve(dve, dst, src, weight, bias=None):
        for j in range(CONV):
            with dve.Fori(0, CT // 4) as i:
                for c4 in range(4):
                    c = i * 4 + c4
                    s, o = src[:, bass.ds(c, 1), j:j + TOK], dst[:, bass.ds(c, 1), :]
                    if j:
                        nc.vector.scalar_tensor_tensor(out=o, in0=s, scalar=weight(j, c), in1=o, op0=ALU.mult, op1=ALU.add)
                    elif bias is not None:
                        nc.vector.tensor_scalar(o, s, weight(j, c), bias(c), ALU.mult, ALU.add)
                    else:
                        nc.vector.tensor_scalar(o, s, weight(j, c), None, ALU.mult)
            dve.drain()

    class Scan:
        par, pad, cw_turned, cw_done = sem("b_par"), sem("b_pad"), sem("b_cw_turned"), sem("b_cw")
        convolved, silu_done = sem("b_conv"), sem("b_silu")
        dt_abs, dt_log, decay_done = sem("b_dt_abs"), sem("b_dt_log"), sem("b_decay")
        cum, turned, xs_done, cb = sem("b_cum"), sem("b_turned"), sem("b_xs"), sem("b_cb")
        table_done, staged, spread, seg = sem("b_table"), sem("b_staged"), sem("b_spread"), sem("b_seg")
        exped, weighed, out_done, copied = sem("b_exped"), sem("b_weighed"), sem("b_out"), sem("b_copied")
        ready = sem("b_ready")
        QUADS = HB // 4
        norm_g = vecs[:, 0:D]
        dt_bias, a_log, d_skip = (vecs[:, D + HB * i:D + HB * (i + 1)] for i in range(3))
        cw = vecs[:, 1100:1100 + CT * (CONV + 1)]
        raw = m4[0:CT * (CONV + 1), 0:P]
        conv = view(m2, 0, CT, TOK)
        xs = view(m2, 3072, TT, D)
        cbm = view(m2, 5120, GB, 3 * P)
        xdt = view(m3, 0, TT, D)
        dtv = view(small, 0, TT, HB)
        tab = view(small, 64, 5, HB)
        st = small[:, 144:208]
        s_tab = view(vecs, 1200, 5, 4)
        e = view(m4, 0, 3, 4, P)
        w = view(m4, 1536, 3, 4, P)
        s_x = view(brT[:].rearrange("p k n -> p (k n)"), 0, TT, 4 * PB)
        s_cb = view(brT[:].rearrange("p k n -> p (k n)"), 512, 3, P)
        toT = ToFeatures(br, brT, 3)

        def load(self, pool, l):
            pool.dma_start(self.norm_g, A["ssm_norm_g"][bass.ds(l, 1), :].partition_broadcast(P)).then_inc(self.par, 16)
            for dst, name in ((self.dt_bias, "ssm_dt_bias"), (self.a_log, "ssm_A_log"), (self.d_skip, "ssm_D")):
                pool.dma_start(dst, A[name][bass.ds(l, 1), :].partition_broadcast(P)).then_inc(self.par, 16)
            taps = CT * CONV
            pool.dma_start(self.raw[0:taps], layer_of(A["ssm_conv_w"], l).rearrange("j (c p) -> (j c) p", p=P)).then_inc(self.par, 16)
            pool.dma_start(self.raw[taps:taps + CT], A["ssm_conv_b"][bass.ds(l, 1), :].rearrange("z (c p) -> (z c) p", p=P)).then_inc(self.par, 16)
            nc.gpsimd.memset(xbc[:, :, 0:CONV - 1], 0.0)

        def pool(self, pool, l):
            pool.wait_ge(self.table_done, l + 1)
            carry(pool)
            with pool.Fori(0, self.QUADS) as i:
                n = l * self.QUADS + i
                pool.wait_ge(self.out_done, n + 1)
                nc.gpsimd.tensor_copy(self.s_tab, self.tab[:, :, bass.ds(i * 4, 4)])
                nc.gpsimd.tensor_copy(self.s_x, self.xdt[:, :, bass.ds(i * 256, 256)])
                nc.gpsimd.tensor_copy(self.s_cb[:, :, :].rearrange("p b n -> p (b n)").unsqueeze(1), self.cbm[:, bass.ds(i // 2, 1), :]).then_inc(self.staged, 1)
            pool.wait_ge(pow_asked, power(l, 2))
            nc.gpsimd.tensor_tensor(self.st[:, 8:12], self.st[:, 4:8], const("minus_half")[:, 0:4], ALU.pow).then_inc(pow_done, 1)

        def pe(self, pe, l):
            n_par = CT * (CONV + 1)
            pe.wait_ge(self.par, l * 96 + 96)
            carry(pe)
            pe.transpose(ps[:, 7, 0:n_par], self.raw, ident[0:n_par, 0:n_par]).then_inc(self.cw_turned, 1)
            pe.wait_ge(self.decay_done, l + 1)
            d = self.tab[:, 0:2, :].rearrange("p t h -> p (t h)")
            pe.matmul(ps[:, 6, 0:2 * HB], const("upto"), d, start=True, stop=True)
            pe.matmul(ps[:, 6, 2 * HB:3 * HB], const("ones"), self.tab[:, 0, :], start=True, stop=True).then_inc(self.cum, 1)
            pe.wait_ge(self.silu_done, l + 1)
            for t in range(TT):
                for c in range(8):
                    ins = pe.transpose(ps[:, 2 * t + c // 4, (c % 4) * P:(c % 4 + 1) * P], self.conv[:, c, t * P:(t + 1) * P], ident)
                ins.then_inc(self.turned, 1)
            for g in range(GB):
                b_, c_ = self.conv[:, 8 + g, :], self.conv[:, 10 + g, :]
                pe.matmul(ps[:, 4 + g, 0:TOK], b_[:, 0:P], c_, start=True, stop=True)
                ins = pe.matmul(ps[:, 4 + g, TOK:384], b_[:, P:TOK], c_[:, P:TOK], start=True, stop=True)
            ins.then_inc(self.cb, 1)
            pe.wait_ge(self.table_done, l + 1)
            carry(pe)
            with pe.Fori(0, self.QUADS) as i:
                n = l * self.QUADS + i
                pe.wait_ge(self.staged, n + 1)
                for t in range(TT):
                    for h in range(4):
                        ins = pe.matmul(ps[:, t, h * P:(h + 1) * P], self.s_tab[:, t, h:h + 1].to_broadcast([P, P]), const("upto"), start=True, stop=True)
                ins.then_inc(self.spread, 1)
                pe.wait_ge(self.weighed, n + 1)
                for h in range(4):
                    cols = slice(h * PB, (h + 1) * PB)
                    pe.matmul(ps[:, 2, h * PB:(h + 1) * PB], self.w[:, 0, h, :], self.s_x[:, 0, cols], start=True, stop=True)
                    o1 = ps[:, 2, 256 + h * PB:256 + (h + 1) * PB]
                    pe.matmul(o1, self.w[:, 1, h, :], self.s_x[:, 0, cols], start=True, stop=False)
                    ins = pe.matmul(o1, self.w[:, 2, h, :], self.s_x[:, 1, cols], start=False, stop=True)
                ins.then_inc(self.out_done, 1)
            pe.wait_ge(self.ready, l + 1)
            self.toT.pe(pe, l)

        def act(self, act, l):
            act.wait_ge(self.cw_turned, l + 1)
            nc.scalar.copy(self.cw, ps[:, 7, 0:CT * (CONV + 1)]).then_inc(self.cw_done, 1)
            act.wait_ge(self.dt_abs, l + 1)
            nc.scalar.activation(self.st[:, 0:32], self.st[:, 0:32], ACT.Exp, scale=-1.0)
            nc.scalar.activation(self.a_log, self.a_log, ACT.Exp)
            act.drain()
            nc.scalar.activation(self.st[:, 0:32], self.st[:, 0:32], ACT.Ln, bias=1.0).then_inc(self.dt_log, 1)
            nc.scalar.activation(z_b, z_b, ACT.Silu)
            act.wait_ge(self.convolved, l + 1)
            nc.scalar.activation(self.conv, self.conv, ACT.Silu)
            act.drain()
            act.sem_inc(self.silu_done, 1)
            act.wait_ge(self.turned, l * 2 + 1)
            nc.scalar.copy(self.xs[:, 0, :], ps[:, 0:2, :].rearrange("p a b -> p (a b)"))
            act.wait_ge(self.turned, l * 2 + 2)
            nc.scalar.copy(self.xs[:, 1, :], ps[:, 2:4, :].rearrange("p a b -> p (a b)")).then_inc(self.xs_done, 1)
            with act.Fori(0, self.QUADS) as i:
                n = l * self.QUADS + i
                act.wait_ge(self.seg, n + 1)
                nc.scalar.activation(self.e, self.e, ACT.Exp).then_inc(self.exped, 1)
                act.wait_ge(self.out_done, n + 2)
                nc.scalar.copy(br[:, :, bass.ds(i * 256, 256)], view_bank(2, TT, 256))
            act.drain()
            act.sem_inc(self.copied, 1)
            self.toT.act(act, l)

        def dve(self, dve, l):
            V = nc.vector
            dve.wait_ge(self.par, l * 96 + 96)
            V.tensor_tensor(self.dtv, dt_raw, bc(self.dt_bias.unsqueeze(1), [P, TT, HB]), ALU.add)
            dve.drain()
            sp_ = view(self.st, 0, TT, HB)
            V.scalar_tensor_tensor(out=sp_, in0=self.dtv, scalar=-1.0, in1=self.dtv, op0=ALU.mult, op1=ALU.max).then_inc(self.dt_abs, 1)
            dve.wait_ge(self.cw_done, l + 1)
            carry(dve)
            convolve(dve, self.conv, xbc, lambda j, c: self.cw[:, bass.ds(c + j * CT, 1)], lambda c: self.cw[:, bass.ds(c + CONV * CT, 1)])
            dve.sem_inc(self.convolved, 1)
            dve.wait_ge(self.dt_log, l + 1)
            V.scalar_tensor_tensor(out=self.dtv, in0=self.dtv, scalar=0.0, in1=sp_, op0=ALU.max, op1=ALU.add)
            dve.drain()
            V.scalar_tensor_tensor(out=self.tab[:, 0:2, :], in0=self.dtv, scalar=-1.0, in1=bc(self.a_log.unsqueeze(1), [P, TT, HB]),
                                   op0=ALU.mult, op1=ALU.mult).then_inc(self.decay_done, 1)
            dve.wait_ge(self.cum, l + 1)
            V.tensor_copy(self.tab[:, 2:4, :], view_bank(6, 3, HB)[:, 0:2, :])
            dve.drain()
            V.tensor_tensor(self.tab[:, 4, :], self.tab[:, 2, :], view_bank(6, 3, HB)[:, 2, :], ALU.subtract)
            dve.wait_ge(self.xs_done, l + 1)
            for t in range(TT):
                V.tensor_tensor(self.xdt[:, t, :].rearrange("p (h d) -> p h d", d=PB), self.xs[:, t, :].rearrange("p (h d) -> p h d", d=PB),
                                bc(self.dtv[:, t, :].unsqueeze(2), [P, HB, PB]), ALU.mult)
            dve.wait_ge(self.cb, l + 1)
            for g in range(GB):
                c3 = view_bank(4 + g, 3, P)
                o3 = self.cbm[:, g, :].rearrange("p (b n) -> p b n", b=3)
                V.tensor_tensor(o3[:, 0:3:2, :], c3[:, 0:3:2, :], bc(const("upto").unsqueeze(1), [P, 2, P]), ALU.mult)
                V.tensor_copy(o3[:, 1, :], c3[:, 1, :])
            dve.drain()
            dve.sem_inc(self.table_done, 1)
            with dve.Fori(0, self.QUADS) as i:
                n = l * self.QUADS + i
                dve.wait_ge(self.spread, n + 1)
                for h in range(4):
                    cols = slice(h * P, (h + 1) * P)
                    for b, (bank, f) in enumerate(((0, 2), (1, 4), (1, 3))):
                        ins = V.tensor_scalar(self.e[:, b, h, :], ps[:, bank, cols], self.s_tab[:, f, h:h + 1], 0.0, ALU.subtract, ALU.min)
                ins.then_inc(self.seg, 1)
                dve.wait_ge(self.exped, n + 1)
                V.tensor_tensor(self.w, self.e, bc(self.s_cb.unsqueeze(2), [P, 3, 4, P]), ALU.mult).then_inc(self.weighed, 1)
            dve.wait_ge(self.copied, l + 1)
            sq = view(m3, 0, TT, D)
            for t in range(TT):
                V.tensor_tensor(sq[:, t, :].rearrange("p (h d) -> p h d", d=PB), self.xs[:, t, :].rearrange("p (h d) -> p h d", d=PB),
                                bc(self.d_skip.unsqueeze(2), [P, HB, PB]), ALU.mult)
            dve.drain()
            V.tensor_tensor(br[:], br[:], sq, ALU.add)
            dve.drain()
            V.tensor_tensor(br[:], br[:], z_b, ALU.mult)
            dve.drain()
            V.tensor_tensor(sq, br[:], br[:], ALU.mult)
            dve.drain()
            V.tensor_reduce(self.st[:, 0:4], sq.rearrange("p t (g n) -> p (t g) n", g=GB), AX.X, ALU.add)
            dve.drain()
            V.tensor_scalar(self.st[:, 4:8], self.st[:, 0:4], float(GB) / D, LN_EPS, ALU.mult, ALU.add).then_inc(pow_asked, 1)
            dve.wait_ge(pow_done, power(l, 2))
            groups = br[:].rearrange("p t (g n) -> p (t g) n", g=GB)
            V.tensor_tensor(groups, groups, bc(self.st[:, 8:12].unsqueeze(2), [P, TT * GB, D // GB]), ALU.mult)
            dve.drain()
            V.tensor_tensor(br[:], br[:], bc(self.norm_g.unsqueeze(1), [P, TT, D]), ALU.mult).then_inc(self.ready, 1)
            self.toT.dve(dve, l)

    class OutProduct:

        def __init__(self, q, w):
            self.q, self.w = q, w

        def sp(self, sp, l):
            for c in range(2):
                load_columns(sp, Block(l, 0, self.q + c), self.w(l), c * 512)

        def pe(self, pe, l):
            for c in range(2):
                b = Block(l, 0, self.q + c)
                pe.wait_ge(wide_full[b.slot], b.landed)
                for t in range(TT):
                    products(pe, ps[:, 2 * t + c, :], lambda k: brT[:, k, t * P:(t + 1) * P], b).then_inc(blk, 1)

    class TurnMerged:
        toT = ToFeatures(merged, brT, 4)

        def pe(self, pe, l):
            self.toT.pe(pe, l)

        def act(self, act, l):
            self.toT.act(act, l)

        def dve(self, dve, l):
            self.toT.dve(dve, l)

    def ffn(q, d, w_in, w_out):
        def gate_up(l, u):
            v = layer_of(A[w_in], l).rearrange("(k p) n -> p k n", p=P)
            return v[:, :, bass.ds(u * UF, UF)], v[:, :, bass.ds(u * UF + FF, UF)]

        def down_rows(l, u):
            return layer_of(A[w_out], l)[bass.ds(u * UF, UF), :].rearrange("(k p) n -> p k n", p=P)
        return Gated(UNITS, q, d, gate_up, down_rows)

    ffn1 = ffn(Q_FFN1, 0, "ffn1_w_in", "ffn1_w_out")
    ffn2 = ffn(Q_FFN2, UNITS, "ffn2_w_in", "ffn2_w_out")
    norm1 = Norm(0, 0, 0, FFN_RES, A["ln1_g"], A["ln1_b"])
    norm2 = Norm(1, 3, 5, 1.0, A["ln2_g"], A["ln2_b"])
    norm3 = Norm(2, 4, 6, FFN_RES, A["ln3_g"], A["ln3_b"])
    diff, stick, scan = DiffAttention(), StickBreaking(), Scan()
    merge_a, merge_c, merge_b = Merge(0, Q_OA, 0), Merge(1, Q_OC, 2), Merge(2, Q_OB, 1)
    out_product = OutProduct(Q_MO, lambda l: layer_of(A["w_mix_out"], l))
    turn_x = ToFeatures(x, xT, -1)
    turn_merged = TurnMerged()
    gate_par = sem("gate_par")

    LAYER = [ffn1, norm1, proj_a, diff, merge_a, proj_c, stick, merge_c, proj_b, scan, merge_b,
             turn_merged, out_product, norm2, ffn2, norm3]
    PHASES = len(LAYER)

    L2 = LAYERS
    rows2 = m4[0:72, 0:P]
    cols2 = vecs[:, 0:72]
    mod = view(vecs, 72, 6, KT)
    scales = view(vecs, 120, 2, KT)
    a_log2, dt_bias2 = vecs[:, 136:144], vecs[:, 144:152]
    out_norm2, q_norm2, k_norm2 = (vecs[:, 152 + HD2 * i:152 + HD2 * (i + 1)] for i in range(3))
    sinks2 = vecs[:, 344:352]
    router_w = view(vecs, 352, KT, ROUTE)
    router_b = vecs[:, 640:676]
    cw2 = vecs[:, 676:676 + CT * CONV]
    trig = view(vecs, 724, 2, TT, HD2 // 2)
    pos_i = ctx.enter_context(nc.sbuf_tensor("pos_i", [P, TT], I32))
    pos_f = vecs[:, 852:854]
    rows_par, cols_par = sem("rows_par"), sem("cols_par")
    gates2 = ln_par

    def load_second(pool):
        r = lambda name: A[name].rearrange("z (k p) -> (z k) p", p=P)
        at = 0
        for name, n in (("c_2", KT), ("b_ada_2", 6 * KT), ("norm_mix_2", KT), ("norm_ffn_2", KT)):
            pool.dma_start(rows2[at:at + n], r(name)).then_inc(rows_par, 16)
            at += n
        for dst, name in ((a_log2, "a_log_2"), (dt_bias2, "dt_bias_2"), (out_norm2, "gdn_out_norm_2"), (q_norm2, "q_norm_2"),
                          (k_norm2, "k_norm_2"), (sinks2, "sinks_2"), (router_b[:, 0:GROUPS], "b_group_2"), (router_b[:, GROUPS:], "b_router_2")):
            pool.dma_start(dst, A[name].partition_broadcast(P)).then_inc(cols_par, 16)
        for dst, name in ((router_w[:, :, 0:GROUPS], "w_group_2"), (router_w[:, :, GROUPS:], "w_router_2")):
            pool.dma_start(dst, A[name].rearrange("z (k p) n -> p (z k) n", p=P)).then_inc(cols_par, 16)
        for t in range(TT):
            pool.dma_start(pos_i[:, t:t + 1], A["positions_2"][:, t * P:(t + 1) * P].rearrange("b p -> p b")).then_inc(cols_par, 16)
    COLS_PAR = 16 * 12

    class Modulation:
        turned, c_done, copied = sem("ada_turned"), sem("ada_c"), sem("ada_copied")
        mod_done, spread = sem("ada_mod"), sem("ada_spread")

        def sp(self, sp, l):
            def block(i, c):
                load_columns(sp, Block(L2, i, Q_ADA + c), A["w_ada_2"].rearrange("z k n -> (z k) n"), i * 1024 + c * 512)
            pairs(sp, 12, block)

        def pe(self, pe, l):
            pe.wait_ge(rows_par, 64)
            pe.transpose(ps[:, 7, 0:72], rows2, ident[0:72, 0:72]).then_inc(self.turned, 1)
            pe.wait_ge(self.c_done, 1)

            def block(i, c):
                b = Block(L2, i, Q_ADA + c)
                pe.wait_ge(wide_full[b.slot], b.landed)
                pe.wait_ge(self.copied, i * 2 + (c + 1))
                for f in range(4):
                    for k in range(KT):
                        ins = pe.matmul(ps[:, c, f:f + 1], b.tile[:, k, f * P:(f + 1) * P], cols2[:, k:k + 1], start=(k == 0), stop=(k == KT - 1))
                    if f % 2:
                        ins.then_inc(blk, 1)
            pairs(pe, 12, block)
            pe.wait_ge(self.mod_done, 1)
            for g in range(2):
                for k in range(KT):
                    ins = pe.matmul(ps[:, 2 + 2 * g + k // 4, (k % 4) * P:(k % 4 + 1) * P], mod[:, 2 + 3 * g, k:k + 1].to_broadcast([P, P]), ident,
                                    start=True, stop=True)
            ins.then_inc(self.spread, 1)

        def act(self, act, l):
            act.wait_ge(self.turned, 1)
            nc.scalar.activation(cols2[:, 0:KT], ps[:, 7, 0:KT], ACT.Silu)
            nc.scalar.copy(cols2[:, KT:72], ps[:, 7, KT:72])
            act.drain()
            act.sem_inc(self.c_done, 1)
            flat = mod.rearrange("p a b -> p (a b)")

            def block(i, c):
                act.wait_ge(blk, Block(L2, i, Q_ADA + c).done(1))
                nc.scalar.copy(flat[:, bass.ds(i * 8 + c * 4, 4)], ps[:, c, 0:4]).then_inc(self.copied, 1)
            pairs(act, 12, block)
            act.wait_ge(self.spread, 1)
            for g in range(2):
                nc.scalar.copy(gates2[:, g, :], ps[:, 2 + 2 * g:4 + 2 * g, :].rearrange("p a b -> p (a b)"))

        def dve(self, dve, l):
            dve.wait_ge(self.copied, 14)
            flat = mod.rearrange("p a b -> p (a b)")
            nc.vector.tensor_tensor(flat, flat, cols2[:, KT:7 * KT], ALU.add)
            dve.drain()
            for g in range(2):
                nc.vector.scalar_tensor_tensor(out=scales[:, g, :], in0=mod[:, 1 + 3 * g, :], scalar=1.0, in1=cols2[:, (7 + g) * KT:(8 + g) * KT],
                                               op0=ALU.add, op1=ALU.mult)
            dve.drain()
            dve.sem_inc(self.mod_done, 1)

    class Modulate:

        def __init__(self, g, power, turn):
            self.g, self.power, self.turn = g, power, turn

        def add_gated(self, dve, gate):
            for t in range(TT):
                acc = ps[:, 2 * t:2 * t + 2, :].rearrange("p a b -> p (a b)")
                nc.vector.tensor_tensor(merged[:, t, :], gates2[:, gate, :], acc, ALU.mult)
            dve.drain()
            nc.vector.tensor_tensor(x[:], x[:], merged[:], ALU.add)
            dve.drain()

        def dve(self, dve, l):
            V = nc.vector
            if self.g:
                self.add_gated(dve, 0)
            V.tensor_tensor(merged[:], x[:], x[:], ALU.mult)
            dve.drain()
            V.tensor_reduce(small[:, 0:2], merged[:], AX.X, ALU.add)
            dve.drain()
            V.tensor_scalar(small[:, 2:4], small[:, 0:2], 1.0 / D, RMS_EPS, ALU.mult, ALU.add).then_inc(pow_asked, 1)
            dve.wait_ge(pow_done, power(L2, self.power))
            for t in range(TT):
                ins = V.tensor_scalar(merged[:, t, :], x[:, t, :], small[:, 4 + t:5 + t], None, ALU.mult)
            ins.then_inc(normed, 1)
            for k in (2, 3, 6, 7):
                dve.wait_ge(feat_turned, turn(L2, self.turn, k // 2))
                V.tensor_scalar(xT[:, k, :], ps[:, k // 2, (k % 2) * TOK:(k % 2 + 1) * TOK], scales[:, self.g, k:k + 1], mod[:, 3 * self.g, k:k + 1], ALU.mult, ALU.add)

        def pool(self, pool, l):
            pool.wait_ge(pow_asked, power(L2, self.power))
            nc.gpsimd.tensor_tensor(small[:, 4:6], small[:, 2:4], const("minus_half")[:, 0:2], ALU.pow).then_inc(pow_done, 1)

        def pe(self, pe, l):
            pe.wait_ge(normed, L2 * 3 + self.g + 1)
            for kp in range(4):
                for kk in range(2):
                    for t in range(TT):
                        k, at = 2 * kp + kk, kk * TOK + t * P
                        ins = pe.transpose(ps[:, kp, at:at + P], merged[:, t, k * P:(k + 1) * P], ident)
                ins.then_inc(feat_turned, 1)

        def act(self, act, l):
            for k in (0, 1, 4, 5):
                act.wait_ge(feat_turned, turn(L2, self.turn, k // 2))
                nc.scalar.activation(xT[:, k, :], ps[:, k // 2, (k % 2) * TOK:(k % 2 + 1) * TOK], ACT.Identity, bias=mod[:, 3 * self.g, k:k + 1], scale=scales[:, self.g, k:k + 1])

    z_2 = view(m1, 0, TT, G2W)
    q_s = view(m1, 1024, TT, G2W)
    ab_2 = view(m1, 2048 + CT * (TOK + CONV - 1), TT, 2 * H2)
    kv_s = view(m1, 5200, TT, 2 * KV2 * HD2)
    w_2 = lambda l: A["w_in_2"].rearrange("z k n -> (z k) n")
    proj_2 = Project("p2", Q_P2, [
        (3, "feat", 512, w_2, W2["qkv"], lambda part, i, c: xbc[:, c * 4 + part * 2:c * 4 + part * 2 + 2, CONV - 1:]),
        (1, "tok", 512, w_2, W2["z"], lambda part, i, c: z_2[:, part:part + 1, :]),
        (1, "tok", 2 * H2, w_2, W2["ab"], lambda part, i, c: ab_2[:, part:part + 1, :]),
        (1, "tok", 512, w_2, W2["sq"], lambda part, i, c: q_s[:, part:part + 1, :]),
        (1, "tok", 256, w_2, W2["skv"], lambda part, i, c: kv_s[:, part:part + 1, :])], first=L2)

    class DeltaRule:
        par, cw_turned, cw_done, convolved, silu_done = sem("g_par"), sem("g_cw_turned"), sem("g_cw"), sem("g_conv"), sem("g_silu")
        turned, tok_done = sem("g_turned"), sem("g_tok")
        ab_abs, ab_log, decay, cum, cums, exps, table = (sem(f"g_{n}") for n in ("ab_abs", "ab_log", "decay", "cum", "cums", "exps", "table"))
        staged, scaled, split, splitT = sem("g_staged"), sem("g_scaled"), sem("g_split"), sem("g_splitT")
        gram, seg, dec, mats = sem("g_gram"), sem("g_seg"), sem("g_dec"), sem("g_mats")
        level, lt, lt_done, upd, upd_done = sem("g_level"), sem("g_lt"), sem("g_lt_done"), sem("g_upd"), sem("g_upd_done")
        u0, u0_done, state, state_done = sem("g_u0"), sem("g_u0_done"), sem("g_state"), sem("g_state_done")
        vnew, vnew_done, out_done = sem("g_vnew"), sem("g_vnew_done"), sem("g_out")
        copied = sem("g_copied")
        QUADS = H2 // 4
        raw = m4[0:CT * CONV, 0:P]
        conv = view(m2, 0, CT, TOK)
        tok = view(m2, 3072, TT, 3 * G2W)
        stage = view(m3, 0, 3, TT, 256)
        kb, vb, kg, qg, kd = (view(m1, 2048 + 512 * i, TT, 256) for i in range(5))
        kT, kbT, qT = (view(m2, 1024 * i, 8, P)[0:HD2] for i in range(3))
        qgT = view(m3, 1536, 4, P)[0:HD2]
        e, mT, aT = (view(m4, 1024 * i, 8, P) for i in range(3))
        T, Tt = (merged[:, i, :].rearrange("p (s n) -> p s n", s=8) for i in range(2))
        xTf = xT[:].rearrange("p k n -> p (k n)")
        LT, LmT = view(xTf, 0, 8, P), view(xTf, 1024, 8, P)
        brf = brT[:].rearrange("p k n -> p (k n)")
        vn = view(brf, 0, 8, HD2)
        wT = view(brf, 512, 4, P)[0:HD2]
        st, stn = view(brf, 1024, 4, HD2)[0:HD2], view(brf, 1280, 4, HD2)[0:HD2]
        tab = view(small, 0, 6, TT, H2)
        s_tab = view(vecs, 900, 6, TT, 4)
        sp_ = view(small, 96, TT, H2)
        ss, rs_ = small[:, 112:144], small[:, 144:176]
        gend = view(small, 176, TT, H2)
        anu = small[:, 192:200]

        def load(self, pool, l):
            pool.dma_start(self.raw, A["conv_w_2"].rearrange("z j (c p) -> (z j c) p", p=P)).then_inc(self.par, 16)
            nc.gpsimd.memset(xbc[:, :, 0:CONV - 1], 0.0)

        def pool(self, pool, l):
            pool.wait_ge(pow_asked, power(L2, 1))
            nc.gpsimd.tensor_tensor(self.rs_, self.ss, const("minus_half")[:, 0:32], ALU.pow).then_inc(pow_done, 1)
            pool.wait_ge(self.table, 1)
            with pool.Fori(0, self.QUADS) as i:
                pool.wait_ge(self.out_done, i + 1)
                for j in range(3):
                    nc.gpsimd.tensor_copy(self.stage[:, j], self.tok[:, :, bass.ds(i * 256 + j * G2W, 256)])
                flat = self.tab.rearrange("p f t h -> p (f t) h")
                nc.gpsimd.tensor_copy(self.s_tab.rearrange("p f t h -> p (f t) h"), flat[:, :, bass.ds(i * 4, 4)]).then_inc(self.staged, 1)
            pool.wait_ge(pow_asked, power(L2, 2))
            nc.gpsimd.tensor_tensor(self.rs_[:, 0:16], self.ss[:, 0:16], const("minus_half")[:, 0:16], ALU.pow).then_inc(pow_done, 1)

        def pe(self, pe, l):
            n_par = CT * CONV
            pe.wait_ge(self.par, 16)
            pe.transpose(ps[:, 7, 0:n_par], self.raw, ident[0:n_par, 0:n_par]).then_inc(self.cw_turned, 1)
            pe.wait_ge(self.decay, 1)
            g2 = self.tab[:, 0].rearrange("p t h -> p (t h)")
            pe.matmul(ps[:, 6, 0:16], const("upto"), g2, start=True, stop=True)
            pe.matmul(ps[:, 6, 16:32], const("ones"), g2, start=True, stop=True).then_inc(self.cum, 1)
            pe.wait_ge(self.silu_done, 1)
            for t in range(TT):
                for c in range(CT):
                    ins = pe.transpose(ps[:, 3 * t + c // 4, (c % 4) * P:(c % 4 + 1) * P], self.conv[:, c, t * P:(t + 1) * P], ident)
                ins.then_inc(self.turned, 1)
            pe.wait_ge(self.table, 1)
            with pe.Fori(0, self.QUADS) as i:
                pe.wait_ge(self.scaled, i + 1)
                carry(pe)
                for n, src in enumerate((self.stage[:, 1], self.kb, self.stage[:, 0])):
                    for s in range(8):
                        t, h = divmod(s, 4)
                        ins = pe.transpose(ps[0:HD2, 2 * n + t, h * P:(h + 1) * P], src[:, t, h * HD2:(h + 1) * HD2], ident)
                for h in range(4):
                    ins = pe.transpose(ps[0:HD2, 6, h * P:(h + 1) * P], self.qg[:, 1, h * HD2:(h + 1) * HD2], ident)
                ins.then_inc(self.split, 1)
                pe.wait_ge(self.splitT, i * 2 + 2)
                for s in range(8):
                    t, h = divmod(s, 4)
                    cols = slice(h * P, (h + 1) * P)
                    pe.matmul(ps[:, t, cols], self.s_tab[:, 0, t, h:h + 1].to_broadcast([P, P]), const("upto"), start=True, stop=True)
                    pe.matmul(ps[:, 2 + t, cols], self.kT[:, s, :], self.kbT[:, s, :], start=True, stop=True)
                    ins = pe.matmul(ps[:, 4 + t, cols], self.kT[:, s, :], self.qT[:, s, :], start=True, stop=True)
                ins.then_inc(self.gram, 1)
                for v in range(LEVELS):
                    n = i * LEVELS + v
                    pe.wait_ge(self.level, n + 1)
                    for s in range(8):
                        ins = pe.matmul(ps[:, s // 4, (s % 4) * P:(s % 4 + 1) * P], self.LmT[:, s, :], self.T[:, s, :], start=True, stop=True)
                    ins.then_inc(self.lt, 1)
                    pe.wait_ge(self.lt_done, n * 2 + 2)
                    for s in range(8):
                        cols = slice((s % 4) * P, (s % 4 + 1) * P)
                        pe.matmul(ps[:, 2 + s // 4, cols], self.Tt[:, s, :], self.LT[:, s, :], start=True, stop=True)
                        ins = pe.matmul(ps[:, 4 + s // 4, cols], self.LT[:, s, :], self.Tt[:, s, :], start=True, stop=True)
                    ins.then_inc(self.upd, 1)
                pe.wait_ge(self.upd_done, i + 1)
                for h in range(4):
                    pe.matmul(ps[:, 6, h * HD2:(h + 1) * HD2], self.Tt[:, h, :], self.vb[:, 0, h * HD2:(h + 1) * HD2], start=True, stop=True)
                for h in range(4):
                    ins = pe.matmul(ps[0:HD2, 0, h * P:(h + 1) * P], self.kg[:, 1, h * HD2:(h + 1) * HD2], self.Tt[:, 4 + h, :], start=True, stop=True)
                ins.then_inc(self.u0, 1)
                pe.wait_ge(self.u0_done, i * 2 + 2)
                for h in range(4):
                    ins = pe.matmul(ps[0:HD2, 1, h * HD2:(h + 1) * HD2], self.kd[:, 0, h * HD2:(h + 1) * HD2], self.vn[:, h, :], start=True, stop=True)
                ins.then_inc(self.state, 1)
                pe.wait_ge(self.state_done, i + 1)
                for h in range(4):
                    o = ps[:, 2, h * HD2:(h + 1) * HD2]
                    pe.matmul(o, self.Tt[:, 4 + h, :], self.vb[:, 1, h * HD2:(h + 1) * HD2], start=True, stop=False)
                    ins = pe.matmul(o, self.wT[:, h, :], self.stn[:, h, :], start=False, stop=True)
                ins.then_inc(self.vnew, 1)
                pe.wait_ge(self.vnew_done, i + 1)
                for h in range(4):
                    pe.matmul(ps[:, 7, h * HD2:(h + 1) * HD2], self.aT[:, h, :], self.vn[:, h, :], start=True, stop=True)
                    o = ps[:, 7, 256 + h * HD2:256 + (h + 1) * HD2]
                    pe.matmul(o, self.qgT[:, h, :], self.st[:, h, :], start=True, stop=False)
                    ins = pe.matmul(o, self.aT[:, 4 + h, :], self.vn[:, 4 + h, :], start=False, stop=True)
                ins.then_inc(self.out_done, 1)

        def act(self, act, l):
            act.wait_ge(self.cw_turned, 1)
            nc.scalar.copy(cw2, ps[:, 7, 0:CT * CONV]).then_inc(self.cw_done, 1)
            act.wait_ge(self.ab_abs, 1)
            nc.scalar.activation(self.sp_, self.sp_, ACT.Exp, scale=-1.0)
            nc.scalar.activation(self.anu, a_log2, ACT.Exp)
            act.drain()
            nc.scalar.activation(self.sp_, self.sp_, ACT.Ln, bias=1.0).then_inc(self.ab_log, 1)
            act.wait_ge(self.convolved, 1)
            nc.scalar.activation(self.tab[:, 2], ab_2[:, :, H2:2 * H2], ACT.Sigmoid)
            nc.scalar.activation(z_2, z_2, ACT.Silu)
            nc.scalar.activation(self.conv, self.conv, ACT.Silu)
            act.drain()
            act.sem_inc(self.silu_done, 1)
            for t in range(TT):
                act.wait_ge(self.turned, t + 1)
                ins = nc.scalar.copy(self.tok[:, t, :], ps[:, 3 * t:3 * t + 3, :].rearrange("p a b -> p (a b)"))
            ins.then_inc(self.tok_done, 1)
            act.wait_ge(self.cums, 1)
            nc.scalar.activation(self.tab[:, 3], self.tab[:, 1], ACT.Exp)
            nc.scalar.activation(self.tab[:, 5], self.gend, ACT.Exp).then_inc(self.exps, 1)
            with act.Fori(0, self.QUADS) as i:
                act.wait_ge(self.split, i + 1)
                two = lambda b: ps[0:HD2, b:b + 2, :].rearrange("p a (h n) -> p (a h) n", n=P)
                nc.scalar.copy(self.kT, two(0))
                nc.scalar.copy(self.qgT, ps[0:HD2, 6, :].rearrange("p (h n) -> p h n", n=P)).then_inc(self.splitT, 1)
                act.wait_ge(self.seg, i + 1)
                nc.scalar.activation(self.e, self.e, ACT.Exp).then_inc(self.dec, 1)
                for v in range(LEVELS):
                    n = i * LEVELS + v
                    act.wait_ge(self.lt, n + 1)
                    nc.scalar.copy(self.LT[:, 0:4, :], view_bank(0, 4, P)).then_inc(self.lt_done, 1)
                act.wait_ge(self.u0, i + 1)
                nc.scalar.copy(self.wT, ps[0:HD2, 0, :].rearrange("p (h n) -> p h n", n=P)).then_inc(self.u0_done, 1)
                act.wait_ge(self.out_done, i + 2)
                nc.scalar.copy(br[:, :, bass.ds(i * 256, 256)], view_bank(7, TT, 256))
            act.drain()
            act.sem_inc(self.copied, 1)

        def dve(self, dve, l):
            V = nc.vector
            dve.wait_ge(cols_par, COLS_PAR)
            a = view(small, 200, TT, H2)
            V.tensor_tensor(a, ab_2[:, :, 0:H2], bc(dt_bias2.unsqueeze(1), [P, TT, H2]), ALU.add)
            dve.drain()
            V.scalar_tensor_tensor(out=self.sp_, in0=a, scalar=-1.0, in1=a, op0=ALU.mult, op1=ALU.max).then_inc(self.ab_abs, 1)
            dve.wait_ge(self.ab_log, 1)
            V.scalar_tensor_tensor(out=a, in0=a, scalar=0.0, in1=self.sp_, op0=ALU.max, op1=ALU.add)
            dve.drain()
            V.scalar_tensor_tensor(out=self.tab[:, 0], in0=a, scalar=-1.0, in1=bc(self.anu.unsqueeze(1), [P, TT, H2]), op0=ALU.mult, op1=ALU.mult).then_inc(self.decay, 1)
            dve.wait_ge(self.cw_done, 1)
            convolve(dve, self.conv, xbc, lambda j, c: cw2[:, bass.ds(c + j * CT, 1)])
            dve.sem_inc(self.convolved, 1)
            dve.wait_ge(self.cum, 1)
            G = view_bank(6, 2, TT, H2)
            V.tensor_copy(self.tab[:, 1], G[:, 0])
            dve.drain()
            V.tensor_tensor(self.gend, G[:, 1], self.tab[:, 1], ALU.subtract)
            dve.drain()
            dve.sem_inc(self.cums, 1)
            dve.wait_ge(self.tok_done, 1)
            sq = view(m3, 0, TT, 16, HD2)
            for t in range(TT):
                qk = self.tok[:, t, 0:1024].rearrange("p (h d) -> p h d", d=HD2)
                V.tensor_tensor(sq[:, t], qk, qk, ALU.mult)
            dve.drain()
            V.tensor_reduce(self.ss, sq.rearrange("p t h d -> p (t h) d"), AX.X, ALU.add)
            dve.drain()
            V.tensor_scalar(self.ss, self.ss, RMS_EPS, None, ALU.add).then_inc(pow_asked, 1)
            dve.wait_ge(self.exps, 1)
            V.tensor_tensor(self.tab[:, 4], self.tab[:, 2], self.tab[:, 3], ALU.mult)
            dve.wait_ge(pow_done, power(L2, 1))
            r2 = self.rs_.rearrange("p (t h) -> p t h", t=TT)
            V.tensor_scalar(r2[:, :, 0:H2], r2[:, :, 0:H2], HD2 ** -0.5, None, ALU.mult)
            dve.drain()
            for t in range(TT):
                qk = self.tok[:, t, 0:1024].rearrange("p (h d) -> p h d", d=HD2)
                V.tensor_tensor(qk, qk, bc(r2[:, t, :].unsqueeze(2), [P, 16, HD2]), ALU.mult)
            dve.drain()
            dve.sem_inc(self.table, 1)
            lev = consts[:, CONSTS["level1"][0]:CONSTS["level1"][0] + LEVELS * P].rearrange("p (v n) -> p v n", n=P)
            with dve.Fori(0, self.QUADS) as i:
                dve.wait_ge(self.staged, i + 1)
                heads = lambda ap: ap.rearrange("p t (h d) -> p (t h) d", d=HD2)
                f = lambda n: bc(self.s_tab[:, n].rearrange("p t h -> p (t h)").unsqueeze(2), [P, 8, HD2])
                V.tensor_tensor(heads(self.kb), heads(self.stage[:, 1]), f(2), ALU.mult)
                V.tensor_tensor(heads(self.vb), heads(self.stage[:, 2]), f(2), ALU.mult)
                V.tensor_tensor(heads(self.kg), heads(self.stage[:, 1]), f(4), ALU.mult)
                V.tensor_tensor(heads(self.qg), heads(self.stage[:, 0]), f(3), ALU.mult)
                V.tensor_tensor(heads(self.kd), heads(self.stage[:, 1]), f(5), ALU.mult).then_inc(self.scaled, 1)
                V.tensor_copy(self.T, bc(ident.unsqueeze(1), [P, 8, P]))
                V.tensor_copy(self.Tt, bc(ident.unsqueeze(1), [P, 8, P]))
                dve.wait_ge(self.split, i + 1)
                two = lambda b: ps[0:HD2, b:b + 2, :].rearrange("p a (h n) -> p (a h) n", n=P)
                V.tensor_copy(self.kbT, two(2))
                V.tensor_copy(self.qT, two(4)).then_inc(self.splitT, 1)
                dve.wait_ge(self.gram, i + 1)
                for s in range(8):
                    t, h = divmod(s, 4)
                    ins = V.tensor_scalar(self.e[:, s, :], ps[:, t, h * P:(h + 1) * P], self.s_tab[:, 1, t, h:h + 1], 0.0, ALU.subtract, ALU.min)
                ins.then_inc(self.seg, 1)
                dve.wait_ge(self.dec, i + 1)
                V.tensor_tensor(self.e, self.e, bc(const("upto").unsqueeze(1), [P, 8, P]), ALU.mult)
                dve.drain()
                big = lambda b: ps[:, b:b + 2, :].rearrange("p a (h n) -> p (a h) n", n=P)
                V.tensor_tensor(self.mT, self.e, big(2), ALU.mult)
                V.tensor_tensor(self.aT, self.e, big(4), ALU.mult)
                dve.drain()
                for v in range(LEVELS):
                    n = i * LEVELS + v
                    V.tensor_tensor(self.LmT, self.mT, bc(lev[:, v:v + 1, :], [P, 8, P]), ALU.mult).then_inc(self.level, 1)
                    dve.wait_ge(self.lt, n + 1)
                    V.tensor_copy(self.LT[:, 4:8, :], view_bank(1, 4, P)).then_inc(self.lt_done, 1)
                    dve.wait_ge(self.upd, n + 1)
                    V.tensor_tensor(self.T, self.T, big(2), ALU.subtract)
                    V.tensor_tensor(self.Tt, self.Tt, big(4), ALU.subtract)
                    dve.drain()
                dve.sem_inc(self.upd_done, 1)
                dve.wait_ge(self.u0, i + 1)
                V.tensor_copy(self.vn[:, 0:4, :], ps[:, 6, 0:256].rearrange("p (h n) -> p h n", n=HD2)).then_inc(self.u0_done, 1)
                dve.wait_ge(self.state, i + 1)
                V.tensor_copy(self.st, ps[0:HD2, 1, 0:256].rearrange("p (h n) -> p h n", n=HD2))
                V.tensor_scalar(self.stn, ps[0:HD2, 1, 0:256].rearrange("p (h n) -> p h n", n=HD2), -1.0, None, ALU.mult).then_inc(self.state_done, 1)
                dve.wait_ge(self.vnew, i + 1)
                V.tensor_copy(self.vn[:, 4:8, :], ps[:, 2, 0:256].rearrange("p (h n) -> p h n", n=HD2)).then_inc(self.vnew_done, 1)
            dve.wait_ge(self.copied, 1)
            o = br[:, :, 0:G2W]
            sq = view(m3, 0, TT, G2W)
            V.tensor_tensor(sq, o, o, ALU.mult)
            dve.drain()
            V.tensor_reduce(self.ss[:, 0:16], sq.rearrange("p t (h d) -> p (t h) d", d=HD2), AX.X, ALU.add)
            dve.drain()
            V.tensor_scalar(self.ss[:, 0:16], self.ss[:, 0:16], 1.0 / HD2, RMS_EPS, ALU.mult, ALU.add).then_inc(pow_asked, 1)
            dve.wait_ge(pow_done, power(L2, 2))
            for t in range(TT):
                oh = o[:, t, :].rearrange("p (h d) -> p h d", d=HD2)
                V.tensor_tensor(oh, oh, bc(self.rs_[:, t * H2:(t + 1) * H2].unsqueeze(2), [P, H2, HD2]), ALU.mult)
            dve.drain()
            for t in range(TT):
                oh = o[:, t, :].rearrange("p (h d) -> p h d", d=HD2)
                V.tensor_tensor(oh, oh, bc(out_norm2.unsqueeze(1), [P, H2, HD2]), ALU.mult)
            dve.drain()
            V.tensor_tensor(o, o, z_2, ALU.mult)

    class WindowAttention:
        roped, angles, trig_done = sem("s_roped"), sem("s_angles"), sem("s_trig")
        staged, turned, qT_done, scored, masked, exped = (sem(f"s_{n}") for n in ("staged", "turned", "qT", "scored", "masked", "exped"))
        weighed, w_turned, wT_done, out_done, ready = (sem(f"s_{n}") for n in ("weighed", "w_turned", "wT", "out", "ready"))
        HEADS = H2 + KV2
        qk = view(m2, 0, TT, HEADS, HD2)
        sq = view(m3, 0, TT, HEADS, HD2)
        half = HD2 // 2
        GQ = H2 // KV2
        q, k, v = view(m4, 0, TT, 256), view(m4, 512, TT, HD2), view(m4, 640, TT, HD2)
        qT, kT = view(m4, 768, GQ, TOK)[0:HD2], m4[0:HD2, 1792:1792 + TOK]
        s0, s1 = view(m2, 1280, GQ, P), view(m2, 1792, GQ, TOK)
        wT = view(m2, 2816, 3 * GQ, P)
        ss, rs_ = small[:, 0:20], small[:, 20:40]
        nmx, sums, esink, inv = (view(small, 48 + 8 * i, TT, H2 // KV2) for i in range(4))
        s_sink = small[:, 88:92]
        ang = view(m3, 1280, 2, TT, HD2 // 2)
        turns = view(m3, 1408, 2, TT, HD2 // 2)
        toT = ToFeatures(br, brT, 1)

        def pool(self, pool, l):
            pool.wait_ge(pow_asked, power(L2, 3))
            nc.gpsimd.tensor_tensor(self.rs_, self.ss, const("minus_half")[:, 0:20], ALU.pow).then_inc(pow_done, 1)
            pool.wait_ge(self.roped, 1)
            with pool.Fori(0, KV2) as g:
                pool.wait_ge(self.out_done, g + 1)
                for t in range(TT):
                    nc.gpsimd.tensor_copy(self.q[:, t, :].rearrange("p (h d) -> p h d", d=HD2), self.qk[:, t, bass.ds(g * 4, 4), :])
                nc.gpsimd.tensor_copy(self.k.unsqueeze(2), self.qk[:, :, bass.ds(g + H2, 1), :])
                nc.gpsimd.tensor_copy(self.s_sink, sinks2[:, bass.ds(g * 4, 4)])
                nc.gpsimd.tensor_copy(self.v, kv_s[:, :, bass.ds(g * HD2 + KV2 * HD2, HD2)]).then_inc(self.staged, 1)

        def pe(self, pe, l):
            with pe.Fori(0, KV2) as g:
                pe.wait_ge(self.staged, g + 1)
                carry(pe)
                for h in range(self.GQ):
                    for t in range(TT):
                        at = (h % 2) * TOK + t * P
                        pe.transpose(ps[0:HD2, h // 2, at:at + P], self.q[:, t, h * HD2:(h + 1) * HD2], ident)
                for t in range(TT):
                    ins = pe.transpose(ps[0:HD2, 2, t * P:(t + 1) * P], self.k[:, t, :], ident)
                ins.then_inc(self.turned, 1)
                pe.wait_ge(self.qT_done, g * 2 + 2)
                for h in range(self.GQ):
                    pe.matmul(ps[:, 3, h * P:(h + 1) * P], self.qT[:, h, 0:P], self.kT[:, 0:P], start=True, stop=True)
                    ins = pe.matmul(ps[:, 4 + h // 2, (h % 2) * TOK:(h % 2 + 1) * TOK], self.qT[:, h, P:TOK], self.kT, start=True, stop=True)
                ins.then_inc(self.scored, 1)
                pe.wait_ge(self.weighed, g + 1)
                for h in range(self.GQ):
                    pe.transpose(ps[:, 0, h * P:(h + 1) * P], self.s0[:, h, :], ident)
                    for b in range(2):
                        ins = pe.transpose(ps[:, 1 + b, h * P:(h + 1) * P], self.s1[:, h, b * P:(b + 1) * P], ident)
                ins.then_inc(self.w_turned, 1)
                pe.wait_ge(self.wT_done, g + 1)
                for h in range(self.GQ):
                    pe.matmul(ps[:, 6, h * HD2:(h + 1) * HD2], self.wT[:, h, :], self.v[:, 0, :], start=True, stop=True)
                    o = ps[:, 6, 256 + h * HD2:256 + (h + 1) * HD2]
                    pe.matmul(o, self.wT[:, 4 + h, :], self.v[:, 0, :], start=True, stop=False)
                    ins = pe.matmul(o, self.wT[:, 8 + h, :], self.v[:, 1, :], start=False, stop=True)
                ins.then_inc(self.out_done, 1)
            pe.wait_ge(self.ready, 1)
            self.toT.pe(pe, L2)

        def act(self, act, l):
            act.wait_ge(self.angles, 1)
            nc.scalar.activation(trig, self.ang, ACT.Sin).then_inc(self.trig_done, 1)
            with act.Fori(0, KV2) as g:
                act.wait_ge(self.turned, g + 1)
                nc.scalar.mul(self.qT, ps[0:HD2, 0:2, :].rearrange("p a (h n) -> p (a h) n", n=TOK), HD2 ** -0.5).then_inc(self.qT_done, 1)
                act.wait_ge(self.masked, g + 1)
                for h in range(self.GQ):
                    nc.scalar.activation(self.s0[:, h, :], self.s0[:, h, :], ACT.Exp, bias=self.nmx[:, 0, h:h + 1], accum_out=self.sums[:, 0, h:h + 1])
                    nc.scalar.activation(self.s1[:, h, :], self.s1[:, h, :], ACT.Exp, bias=self.nmx[:, 1, h:h + 1], accum_out=self.sums[:, 1, h:h + 1])
                nc.scalar.activation(self.esink, self.esink, ACT.Exp).then_inc(self.exped, 1)
                act.wait_ge(self.w_turned, g + 1)
                nc.scalar.copy(self.wT, ps[:, 0:3, :].rearrange("p a (h n) -> p (a h) n", n=P)).then_inc(self.wT_done, 1)
                act.wait_ge(self.out_done, g + 2)
                nc.scalar.copy(br[:, :, bass.ds(g * 256 + G2W, 256)], view_bank(6, TT, 256))
            act.drain()
            act.sem_inc(self.ready, 1)
            self.toT.act(act, L2)

        def dve(self, dve, l):
            V = nc.vector
            V.tensor_copy(pos_f, pos_i[:])
            dve.drain()
            for t in range(TT):
                V.tensor_scalar(self.ang[:, 1, t, :], const("inv_freq"), pos_f[:, t:t + 1], None, ALU.mult)
            dve.drain()
            magic = 1.5 * 2.0 ** 23
            a1, a0 = self.ang[:, 1], self.ang[:, 0]
            V.tensor_scalar(self.turns[:, 0], a1, 0.5 / np.pi, 0.25, ALU.mult, ALU.add)
            V.tensor_scalar(self.turns[:, 1], a1, 0.5 / np.pi, None, ALU.mult)
            V.tensor_copy(a0, a1)
            dve.drain()
            V.tensor_scalar(self.turns, self.turns, magic, None, ALU.add)
            dve.drain()
            V.tensor_scalar(self.turns, self.turns, magic, None, ALU.subtract)
            dve.drain()
            rest = 2.0 * np.pi
            flat = lambda ap: ap.rearrange("p a t n -> p (a t n)")
            for bits in (2.0 ** 5, 2.0 ** 17, None):
                part = rest if bits is None else np.floor(rest * bits) / bits
                rest -= part
                V.scalar_tensor_tensor(out=flat(self.ang), in0=flat(self.turns), scalar=-float(part), in1=flat(self.ang), op0=ALU.mult, op1=ALU.add)
                dve.drain()
            V.tensor_scalar(a0, a0, 0.5 * np.pi, None, ALU.add)
            dve.drain()
            V.tensor_scalar(flat(self.ang), flat(self.ang), 3.1415925, -3.1415925, ALU.min, ALU.max).then_inc(self.angles, 1)
            heads = lambda ap: ap.rearrange("p t (h d) -> p t h d", d=HD2)
            qh, kh = heads(q_s), heads(kv_s[:, :, 0:KV2 * HD2])
            V.tensor_tensor(self.sq[:, :, 0:H2, :], qh, qh, ALU.mult)
            V.tensor_tensor(self.sq[:, :, H2:, :], kh, kh, ALU.mult)
            dve.drain()
            V.tensor_reduce(self.ss, self.sq.rearrange("p t h d -> p (t h) d"), AX.X, ALU.add)
            dve.drain()
            V.tensor_scalar(self.ss, self.ss, 1.0 / HD2, RMS_EPS, ALU.mult, ALU.add).then_inc(pow_asked, 1)
            dve.wait_ge(pow_done, power(L2, 3))
            r = self.rs_.rearrange("p (t h) -> p t h", t=TT)
            for t in range(TT):
                V.tensor_tensor(self.qk[:, t, 0:H2, :], qh[:, t], bc(r[:, t, 0:H2].unsqueeze(2), [P, H2, HD2]), ALU.mult)
                V.tensor_tensor(self.qk[:, t, H2:, :], kh[:, t], bc(r[:, t, H2:].unsqueeze(2), [P, KV2, HD2]), ALU.mult)
            dve.drain()
            for t in range(TT):
                V.tensor_tensor(self.qk[:, t, 0:H2, :], self.qk[:, t, 0:H2, :], bc(q_norm2.unsqueeze(1), [P, H2, HD2]), ALU.mult)
                V.tensor_tensor(self.qk[:, t, H2:, :], self.qk[:, t, H2:, :], bc(k_norm2.unsqueeze(1), [P, KV2, HD2]), ALU.mult)
            dve.wait_ge(self.trig_done, 1)
            dve.drain()
            for t in range(TT):
                a, b = self.qk[:, t, :, 0:self.half], self.qk[:, t, :, self.half:]
                cos, sin = (bc(trig[:, c, t, :].unsqueeze(1), [P, self.HEADS, self.half]) for c in range(2))
                ac, bs, bcs, as_ = (view(m3, 320 * i, self.HEADS, self.half) for i in range(4))
                V.tensor_tensor(ac, a, cos, ALU.mult)
                V.tensor_tensor(bs, b, sin, ALU.mult)
                V.tensor_tensor(bcs, b, cos, ALU.mult)
                V.tensor_tensor(as_, a, sin, ALU.mult)
                dve.drain()
                V.tensor_tensor(a, ac, bs, ALU.subtract)
                V.tensor_tensor(b, bcs, as_, ALU.add)
                dve.drain()
            dve.sem_inc(self.roped, 1)
            causal, window = (bc(const(n).unsqueeze(1), [P, self.GQ, P]) for n in ("causal_add", "window_add"))
            with dve.Fori(0, KV2) as g:
                dve.wait_ge(self.turned, g + 1)
                V.tensor_copy(self.kT, ps[0:HD2, 2, 0:TOK]).then_inc(self.qT_done, 1)
                dve.wait_ge(self.scored, g + 1)
                own = ps[:, 4:6, :].rearrange("p a (h n) -> p (a h) n", n=TOK)
                V.tensor_tensor(self.s0, view_bank(3, self.GQ, P), causal, ALU.add)
                V.tensor_tensor(self.s1[:, :, 0:P], own[:, :, 0:P], window, ALU.add)
                V.tensor_tensor(self.s1[:, :, P:TOK], own[:, :, P:TOK], causal, ALU.add)
                dve.drain()
                V.tensor_reduce(self.nmx[:, 0, :], self.s0, AX.X, ALU.max)
                V.tensor_reduce(self.nmx[:, 1, :], self.s1, AX.X, ALU.max)
                dve.drain()
                sk = bc(self.s_sink.unsqueeze(1), [P, TT, self.GQ])
                V.tensor_tensor(self.nmx, self.nmx, sk, ALU.max)
                dve.drain()
                V.tensor_scalar(self.nmx, self.nmx, -1.0, None, ALU.mult)
                dve.drain()
                V.tensor_tensor(self.esink, self.nmx, sk, ALU.add)
                dve.drain()
                dve.sem_inc(self.masked, 1)
                dve.wait_ge(self.exped, g + 1)
                V.tensor_tensor(self.inv, self.sums, self.esink, ALU.add)
                dve.drain()
                V.reciprocal(self.inv, self.inv)
                dve.drain()
                V.tensor_tensor(self.s0, self.s0, bc(self.inv[:, 0, :].unsqueeze(2), [P, self.GQ, P]), ALU.mult)
                V.tensor_tensor(self.s1, self.s1, bc(self.inv[:, 1, :].unsqueeze(2), [P, self.GQ, TOK]), ALU.mult).then_inc(self.weighed, 1)
            self.toT.dve(dve, L2)

    combine = view(vecs, 1000, TT, EXPERTS)

    class Router:
        logits_done, maxed, exped, diffed, exped2 = (sem(f"r_{n}") for n in ("logits", "maxed", "exped", "diffed", "exped2"))
        lg = view(m3, 0, TT, ROUTE)
        sub = view(m3, 80, TT, GROUPS)
        hot = view(m3, 100, TT, GROUPS)
        cnt = view(m3, 120, TT, PER_GROUP)
        prod = view(m3, 160, TT, GROUPS, PER_GROUP)
        ing, hot1, hot2, tmp = (view(m3, 256 + 16 * i, TT, PER_GROUP) for i in range(4))
        gm, gs, m1_, m2_, e2, w1, w2 = (m3[:, 340 + 2 * i:342 + 2 * i] for i in range(7))

        def pe(self, pe, l):
            for t in range(TT):
                for k in range(KT):
                    ins = pe.matmul(ps[:, 4, t * ROUTE:(t + 1) * ROUTE], xT[:, k, t * P:(t + 1) * P], router_w[:, k, :], start=(k == 0), stop=(k == KT - 1))
            ins.then_inc(self.logits_done, 1)

        def act(self, act, l):
            act.wait_ge(self.maxed, 1)
            nc.scalar.activation(self.sub, self.sub, ACT.Exp).then_inc(self.exped, 1)
            act.wait_ge(self.diffed, 1)
            nc.scalar.activation(self.e2, self.e2, ACT.Exp).then_inc(self.exped2, 1)

        def first_of(self, dve, hot, values, top, n):
            V = nc.vector
            V.tensor_tensor(hot, values, bc(top.unsqueeze(2), [P, TT, n]), ALU.is_equal)
            dve.drain()
            for t in range(TT):
                V.tensor_tensor_scan(self.cnt[:, t, 0:n], const("ones")[:, 0:n], hot[:, t, :], 0.0, ALU.mult, ALU.add)
            dve.drain()
            V.scalar_tensor_tensor(out=hot, in0=self.cnt[:, :, 0:n], scalar=1.0, in1=hot, op0=ALU.is_equal, op1=ALU.mult)
            dve.drain()

        def dve(self, dve, l):
            V = nc.vector
            dve.wait_ge(self.logits_done, 1)
            V.tensor_tensor(self.lg, view_bank(4, TT, ROUTE), bc(router_b.unsqueeze(1), [P, TT, ROUTE]), ALU.add)
            dve.drain()
            gl = self.lg[:, :, 0:GROUPS]
            V.tensor_reduce(self.gm, gl, AX.X, ALU.max)
            dve.drain()
            V.tensor_tensor(self.sub, gl, bc(self.gm.unsqueeze(2), [P, TT, GROUPS]), ALU.subtract).then_inc(self.maxed, 1)
            self.first_of(dve, self.hot, gl, self.gm, GROUPS)
            for t in range(TT):
                V.tensor_tensor(self.prod[:, t], self.lg[:, t, GROUPS:].rearrange("p (g e) -> p g e", g=GROUPS),
                                bc(self.hot[:, t, :].unsqueeze(2), [P, GROUPS, PER_GROUP]), ALU.mult)
            dve.drain()
            for t in range(TT):
                V.tensor_reduce(self.ing[:, t, :], self.prod[:, t].rearrange("p g e -> p e g"), AX.X, ALU.add)
            dve.drain()
            V.tensor_reduce(self.m1_, self.ing, AX.X, ALU.max)
            dve.drain()
            self.first_of(dve, self.hot1, self.ing, self.m1_, PER_GROUP)
            V.scalar_tensor_tensor(out=self.tmp, in0=self.hot1, scalar=NEG, in1=self.ing, op0=ALU.mult, op1=ALU.add)
            dve.drain()
            V.tensor_reduce(self.m2_, self.tmp, AX.X, ALU.max)
            dve.drain()
            V.tensor_tensor(self.e2, self.m2_, self.m1_, ALU.subtract).then_inc(self.diffed, 1)
            self.first_of(dve, self.hot2, self.tmp, self.m2_, PER_GROUP)
            dve.wait_ge(self.exped, 1)
            V.tensor_reduce(self.gs, self.sub, AX.X, ALU.add)
            dve.wait_ge(self.exped2, 1)
            V.tensor_scalar(self.w1, self.e2, 1.0, None, ALU.add)
            dve.drain()
            V.tensor_tensor(self.w1, self.w1, self.gs, ALU.mult)
            dve.drain()
            V.reciprocal(self.w1, self.w1)
            dve.drain()
            V.tensor_tensor(self.w2, self.w1, self.e2, ALU.mult)
            dve.drain()
            V.tensor_tensor(self.hot1, self.hot1, bc(self.w1.unsqueeze(2), [P, TT, PER_GROUP]), ALU.mult)
            V.tensor_tensor(self.hot2, self.hot2, bc(self.w2.unsqueeze(2), [P, TT, PER_GROUP]), ALU.mult)
            dve.drain()
            V.tensor_tensor(self.hot1, self.hot1, self.hot2, ALU.add)
            dve.drain()
            for t in range(TT):
                V.tensor_tensor(combine[:, t, :].rearrange("p (g e) -> p g e", g=GROUPS), bc(self.hot1[:, t:t + 1, :], [P, GROUPS, PER_GROUP]),
                                bc(self.hot[:, t, :].unsqueeze(2), [P, GROUPS, PER_GROUP]), ALU.mult)

    def expert_in(l, u):
        return tuple(A[n][0, bass.ds(u, 1)].rearrange("z (k p) n -> p (z k) n", p=P) for n in ("w_gate_2", "w_up_2"))

    def expert_out(l, u):
        return A["w_down_2"][0, bass.ds(u, 1)].rearrange("z (k p) n -> p (z k) n", p=P)

    experts = Gated(EXPERTS, Q_MOE, 0, expert_in, expert_out, weight=lambda t, u: combine[:, t, bass.ds(u, 1)])
    modulation, delta, window, router = Modulation(), DeltaRule(), WindowAttention(), Router()
    mod_mix, mod_ffn = Modulate(0, 0, 0), Modulate(1, 4, 2)
    out_2 = OutProduct(Q_W2, lambda l: A["w_out_2"].rearrange("z k n -> (z k) n"))

    class Last:

        def dve(self, dve, l):
            mod_ffn.add_gated(dve, 1)

    last = Last()
    SECOND = [modulation, mod_mix, proj_2, delta, window, out_2, mod_ffn, router, experts, last]

    in_par = sem("in_par")
    zeroed = sem("zeroed")
    stored = sem("stored")
    block = ctx.enter_context(nc.Block())

    @block.sync
    def _(sp):
        sp.dma_start(consts[:], A["shape_constants"]).then_inc(in_par, 16)
        sp.dma_start(x[:], A["x"].rearrange("b (t p) d -> p (b t) d", p=P)).then_inc(in_par, 16)
        with sp.Fori(0, LAYERS) as l:
            for phase in (ffn1, proj_a, merge_a, proj_c, merge_c, proj_b, merge_b, out_product, ffn2):
                phase.sp(sp, l)
        for phase in (modulation, proj_2, out_2, experts):
            phase.sp(sp, L2)
        sp.wait_ge(phase_left, (LAYERS * PHASES + len(SECOND) + 1) * 4)
        sp.dma_start(out.rearrange("b (t p) d -> p (b t) d", p=P), x[:]).then_inc(stored, 16)
        sp.wait_ge(stored, 16)

    @block.tensor
    def _(pe):
        pe.sem_inc(blk, BLK0)
        pe.sem_inc(dn, DN0)
        pe.sem_inc(hid_turned, 2)
        for s in (diff, stick, scan, delta, window):
            pe.sem_inc(s.out_done, 1)
        pe.wait_ge(in_par, 32)
        pe.wait_ge(zeroed, 1)
        turn_x.pe(pe, 0)
        leave(pe, 0)
        with pe.Fori(0, LAYERS) as l:
            for n, phase in enumerate(LAYER):
                phase.pe(pe, l)
                leave(pe, l * PHASES + n + 1)
        for n, phase in enumerate(SECOND):
            if phase not in (last,):
                phase.pe(pe, L2)
            leave(pe, LAYERS * PHASES + n + 1)

    @block.scalar
    def _(act):
        act.sem_inc(hidT_done, 2)
        for p_ in (proj_a, proj_c, proj_b, proj_2):
            p_.start(act, None)
        act.sem_inc(modulation.copied, 2)
        turn_x.act(act, 0)
        leave(act, 0)
        with act.Fori(0, LAYERS) as l:
            for n, phase in enumerate(LAYER):
                if phase is not out_product:
                    phase.act(act, l)
                leave(act, l * PHASES + n + 1)
        for n, phase in enumerate(SECOND):
            if phase not in (out_2, last,):
                phase.act(act, L2)
            leave(act, LAYERS * PHASES + n + 1)

    @block.vector
    def _(dve):
        dve.sem_inc(hid_done, 2)
        for p_ in (proj_a, proj_c, proj_b, proj_2):
            p_.start(None, dve)
        nc.vector.memset(zrow[:], 0.0).then_inc(zeroed, 1)
        turn_x.dve(dve, 0)
        leave(dve, 0)
        with dve.Fori(0, LAYERS) as l:
            for n, phase in enumerate(LAYER):
                if phase is not out_product:
                    phase.dve(dve, l)
                leave(dve, l * PHASES + n + 1)
        for n, phase in enumerate(SECOND):
            if phase not in (out_2,):
                phase.dve(dve, L2)
            leave(dve, LAYERS * PHASES + n + 1)

    @block.gpsimd
    def _(pool):
        pool.wait_ge(in_par, 32)
        leave(pool, 0)
        with pool.Fori(0, LAYERS) as l:
            for n, phase in enumerate(LAYER):
                if phase is ffn1:
                    norm1.load(pool, l)
                elif phase is proj_a:
                    norm2.load(pool, l)
                    diff.load(pool, l)
                    pool.dma_start(gate_row[:], A["gate_bias"].rearrange("l r d -> l (r d)")[bass.ds(l, 1), :]).then_inc(gate_par, 16)
                elif phase is proj_b:
                    scan.load(pool, l)
                elif phase is ffn2:
                    norm3.load(pool, l)
                elif phase is merge_a:
                    pool.wait_ge(gate_par, l * 16 + 16)
                    carry(pool)
                if phase in (norm1, norm2, norm3, diff, stick, scan):
                    phase.pool(pool, l)
                leave(pool, l * PHASES + n + 1)
        for n, phase in enumerate(SECOND):
            if phase is modulation:
                load_second(pool)
            elif phase is proj_2:
                delta.load(pool, L2)
            if phase in (mod_mix, delta, window, mod_ffn):
                phase.pool(pool, L2)
            leave(pool, LAYERS * PHASES + n + 1)

    ctx.close()


NAMES = ["x", "ffn1_w_in", "ffn1_w_out", "ln1_g", "ln1_b", "w_mix_in", "gate_bias", "diff_lambda", "diff_subln_g",
         "ssm_conv_w", "ssm_conv_b", "ssm_dt_bias", "ssm_A_log", "ssm_D", "ssm_norm_g", "w_branch", "w_mix_out",
         "ln2_g", "ln2_b", "ffn2_w_in", "ffn2_w_out", "ln3_g", "ln3_b", "c_2", "positions_2", "w_ada_2", "b_ada_2",
         "norm_mix_2", "w_in_2", "conv_w_2", "a_log_2", "dt_bias_2", "gdn_out_norm_2", "q_norm_2", "k_norm_2",
         "sinks_2", "w_out_2", "norm_ffn_2", "w_group_2", "b_group_2", "w_router_2", "b_router_2", "w_gate_2",
         "w_up_2", "w_down_2"]


def kernel(**inputs):
    import concourse.bacc as bacc
    from concourse.bass_utils import run_bass_kernel_spmd
    arrays = {n: np.ascontiguousarray(inputs[n]) for n in NAMES}
    arrays["shape_constants"] = SHAPE_CONSTANTS
    nc = bacc.Bacc("TRN2", target_bir_lowering=False, num_devices=1)
    aps = {n: nc.dram_tensor(f"in_{n}", a.shape, mybir.dt.from_np(a.dtype), kind="ExternalInput").ap() for n, a in arrays.items()}
    out = nc.dram_tensor("out", (1, TOK, D), F32, kind="ExternalOutput").ap()
    build(nc, aps, out)
    r = run_bass_kernel_spmd(nc, [{f"in_{n}": a for n, a in arrays.items()}], core_ids=[0])
    return r.results[0]["out"]
```

```python
from contextlib import ExitStack

import numpy as np

import concourse.bass as bass
from concourse import mybir

F32 = mybir.dt.float32
F32R = mybir.dt.float32r
I32 = mybir.dt.int32
ACT = mybir.ActivationFunctionType
ALU = mybir.AluOpType
AX = mybir.AxisListType

P = 128
TT = 2
TOK = P * TT
D = 1024
KT = D // P
LAYERS = 2
FF = 2816
UF = 256
UNITS = FF // UF
ALPHA = (2 * LAYERS) ** 0.25
FFN_RES = 0.5
LN_EPS = 1e-5
RMS_EPS = 1e-6
NEG = -1e30

HA, HDA, ROT_A = 8, 64, 16
HB, PB, GB, NB, CONV = 16, 64, 2, 128, 4
CONV_DIM = HB * PB + 2 * GB * NB
CT = CONV_DIM // P
HC, HDC = 16, 64
C_QA, C_KA, C_VA, C_Z, C_XBC = 0, 1024, 2048, 3072, 4096
C_DT = C_XBC + CONV_DIM
C_QC = C_DT + HB
C_KC, C_VC, C_G = C_QC + 1024, C_QC + 2048, C_QC + 3072

H2, HD2, KV2 = 8, 64, 2
G2W = H2 * HD2
EXPERTS, GROUPS, PER_GROUP = 32, 4, 8
ROUTE = GROUPS + EXPERTS
W2 = dict(qkv=0, z=3 * G2W, ab=4 * G2W, sq=4 * G2W + 2 * H2, skv=5 * G2W + 2 * H2)
LEVELS = 7

Q_FFN1 = 0
Q_A = Q_FFN1 + UNITS
Q_OA = Q_A + 6
Q_C = Q_OA + 4
Q_OC = Q_C + 6
Q_B = Q_OC + 4
Q_OB = Q_B + 6
Q_MO = Q_OB + 4
Q_FFN2 = Q_MO + 2
Q_LAYER = Q_FFN2 + UNITS
assert Q_LAYER % 2 == 0
Q_ADA = 0
Q_P2 = Q_ADA + 12
Q_W2 = Q_P2 + 7
Q_MOE = Q_W2 + 2
D_LAYER = 2 * UNITS

CONSTS = {}


def shape_constants():
    p = np.arange(P)[:, None]
    j = np.arange(P)[None, :]
    parts = [
        ("ident", p == j),
        ("ones", np.ones((P, P))),
        ("upto", p <= j),
        ("from_", p >= j),
        ("chunk_add", np.where(j // 64 <= p // 64, 0, NEG)),
        ("stick_add", np.concatenate([np.where(p < j, 0, NEG), 0 * (p + j), np.where(p < j, 0, NEG)], 1)),
        ("causal_add", np.where(j <= p, 0, NEG)),
        ("window_add", np.where(j > p, 0, NEG)),
    ]
    for b in [1 << n for n in range(LEVELS)]:
        parts.append((f"level{b}", ((j // b) % 2 == 1) & (p // b == j // b - 1)))
    half = ROT_A // 2
    inv = np.float32(500000.0) ** (-np.arange(half, dtype=np.float32) * np.float32(2.0) / np.float32(ROT_A))
    ang = np.arange(TOK, dtype=np.float32)[:, None] * inv[None, :].astype(np.float32)
    for name, f in (("cos_a", np.cos), ("sin_a", np.sin)):
        t = f(ang.astype(np.float32)).astype(np.float32).reshape(TT, P, half)
        parts.append((name, t.transpose(1, 0, 2).reshape(P, TT * half)))
    h2 = HD2 // 2
    inv2 = np.power(np.float32(10000.0), -np.arange(h2, dtype=np.float32) / np.float32(h2))
    parts.append(("inv_freq", np.broadcast_to(inv2.astype(np.float32), (P, h2))))
    li = [0.8 - 0.6 * np.exp(-0.3 * l) for l in range(LAYERS)]
    parts.append(("lam_init", np.broadcast_to(np.array(li, np.float32), (P, LAYERS))))
    parts.append(("one_minus_lam", np.broadcast_to(1.0 - np.array(li), (P, LAYERS))))
    parts.append(("minus_half", np.full((P, 64), -0.5)))
    at, cols = 0, []
    for name, a in parts:
        a = np.asarray(a, np.float32)
        CONSTS[name] = (at, a.shape[1])
        at += a.shape[1]
        cols.append(a)
    return np.ascontiguousarray(np.concatenate(cols, 1))


SHAPE_CONSTANTS = shape_constants()


def build(nc, A, out, stop=99):
    ctx = ExitStack()

    place = {}

    def sb(name, shape, dt=F32):
        place[name] = nc.sbuf_base
        return ctx.enter_context(nc.sbuf_tensor(name, shape, dt))

    def over(name, shape, other, col=0, dt=F32R):
        return nc.alloc_sbuf_tensor_at(name, shape, dt, offset=place[other] + 4 * col)

    def sem(name):
        return ctx.enter_context(nc.semaphore(name))

    consts = sb("consts", [P, SHAPE_CONSTANTS.shape[1]])
    wide = [sb(f"wide{s}", [P, KT, 512]) for s in range(2)]
    down = [sb(f"down{s}", [P, 2, D]) for s in range(2)]
    x = sb("x", [P, TT, D])
    xT = [sb(f"xT_{part}", [P, KT, TOK], F32R) for part in ("hi", "lo")]
    ln_par = sb("ln_par", [P, 2, D])
    sil = sb("sil", [P, TT, UF])
    hid = sb("hid", [P, TT, UF])
    hidT = [sb(f"hidT_{part}", [P, TT, 2, P], F32R) for part in ("hi", "lo")]
    c_parts = [sb(f"c_{part}", [P, KT], F32R) for part in ("hi", "lo")]
    small = sb("small", [P, 256])
    zrow = sb("zrow", [1, 512])
    merged = sb("merged", [P, TT, D])
    m1 = sb("m1", [P, 6144])
    work = sb("work", [P, 16384])
    vecs = sb("vecs", [P, 1536])
    ps = ctx.enter_context(nc.psum_tensor("ps", [P, 8, 512], F32))

    def const(name, rows=P):
        at, n = CONSTS[name]
        return consts[0:rows, at:at + n]

    ident = const("ident")

    def view(t, at, *dims):
        n = int(np.prod(dims))
        names = " ".join(f"d{i}" for i in range(len(dims)))
        return t[:, at:at + n].rearrange(f"p ({names}) -> p {names}", **{f"d{i}": d for i, d in enumerate(dims)})

    m2, m3, m4 = work[:, 0:6144], work[:, 6144:8192], work[:, 8192:11264]
    br = view(work, 11264, TT, D)
    scratch = work[:, 13312:15360]

    wide_hi, wide_lo = ([over(f"wide_{part}{s}", [P, KT, 512], "work", (2 * i + s) * KT * 512) for s in range(2)] for i, part in enumerate(("hi", "lo")))
    down_hi = [over(f"down_hi{s}", [P, 2, D], "m1", s * 2 * D) for s in range(2)]
    down_lo = [over("down_lo0", [P, 2, D], "m1", 4 * D), over("down_lo1", [P, 2, D], "merged")]
    brT = [over(f"brT_{part}", [P, KT, TOK], "m1", 2048 * (i + 1)) for i, part in enumerate(("hi", "lo"))]
    xT_work = over("xT_work", [P, KT * TOK], "xT_hi", dt=F32)

    def bc(ap, shape):
        return ap.to_broadcast(shape) if not isinstance(shape, int) else ap.to_broadcast([shape])

    wide_full = [sem(f"wide_full{s}") for s in range(2)]
    down_full = [sem(f"down_full{s}") for s in range(2)]
    wide_rounded, down_rounded = sem("wide_rounded"), sem("down_rounded")
    wide_split, down_split = sem("wide_split"), sem("down_split")
    blk = sem("block_done")
    dn = sem("down_done")
    BLK0, DN0, WS0, DS0 = 3, 2, 5, 2
    phase_left = sem("phase_left")

    pow_asked, pow_done = sem("pow_asked"), sem("pow_done")
    POW_LAYER = 5
    feat_turned = sem("to_features")
    feat_rounded = sem("feat_rounded")
    TURN_LAYER = 7

    def power(l, nth):
        return l * POW_LAYER + (nth + 1)

    def turn(l, nth, kp):
        return l * (4 * TURN_LAYER) + (4 * (nth + 1) + kp + 1)

    class Block:

        def __init__(self, l, i, c):
            self.number = l * Q_LAYER + i * 2 + c
            self.slot = c % 2
            self.landed = (l * (Q_LAYER // 2) + i + c // 2 + 1) * 32
            self.may_load = self.number * 4 + (WS0 - 4)
            self.may_split = self.number * 2 + (BLK0 - 2)
            self.tile, self.hi, self.lo = wide[self.slot], wide_hi[self.slot], wide_lo[self.slot]

        def rounded(self, q):
            return self.number * 4 + (q + 1)

        def split(self, q):
            return self.number * 4 + (WS0 + q + 1)

        def done(self, t):
            return self.number * 2 + (BLK0 + t + 1)

    class Down:
        def __init__(self, l, i, c):
            self.number = l * D_LAYER + i * 2 + c
            self.slot = c % 2
            self.landed = (l * (D_LAYER // 2) + i + c // 2 + 1) * 16
            self.may_load = self.number + (DS0 - 1)
            self.may_split = self.number + (DN0 - 1)
            self.rounded = self.number + 1
            self.split = self.number + (DS0 + 1)
            self.tile, self.hi, self.lo = down[self.slot], down_hi[self.slot], down_lo[self.slot]

    def steps(eng, n, first, body, last):
        first()
        with eng.Fori(0, (n - 1) // 2) as i:
            body(i, 1)
            body(i, 2)
        if (n - 1) % 2:
            body(0, n - 1)
        last()

    def pairs(eng, n, body):
        with eng.Fori(0, n // 2) as i:
            body(i, 0)
            body(i, 1)
        if n % 2:
            body(0, n - 1)

    carried = sem("waits_carried")

    def carry(eng):
        eng.sem_inc(carried, 1)

    def leave(eng, phase):
        eng.drain()
        eng.sem_inc(phase_left, 1)
        eng.wait_ge(phase_left, phase * 4 + 4)
        carry(eng)

    def load_halves(sp, b, lo, hi, dst):
        sp.wait_ge(wide_split, b.may_load)
        sp.dma_start(dst[0], lo).then_inc(wide_full[b.slot], 16)
        sp.dma_start(dst[1], hi).then_inc(wide_full[b.slot], 16)

    def load_columns(sp, b, w, col, n=512):
        v = w.rearrange("(k p) n -> p k n", p=P)[:, :, bass.ds(col, n)]
        load_halves(sp, b, v[:, 0:4, :], v[:, 4:8, :], (b.tile[:, 0:4, 0:n], b.tile[:, 4:8, 0:n]))

    def layer_of(ap, l):
        names = " ".join("abcd"[:len(ap.shape) - 1])
        return ap[bass.ds(l, 1)].rearrange(f"z {names} -> (z {names.split()[0]}) {' '.join(names.split()[1:])}")

    def round_block(act, b, n=512):
        act.wait_ge(wide_full[b.slot], b.landed)
        act.wait_ge(blk, b.may_split)
        for q in range(4):
            nc.scalar.copy(b.hi[:, 2 * q:2 * q + 2, 0:n], b.tile[:, 2 * q:2 * q + 2, 0:n]).then_inc(wide_rounded, 1)

    def rest_of_block(dve, b, n=512):
        for q in range(4):
            k = slice(2 * q, 2 * q + 2)
            dve.wait_ge(wide_rounded, b.rounded(q))
            nc.vector.tensor_tensor(b.lo[:, k, 0:n], b.tile[:, k, 0:n], b.hi[:, k, 0:n], ALU.subtract).then_inc(wide_split, 1)

    def three(pe, out, a, b, start, stop):
        pe.matmul(out, a[0], b[0], start=start, stop=False)
        pe.matmul(out, a[0], b[1], start=False, stop=False)
        return pe.matmul(out, a[1], b[0], start=False, stop=stop)

    def products(pe, bank, stat, t, b, n=512, start=True):
        for k in range(KT):
            if t == 0 and k % 2 == 0:
                pe.wait_ge(wide_split, b.split(k // 2))
            last = three(pe, bank[:, 0:n], [s[:, k, t * P:(t + 1) * P] for s in stat], [w[:, k, 0:n] for w in (b.hi, b.lo)],
                         start and k == 0, k == KT - 1)
        return last

    class ToFeatures:

        def __init__(self, src, dst, nth):
            self.src, self.dst, self.nth = src, dst, nth

        def pe(self, pe, l):
            for kp in range(4):
                for kk in range(2):
                    for t in range(TT):
                        k = 2 * kp + kk
                        at = kk * TOK + t * P
                        ins = pe.transpose(ps[:, kp, at:at + P], self.src[:, t, k * P:(k + 1) * P], ident)
                ins.then_inc(feat_turned, 1)

        def act(self, act, l):
            for kp in range(4):
                act.wait_ge(feat_turned, turn(l, self.nth, kp))
                nc.scalar.copy(self.dst[0][:, 2 * kp:2 * kp + 2, :], view_bank(kp, 2, TOK)).then_inc(feat_rounded, 1)

        def dve(self, dve, l):
            for kp in range(4):
                dve.wait_ge(feat_rounded, turn(l, self.nth, kp))
                k = slice(2 * kp, 2 * kp + 2)
                nc.vector.tensor_tensor(self.dst[1][:, k, :], view_bank(kp, 2, TOK), self.dst[0][:, k, :], ALU.subtract)

    def view_bank(b, *dims):
        names = " ".join(f"d{i}" for i in range(len(dims)))
        n = int(np.prod(dims))
        return ps[:, b, 0:n].rearrange(f"p ({names}) -> p {names}", **{f"d{i}": d for i, d in enumerate(dims)})

    sil_done = sem("sil_done")
    hid_done = sem("hid_done")
    hid_turned = sem("hid_turned")
    hidT_rounded = sem("hidT_rounded")
    hidT_done = sem("hidT_done")
    HALVES_LAYER = 4 * UNITS

    class Gated:

        def __init__(self, units, q, d, gate_up, down_rows, weight=None):
            self.units, self.q, self.d = units, q, d
            self.gate_up, self.down_rows, self.weight = gate_up, down_rows, weight

        def sp(self, sp, l):
            def unit(i, c):
                b, d = Block(l, i, self.q + c), Down(l, i, self.d + c)
                lo, hi = self.gate_up(l, i * 2 + c)
                load_halves(sp, b, lo, hi, (b.tile[:, :, 0:UF], b.tile[:, :, UF:2 * UF]))
                sp.wait_ge(down_split, d.may_load)
                sp.dma_start(d.tile[:], self.down_rows(l, i * 2 + c)).then_inc(down_full[d.slot], 16)
            pairs(sp, self.units, unit)

        def blocks(self, l, i, c):
            return Block(l, i, self.q + c), Down(l, i, self.d + c), l * HALVES_LAYER + i * 4 + (2 * self.d + c * 2)

        def pe(self, pe, l):
            for bank in range(4):
                pe.matmul(ps[:, bank, :], zrow[0:1, 0:P], zrow[0:1, :], start=True, stop=False, skip_group_check=True)

            def gate_up(i, c):
                b, d, n = self.blocks(l, i, c)
                for t in range(TT):
                    pe.wait_ge(hid_done, n + t + 1)
                    products(pe, ps[:, 4 + t, :], xT, t, b).then_inc(blk, 1)

            def turn_hidden(i, c):
                b, d, n = self.blocks(l, i, c)
                for t in range(TT):
                    pe.wait_ge(hid_done, n + t + 3)
                    pe.wait_ge(hidT_done, n + t + 1)
                    for k in range(2):
                        ins = pe.transpose(ps[:, 6 + t, k * P:(k + 1) * P], hid[:, t, k * P:(k + 1) * P], ident)
                    ins.then_inc(hid_turned, 1)

            def down_products(i, c):
                b, d, n = self.blocks(l, i, c)
                pe.wait_ge(down_split, d.split)
                for t in range(TT):
                    pe.wait_ge(hidT_done, n + t + 3)
                    for half in range(2):
                        cols = slice(half * 512, (half + 1) * 512)
                        for k in range(2):
                            a, w = [h[:, t, k, :] for h in hidT], [h[:, k, cols] for h in (d.hi, d.lo)]
                            for u, v in ((0, 0), (0, 1), (1, 0)):
                                ins = pe.matmul(ps[:, 2 * t + half, :], a[u], w[v], start=False, stop=False, skip_group_check=True)
                ins.then_inc(dn, 1)

            def first():
                gate_up(0, 0)
                turn_hidden(0, 0)

            def unit(i, c):
                gate_up(i, c)
                down_products(i, c - 1)
                turn_hidden(i, c)
            steps(pe, self.units, first, unit, lambda: down_products(0, self.units - 1))

        def act(self, act, l):
            def split(i, c):
                b, d, n = self.blocks(l, i, c)
                round_block(act, b)

            def rest(i, c):
                b, d, n = self.blocks(l, i, c)
                for t in range(TT):
                    act.wait_ge(blk, b.done(t))
                    nc.scalar.activation(sil[:, t, :], ps[:, 4 + t, 0:UF], ACT.Silu).then_inc(sil_done, 1)
                act.wait_ge(down_full[d.slot], d.landed)
                act.wait_ge(dn, d.may_split)
                nc.scalar.copy(d.hi[:], d.tile[:]).then_inc(down_rounded, 1)
                for t in range(TT):
                    act.wait_ge(hid_turned, n + t + 3)
                    nc.scalar.copy(hidT[0][:, t], ps[:, 6 + t, 0:UF].rearrange("p (k n) -> p k n", k=2)).then_inc(hidT_rounded, 1)

            def unit(i, c):
                split(i, c)
                rest(i, c - 1)
            steps(act, self.units, lambda: split(0, 0), unit, lambda: rest(0, self.units - 1))

        def dve(self, dve, l):
            def split(i, c):
                b, d, n = self.blocks(l, i, c)
                rest_of_block(dve, b)

            def rest(i, c):
                b, d, n = self.blocks(l, i, c)
                for t in range(TT):
                    dve.wait_ge(sil_done, n + t + 1)
                    dve.wait_ge(hid_turned, n + t + 1)
                    if self.weight is None:
                        nc.vector.tensor_tensor(hid[:, t, :], sil[:, t, :], ps[:, 4 + t, UF:2 * UF], ALU.mult).then_inc(hid_done, 1)
                    else:
                        nc.vector.scalar_tensor_tensor(out=hid[:, t, :], in0=sil[:, t, :], scalar=self.weight(t, i * 2 + c),
                                                       in1=ps[:, 4 + t, UF:2 * UF], op0=ALU.mult, op1=ALU.mult).then_inc(hid_done, 1)
                dve.wait_ge(down_rounded, d.rounded)
                nc.vector.tensor_tensor(d.lo[:], d.tile[:], d.hi[:], ALU.subtract).then_inc(down_split, 1)
                for t in range(TT):
                    dve.wait_ge(hidT_rounded, n + t + 1)
                    nc.vector.tensor_tensor(hidT[1][:, t], ps[:, 6 + t, 0:UF].rearrange("p (k n) -> p k n", k=2), hidT[0][:, t],
                                            ALU.subtract).then_inc(hidT_done, 1)

            def unit(i, c):
                split(i, c)
                rest(i, c - 1)
            steps(dve, self.units, lambda: split(0, 0), unit, lambda: rest(0, self.units - 1))

    norm_par = sem("norm_par")
    normed = sem("normed")

    class Norm:

        def __init__(self, nth, power, turn, r, g, b):
            self.nth, self.power, self.r, self.g, self.b = nth, power, r, g, b
            self.toT = ToFeatures(x, xT, turn)

        def load(self, pool, l):
            pool.dma_start(ln_par[:, 0, :], self.g[bass.ds(l, 1), :].partition_broadcast(P)).then_inc(norm_par, 16)
            pool.dma_start(ln_par[:, 1, :], self.b[bass.ds(l, 1), :].partition_broadcast(P)).then_inc(norm_par, 16)

        def dve(self, dve, l):
            st, mv = view(small, 0, TT, 2, 6), view(small, 24, TT, 2)
            for t in range(TT):
                nc.vector.tensor_scalar(x[:, t, :], x[:, t, :], ALPHA, None, ALU.mult)
            dve.drain()
            for t in range(TT):
                acc = ps[:, 2 * t:2 * t + 2, :].rearrange("p a b -> p (a b)")
                nc.vector.scalar_tensor_tensor(out=x[:, t, :], in0=acc, scalar=self.r, in1=x[:, t, :], op0=ALU.mult, op1=ALU.add)
            dve.drain()
            for t in range(TT):
                for h in range(2):
                    nc.vector.bn_stats(st[:, t, h, :], x[:, t, h * 512:(h + 1) * 512])
            dve.drain()
            for t in range(TT):
                nc.vector.bn_aggr(mv[:, t, :], st[:, t].rearrange("p a b -> p (a b)"))
            dve.drain()
            nc.vector.tensor_scalar(small[:, 30:32], mv[:, :, 1], LN_EPS, None, ALU.add).then_inc(pow_asked, 1)
            dve.wait_ge(pow_done, power(l, self.power))
            dve.wait_ge(norm_par, l * 96 + (self.nth + 1) * 32)
            for t in range(TT):
                nc.vector.tensor_scalar(x[:, t, :], x[:, t, :], mv[:, t, 0:1], small[:, 32 + t:33 + t], ALU.subtract, ALU.mult)
            dve.drain()
            nc.vector.tensor_tensor(x[:], x[:], bc(ln_par[:, 0:1, :], [P, TT, D]), ALU.mult)
            dve.drain()
            nc.vector.tensor_tensor(x[:], x[:], bc(ln_par[:, 1:2, :], [P, TT, D]), ALU.add).then_inc(normed, 1)
            self.toT.dve(dve, l)

        def pool(self, pool, l):
            pool.wait_ge(pow_asked, power(l, self.power))
            nc.gpsimd.tensor_tensor(small[:, 32:34], small[:, 30:32], const("minus_half")[:, 0:2], ALU.pow).then_inc(pow_done, 1)

        def pe(self, pe, l):
            pe.wait_ge(normed, l * 3 + (self.nth + 1))
            self.toT.pe(pe, l)

        def act(self, act, l):
            self.toT.act(act, l)

    copied = [sem(f"projection_copied{part}") for part in range(2)]
    COPIED_LAYER = 6 + 6 + 6

    class Project:

        def __init__(self, q, before, blocks):
            self.q, self.before, self.blocks = q, before, blocks

        def sp(self, sp, l):
            for c, (kind, w, col, n, dst) in enumerate(self.blocks):
                load_columns(sp, Block(l, 0, self.q + c), w(l), col, n)

        def pe(self, pe, l):
            for c, (kind, w, col, n, dst) in enumerate(self.blocks):
                b = Block(l, 0, self.q + c)
                for part in range(2):
                    pe.wait_ge(copied[part], l * COPIED_LAYER + (self.before + c + 1))
                    bank = ps[:, 2 * (c % 2) + part, :]
                    if kind == "tok":
                        last = products(pe, bank, xT, part, b, n)
                    else:
                        for f in range(2):
                            at = (2 * part + f) * P
                            for k in range(KT):
                                if part == 0 and f == 0 and k % 2 == 0:
                                    pe.wait_ge(wide_split, b.split(k // 2))
                                last = three(pe, bank[:, f * TOK:(f + 1) * TOK], [h[:, k, at:at + P] for h in (b.hi, b.lo)],
                                             [s[:, k, :] for s in xT], k == 0, k == KT - 1)
                    last.then_inc(blk, 1)

        def copy(self, eng, op, l, part, c):
            kind, w, col, n, dst = self.blocks[c]
            eng.wait_ge(blk, Block(l, 0, self.q + c).done(part))
            bank = 2 * (c % 2) + part
            src = ps[:, bank:bank + 1, 0:n] if kind == "tok" else view_bank(bank, 2, TOK)
            op(dst(part), src).then_inc(copied[part], 1)

        def act(self, act, l):
            for c, (kind, w, col, n, dst) in enumerate(self.blocks):
                round_block(act, Block(l, 0, self.q + c), n)
                if c:
                    self.copy(act, nc.scalar.copy, l, 0, c - 1)
            self.copy(act, nc.scalar.copy, l, 0, len(self.blocks) - 1)

        def dve(self, dve, l):
            for c, (kind, w, col, n, dst) in enumerate(self.blocks):
                rest_of_block(dve, Block(l, 0, self.q + c), n)
                if c:
                    self.copy(dve, nc.vector.tensor_copy, l, 1, c - 1)
            self.copy(dve, nc.vector.tensor_copy, l, 1, len(self.blocks) - 1)

    w_mix = lambda l: layer_of(A["w_mix_in"], l)

    qkv_a = view(m1, 0, 3, TT, D)
    proj_a = Project(Q_A, 0, [("tok", w_mix, C_QA + c * 512, 512, lambda part, c=c: qkv_a[:, c // 2, part:part + 1, (c % 2) * 512:(c % 2 + 1) * 512])
                              for c in range(6)])

    class DiffAttention:
        par = sem("a_par")
        lam_sum, lam_exp = sem("a_lam_sum"), sem("a_lam_exp")
        roped = sem("a_roped")
        staged, turned, qT_done, kT_done = sem("a_staged"), sem("a_turned"), sem("a_qT"), sem("a_kT")
        scored, masked, exped, mixed = sem("a_scored"), sem("a_masked"), sem("a_exped"), sem("a_mixed")
        w_turned, wT_done, out_done = sem("a_w_turned"), sem("a_wT"), sem("a_out")
        ready = sem("a_ready")
        stage = view(m4, 0, 3, TT, P)
        qT, kT = view(m4, 768, 2, TOK)[0:HDA], view(m4, 1280, 2, TOK)[0:HDA]
        sm = m2[:, 0:768]
        w = m2[:, 768:1152]
        wT = view(m2, 1152, 3, P)
        st = m2[:, 1536:1600]
        subln = vecs[:, 0:2 * HDA]
        lam4 = view(vecs, 128, 4, HDA)
        toT = ToFeatures(br, brT, 1)

        def load(self, pool, l):
            pool.dma_start(self.subln, A["diff_subln_g"][bass.ds(l, 1), :].partition_broadcast(P)).then_inc(self.par, 16)
            pool.dma_start(vecs[:, 128:384], A["diff_lambda"].rearrange("l a d -> l (a d)")[bass.ds(l, 1), :].partition_broadcast(P)).then_inc(self.par, 16)

        def pool(self, pool, l):
            pool.wait_ge(self.roped, l + 1)
            carry(pool)
            with pool.Fori(0, HA) as h:
                n = l * HA + h
                pool.wait_ge(self.out_done, n + 1)
                for j in range(3):
                    ins = nc.gpsimd.tensor_copy(self.stage[:, j], qkv_a[:, j, :, bass.ds(h * P, P)])
                ins.then_inc(self.staged, 1)
            pool.wait_ge(pow_asked, power(l, 1))
            nc.gpsimd.tensor_tensor(self.st[:, 32:48], self.st[:, 16:32], const("minus_half")[:, 0:16], ALU.pow).then_inc(pow_done, 1)

        def pe(self, pe, l):
            with pe.Fori(0, HA) as h:
                n = l * HA + h
                pe.wait_ge(self.staged, n + 1)
                carry(pe)
                for j in range(2):
                    for m in range(2):
                        for t in range(TT):
                            ins = pe.transpose(ps[0:HDA, j, m * TOK + t * P:m * TOK + (t + 1) * P],
                                               self.stage[:, j, t, m * HDA:(m + 1) * HDA], ident)
                    ins.then_inc(self.turned, 1)
                pe.wait_ge(self.qT_done, n + 1)
                pe.wait_ge(self.kT_done, n + 1)
                for t in range(TT):
                    keys = (t + 1) * P
                    for m in range(2):
                        ins = pe.matmul(ps[:, 2 + t, m * keys:(m + 1) * keys], self.qT[:, m, t * P:(t + 1) * P],
                                        self.kT[:, m, 0:keys], start=True, stop=True)
                ins.then_inc(self.scored, 1)
                pe.wait_ge(self.mixed, n + 1)
                for b in range(3):
                    ins = pe.transpose(ps[:, 4, b * P:(b + 1) * P], self.w[:, b * P:(b + 1) * P], ident)
                ins.then_inc(self.w_turned, 1)
                pe.wait_ge(self.wT_done, n + 1)
                pe.matmul(ps[:, 5, 0:P], self.wT[:, 0, :], self.stage[:, 2, 0, :], start=True, stop=True)
                pe.matmul(ps[:, 5, P:2 * P], self.wT[:, 1, :], self.stage[:, 2, 0, :], start=True, stop=False)
                pe.matmul(ps[:, 5, P:2 * P], self.wT[:, 2, :], self.stage[:, 2, 1, :], start=False, stop=True).then_inc(self.out_done, 1)
            pe.wait_ge(self.ready, l + 1)
            self.toT.pe(pe, l)

        def act(self, act, l):
            act.wait_ge(self.lam_sum, l + 1)
            nc.scalar.activation(self.st[:, 52:54], self.st[:, 50:52], ACT.Exp).then_inc(self.lam_exp, 1)
            with act.Fori(0, HA) as h:
                n = l * HA + h
                act.wait_ge(self.turned, n * 2 + 1)
                nc.scalar.mul(self.qT, ps[0:HDA, 0, :].rearrange("p (m n) -> p m n", m=2), HDA ** -0.5).then_inc(self.qT_done, 1)
                act.wait_ge(self.masked, n + 1)
                at = 0
                for t in range(TT):
                    keys = (t + 1) * P
                    for m in range(2):
                        c = 2 * t + m
                        ins = nc.scalar.activation(self.sm[:, at:at + keys], self.sm[:, at:at + keys], ACT.Exp,
                                                   bias=self.st[:, c:c + 1], accum_out=self.st[:, 4 + c:5 + c])
                        at += keys
                ins.then_inc(self.exped, 1)
                act.wait_ge(self.w_turned, n + 1)
                nc.scalar.copy(self.wT, view_bank(4, 3, P)).then_inc(self.wT_done, 1)
            self.toT.act(act, l)

        def dve(self, dve, l):
            V, st = nc.vector, self.st
            dve.wait_ge(self.par, l * 32 + 32)
            pr = view(m3, 0, 2, HDA)
            V.tensor_tensor(pr, self.lam4[:, 0:4:2, :], self.lam4[:, 1:4:2, :], ALU.mult)
            dve.drain()
            V.tensor_reduce(st[:, 50:52], pr, AX.X, ALU.add).then_inc(self.lam_sum, 1)
            V.tensor_copy(st[:, 56:57], const("lam_init")[:, bass.ds(l, 1)])
            V.tensor_copy(st[:, 57:58], const("one_minus_lam")[:, bass.ds(l, 1)])
            dve.drain()
            V.tensor_scalar(self.subln, self.subln, st[:, 57:58], None, ALU.mult)
            dve.wait_ge(self.lam_exp, l + 1)
            V.tensor_tensor(st[:, 54:55], st[:, 53:54], st[:, 52:53], ALU.subtract)
            dve.drain()
            V.tensor_tensor(st[:, 55:56], st[:, 54:55], st[:, 56:57], ALU.subtract)
            half = ROT_A // 2
            for t in range(TT):
                maps = qkv_a[:, 0:2, t, :].rearrange("p j (m d) -> p j m d", d=HDA)
                a, b = maps[:, :, :, 0:half], maps[:, :, :, half:ROT_A]
                cos, sin = (bc(const(c)[:, t * half:(t + 1) * half].unsqueeze(1).unsqueeze(1), [P, 2, 16, half]) for c in ("cos_a", "sin_a"))
                ac, bs, bcs, as_ = (view(m3, 256 + 256 * (4 * t + i), 2, 16, half) if 4 * t + i < 7 else view(m2, 4096, 2, 16, half) for i in range(4))
                V.tensor_tensor(ac, a, cos, ALU.mult)
                V.tensor_tensor(bs, b, sin, ALU.mult)
                V.tensor_tensor(bcs, b, cos, ALU.mult)
                V.tensor_tensor(as_, a, sin, ALU.mult)
                dve.drain()
                V.tensor_tensor(a, ac, bs, ALU.subtract)
                V.tensor_tensor(b, bcs, as_, ALU.add)
            dve.drain()
            dve.sem_inc(self.roped, 1)
            mask = const("chunk_add")
            s0 = self.sm[:, 0:256].rearrange("p (m k) -> p m k", m=2)
            s1 = self.sm[:, 256:768].rearrange("p (m k) -> p m k", m=2)
            with dve.Fori(0, HA) as h:
                n = l * HA + h
                dve.wait_ge(self.turned, n * 2 + 2)
                V.tensor_copy(self.kT, ps[0:HDA, 1, :].rearrange("p (m n) -> p m n", m=2)).then_inc(self.kT_done, 1)
                dve.wait_ge(self.scored, n + 1)
                V.tensor_tensor(s0, view_bank(2, 2, P), bc(mask.unsqueeze(1), [P, 2, P]), ALU.add)
                V.tensor_copy(s1[:, :, 0:P], view_bank(3, 2, TOK)[:, :, 0:P])
                V.tensor_tensor(s1[:, :, P:TOK], view_bank(3, 2, TOK)[:, :, P:TOK], bc(mask.unsqueeze(1), [P, 2, P]), ALU.add)
                dve.drain()
                V.tensor_reduce(st[:, 0:2], s0, AX.X, ALU.max, negate=True)
                V.tensor_reduce(st[:, 2:4], s1, AX.X, ALU.max, negate=True).then_inc(self.masked, 1)
                dve.wait_ge(self.exped, n + 1)
                V.reciprocal(st[:, 8:12], st[:, 4:8])
                dve.drain()
                V.tensor_scalar(st[:, 12:16], st[:, 8:12], st[:, 55:56], None, ALU.mult)
                V.tensor_scalar(self.w[:, 0:P], s0[:, 0, :], st[:, 8:9], None, ALU.mult)
                V.tensor_scalar(self.w[:, P:3 * P], s1[:, 0, :], st[:, 10:11], None, ALU.mult)
                dve.drain()
                V.scalar_tensor_tensor(out=self.w[:, 0:P], in0=s0[:, 1, :], scalar=st[:, 13:14], in1=self.w[:, 0:P], op0=ALU.mult, op1=ALU.add)
                V.scalar_tensor_tensor(out=self.w[:, P:3 * P], in0=s1[:, 1, :], scalar=st[:, 15:16], in1=self.w[:, P:3 * P],
                                       op0=ALU.mult, op1=ALU.add).then_inc(self.mixed, 1)
                dve.wait_ge(self.out_done, n + 2)
                V.tensor_copy(br[:, :, bass.ds(h * P, P)], view_bank(5, TT, P))
            dve.drain()
            heads = br[:].rearrange("p t (h e) -> p (t h) e", e=P)
            sq = view(m3, 0, TT * HA, P)
            V.tensor_tensor(sq, heads, heads, ALU.mult)
            dve.drain()
            V.tensor_reduce(st[:, 0:16], sq, AX.X, ALU.add)
            dve.drain()
            V.tensor_scalar(st[:, 16:32], st[:, 0:16], 1.0 / P, LN_EPS, ALU.mult, ALU.add).then_inc(pow_asked, 1)
            dve.wait_ge(pow_done, power(l, 1))
            V.tensor_tensor(heads, heads, bc(st[:, 32:48].unsqueeze(2), [P, TT * HA, P]), ALU.mult)
            dve.drain()
            V.tensor_tensor(heads, heads, bc(self.subln.unsqueeze(1), [P, TT * HA, P]), ALU.mult).then_inc(self.ready, 1)
            self.toT.dve(dve, l)

    gate_done, half_added = sem("branch_gate"), sem("branch_added")
    gate_par = sem("gate_par")
    gate_row = m1[0:1, 1024:2048]

    class Merge:

        def __init__(self, nth, q, r):
            self.nth, self.q, self.r = nth, q, r
            self.gates = view(m1, 0, TT, 512)

        def blocks(self, l):
            return [Block(l, 0, self.q + j) for j in range(4)]

        def sp(self, sp, l):
            w = A["w_branch"][bass.ds(l, 1), self.r].rearrange("z k n -> (z k) n")
            for j, b in enumerate(self.blocks(l)):
                if j % 2 == 0:
                    load_columns(sp, b, w, (j // 2) * 512)
                else:
                    load_columns(sp, b, w_mix(l), C_G + self.r * D + (j // 2) * 512)

        def load(self, pool, l):
            row = A["gate_bias"][bass.ds(l, 1), self.r, :]
            pool.dma_start(gate_row, row).then_inc(gate_par, 16)

        def pe(self, pe, l):
            for j, b in enumerate(self.blocks(l)):
                for t in range(TT):
                    bank = ps[:, 2 * j + t, :]
                    if j % 2 == 0:
                        products(pe, bank, brT, t, b).then_inc(blk, 1)
                    else:
                        if j == 1 and t == 0:
                            pe.wait_ge(gate_par, l * 48 + (self.nth + 1) * 16)
                            carry(pe)
                        pe.matmul(bank, const("ones", 1), gate_row[:, (j // 2) * 512:(j // 2 + 1) * 512], start=True, stop=False)
                        products(pe, bank, xT, t, b, start=False).then_inc(blk, 1)

        def act(self, act, l):
            blocks = self.blocks(l)
            for b in blocks:
                round_block(act, b)
            for c in range(2):
                if c == 1:
                    act.wait_ge(half_added, l * 6 + (self.nth * 2 + 1))
                for t in range(TT):
                    act.wait_ge(blk, blocks[2 * c + 1].done(t))
                    nc.scalar.activation(self.gates[:, t, :], ps[:, 4 * c + 2 + t, :], ACT.Sigmoid).then_inc(gate_done, 1)

        def dve(self, dve, l):
            blocks = self.blocks(l)
            for b in blocks:
                rest_of_block(dve, b)
            for c in range(2):
                cols = slice(c * 512, (c + 1) * 512)
                for t in range(TT):
                    dve.wait_ge(blk, blocks[2 * c].done(t))
                    dve.wait_ge(gate_done, l * 12 + (self.nth * 4 + 2 * c + t + 1))
                    dst = merged[:, t, cols] if self.nth == 0 else self.gates[:, t, :]
                    ins = nc.vector.tensor_tensor(dst, self.gates[:, t, :], ps[:, 4 * c + t, :], ALU.mult)
                if self.nth:
                    dve.drain()
                    ins = nc.vector.tensor_tensor(merged[:, :, cols], merged[:, :, cols], self.gates, ALU.add)
                ins.then_inc(half_added, 1)

    qk_c = view(m1, 0, 16, TOK)
    v_c = view(m1, 4096, TT, D)
    proj_c = Project(Q_C, 6, [("feat", w_mix, C_QC + c * 512, 512, lambda part, c=c: qk_c[:, c * 4 + part * 2:c * 4 + part * 2 + 2, :])
                              for c in range(4)]
                     + [("tok", w_mix, C_VC + c * 512, 512, lambda part, c=c: v_c[:, part:part + 1, c * 512:(c + 1) * 512]) for c in range(2)])

    class StickBreaking:
        staged, scored, absed, logged = sem("c_staged"), sem("c_scored"), sem("c_abs"), sem("c_log")
        stay, summed, shifted, weighed = sem("c_stay"), sem("c_summed"), sem("c_shifted"), sem("c_weighed")
        out_done, ready = sem("c_out"), sem("c_ready")
        qk = view(m4, 0, 2, TOK)
        v = view(m4, 512, TT, P)
        z = view(m2, 0, 2, 384)
        ab = view(m2, 768, 2, 384)
        lg = view(m2, 1536, 2, 384)
        sp_ = view(m2, 2304, 2, 384)
        a = view(m2, 3072, 2, 384)
        toT = ToFeatures(br, brT, 2)

        def pool(self, pool, l):
            with pool.Fori(0, HC // 2) as h:
                n = l * (HC // 2) + h
                pool.wait_ge(self.out_done, n + 1)
                nc.gpsimd.tensor_copy(self.qk[:, 0:1, :], qk_c[:, bass.ds(h, 1), :])
                nc.gpsimd.tensor_copy(self.qk[:, 1:2, :], qk_c[:, bass.ds(h + 8, 1), :])
                nc.gpsimd.tensor_copy(self.v, v_c[:, :, bass.ds(h * P, P)]).then_inc(self.staged, 1)

        def pe(self, pe, l):
            with pe.Fori(0, HC // 2) as h:
                n = l * (HC // 2) + h
                pe.wait_ge(self.staged, n + 1)
                for e in range(2):
                    rows = slice(e * HDC, (e + 1) * HDC)
                    pe.matmul(ps[:, e, 0:TOK], self.qk[rows, 1, 0:P], self.qk[rows, 0, :], start=True, stop=True)
                    ins = pe.matmul(ps[:, e, TOK:384], self.qk[rows, 1, P:TOK], self.qk[rows, 0, P:TOK], start=True, stop=True)
                ins.then_inc(self.scored, 1)
                pe.wait_ge(self.stay, n + 1)
                for e in range(2):
                    pe.matmul(ps[:, 2 + e, 0:384], const("from_"), self.sp_[:, e, :], start=True, stop=False)
                    ins = pe.matmul(ps[:, 2 + e, P:TOK], const("ones"), self.sp_[:, e, TOK:384], start=False, stop=True)
                ins.then_inc(self.summed, 1)
                pe.wait_ge(self.weighed, n + 1)
                for e in range(2):
                    cols = slice(e * HDC, (e + 1) * HDC)
                    pe.matmul(ps[:, 4, e * HDC:(e + 1) * HDC], self.a[:, e, 0:P], self.v[:, 0, cols], start=True, stop=True)
                    pe.matmul(ps[:, 4, P + e * HDC:P + (e + 1) * HDC], self.a[:, e, P:TOK], self.v[:, 0, cols], start=True, stop=False)
                    ins = pe.matmul(ps[:, 4, P + e * HDC:P + (e + 1) * HDC], self.a[:, e, TOK:384], self.v[:, 1, cols], start=False, stop=True)
                ins.then_inc(self.out_done, 1)
            pe.wait_ge(self.ready, l + 1)
            self.toT.pe(pe, l)

        def act(self, act, l):
            with act.Fori(0, HC // 2) as h:
                n = l * (HC // 2) + h
                act.wait_ge(self.absed, n + 1)
                nc.scalar.activation(self.lg, self.ab, ACT.Exp, scale=-1.0)
                act.drain()
                nc.scalar.activation(self.lg, self.lg, ACT.Ln, bias=1.0).then_inc(self.logged, 1)
                act.wait_ge(self.shifted, n + 1)
                nc.scalar.activation(self.a, self.a, ACT.Exp).then_inc(self.weighed, 1)
                act.wait_ge(self.out_done, n + 2)
                nc.scalar.copy(br[:, :, bass.ds(h * P, P)], view_bank(4, TT, P))
            act.drain()
            act.sem_inc(self.ready, 1)
            self.toT.act(act, l)

        def dve(self, dve, l):
            V = nc.vector
            with dve.Fori(0, HC // 2) as h:
                n = l * (HC // 2) + h
                dve.wait_ge(self.scored, n + 1)
                V.scalar_tensor_tensor(out=self.z, in0=ps[:, 0:2, 0:384], scalar=HDC ** -0.5,
                                       in1=bc(const("stick_add").unsqueeze(1), [P, 2, 384]), op0=ALU.mult, op1=ALU.add)
                dve.drain()
                V.scalar_tensor_tensor(out=self.ab, in0=self.z, scalar=-1.0, in1=self.z, op0=ALU.mult, op1=ALU.max).then_inc(self.absed, 1)
                dve.wait_ge(self.logged, n + 1)
                V.scalar_tensor_tensor(out=self.sp_, in0=self.z, scalar=0.0, in1=self.lg, op0=ALU.max, op1=ALU.add).then_inc(self.stay, 1)
                dve.wait_ge(self.summed, n + 1)
                V.tensor_tensor(self.a, self.z, ps[:, 2:4, 0:384], ALU.subtract).then_inc(self.shifted, 1)
            self.toT.dve(dve, l)

    z_b = view(m1, 0, TT, D)
    xbc = view(m1, 2048, CT, TOK + CONV - 1)
    dt_raw = view(m1, 2048 + CT * (TOK + CONV - 1), TT, HB)
    proj_b = Project(Q_B, 12, [("tok", w_mix, C_Z + c * 512, 512, lambda part, c=c: z_b[:, part:part + 1, c * 512:(c + 1) * 512]) for c in range(2)]
                     + [("feat", w_mix, C_XBC + c * 512, 512, lambda part, c=c: xbc[:, c * 4 + part * 2:c * 4 + part * 2 + 2, CONV - 1:]) for c in range(3)]
                     + [("tok", w_mix, C_DT, HB, lambda part: dt_raw[:, part:part + 1, :])])

    def convolve(dve, dst, src, weight, bias=None):
        for j in range(CONV):
            with dve.Fori(0, CT // 4) as i:
                for c4 in range(4):
                    c = i * 4 + c4
                    s, o = src[:, bass.ds(c, 1), j:j + TOK], dst[:, bass.ds(c, 1), :]
                    if j:
                        nc.vector.scalar_tensor_tensor(out=o, in0=s, scalar=weight(j, c), in1=o, op0=ALU.mult, op1=ALU.add)
                    elif bias is not None:
                        nc.vector.tensor_scalar(o, s, weight(j, c), bias(c), ALU.mult, ALU.add)
                    else:
                        nc.vector.tensor_scalar(o, s, weight(j, c), None, ALU.mult)
            dve.drain()

    class Scan:
        par, pad, cw_turned, cw_done = sem("b_par"), sem("b_pad"), sem("b_cw_turned"), sem("b_cw")
        convolved, silu_done = sem("b_conv"), sem("b_silu")
        dt_abs, dt_log, decay_done = sem("b_dt_abs"), sem("b_dt_log"), sem("b_decay")
        cum, turned, xs_done, cb = sem("b_cum"), sem("b_turned"), sem("b_xs"), sem("b_cb")
        table_done, staged, spread, seg = sem("b_table"), sem("b_staged"), sem("b_spread"), sem("b_seg")
        exped, weighed, out_done, copied = sem("b_exped"), sem("b_weighed"), sem("b_out"), sem("b_copied")
        ready = sem("b_ready")
        QUADS = HB // 4
        norm_g = vecs[:, 0:D]
        dt_bias, a_log, d_skip = (vecs[:, D + HB * i:D + HB * (i + 1)] for i in range(3))
        cw = vecs[:, 1100:1100 + CT * (CONV + 1)]
        raw = m1[0:CT * (CONV + 1), 5800:5800 + P]
        conv = view(m2, 0, CT, TOK)
        xs = view(m2, 3072, TT, D)
        cbm = view(m2, 5120, GB, 3 * P)
        xdt = view(m3, 0, TT, D)
        dtv = view(small, 0, TT, HB)
        tab = view(small, 64, 5, HB)
        st = small[:, 144:208]
        s_tab = view(vecs, 1200, 5, 4)
        e = view(m4, 0, 3, 4, P)
        w = view(m4, 1536, 3, 4, P)
        s_x = view(scratch, 0, TT, 4 * PB)
        s_cb = view(scratch, 512, 3, P)
        toT = ToFeatures(br, brT, 3)

        def load(self, pool, l):
            pool.dma_start(self.norm_g, A["ssm_norm_g"][bass.ds(l, 1), :].partition_broadcast(P)).then_inc(self.par, 16)
            for dst, name in ((self.dt_bias, "ssm_dt_bias"), (self.a_log, "ssm_A_log"), (self.d_skip, "ssm_D")):
                pool.dma_start(dst, A[name][bass.ds(l, 1), :].partition_broadcast(P)).then_inc(self.par, 16)
            taps = CT * CONV
            pool.dma_start(self.raw[0:taps], layer_of(A["ssm_conv_w"], l).rearrange("j (c p) -> (j c) p", p=P)).then_inc(self.par, 16)
            pool.dma_start(self.raw[taps:taps + CT], A["ssm_conv_b"][bass.ds(l, 1), :].rearrange("z (c p) -> (z c) p", p=P)).then_inc(self.par, 16)
            nc.gpsimd.memset(xbc[:, :, 0:CONV - 1], 0.0)

        def pool(self, pool, l):
            pool.wait_ge(self.table_done, l + 1)
            carry(pool)
            with pool.Fori(0, self.QUADS) as i:
                n = l * self.QUADS + i
                pool.wait_ge(self.out_done, n + 1)
                nc.gpsimd.tensor_copy(self.s_tab, self.tab[:, :, bass.ds(i * 4, 4)])
                nc.gpsimd.tensor_copy(self.s_x, self.xdt[:, :, bass.ds(i * 256, 256)])
                nc.gpsimd.tensor_copy(self.s_cb[:, :, :].rearrange("p b n -> p (b n)").unsqueeze(1), self.cbm[:, bass.ds(i // 2, 1), :]).then_inc(self.staged, 1)
            pool.wait_ge(pow_asked, power(l, 2))
            nc.gpsimd.tensor_tensor(self.st[:, 8:12], self.st[:, 4:8], const("minus_half")[:, 0:4], ALU.pow).then_inc(pow_done, 1)

        def pe(self, pe, l):
            n_par = CT * (CONV + 1)
            pe.wait_ge(self.par, l * 96 + 96)
            carry(pe)
            pe.transpose(ps[:, 7, 0:n_par], self.raw, ident[0:n_par, 0:n_par]).then_inc(self.cw_turned, 1)
            pe.wait_ge(self.decay_done, l + 1)
            d = self.tab[:, 0:2, :].rearrange("p t h -> p (t h)")
            pe.matmul(ps[:, 6, 0:2 * HB], const("upto"), d, start=True, stop=True)
            pe.matmul(ps[:, 6, 2 * HB:3 * HB], const("ones"), self.tab[:, 0, :], start=True, stop=True).then_inc(self.cum, 1)
            pe.wait_ge(self.silu_done, l + 1)
            for t in range(TT):
                for c in range(8):
                    ins = pe.transpose(ps[:, 2 * t + c // 4, (c % 4) * P:(c % 4 + 1) * P], self.conv[:, c, t * P:(t + 1) * P], ident)
                ins.then_inc(self.turned, 1)
            for g in range(GB):
                b_, c_ = self.conv[:, 8 + g, :], self.conv[:, 10 + g, :]
                pe.matmul(ps[:, 4 + g, 0:TOK], b_[:, 0:P], c_, start=True, stop=True)
                ins = pe.matmul(ps[:, 4 + g, TOK:384], b_[:, P:TOK], c_[:, P:TOK], start=True, stop=True)
            ins.then_inc(self.cb, 1)
            pe.wait_ge(self.table_done, l + 1)
            carry(pe)
            with pe.Fori(0, self.QUADS) as i:
                n = l * self.QUADS + i
                pe.wait_ge(self.staged, n + 1)
                for t in range(TT):
                    for h in range(4):
                        ins = pe.matmul(ps[:, t, h * P:(h + 1) * P], self.s_tab[:, t, h:h + 1].to_broadcast([P, P]), const("upto"), start=True, stop=True)
                ins.then_inc(self.spread, 1)
                pe.wait_ge(self.weighed, n + 1)
                for h in range(4):
                    cols = slice(h * PB, (h + 1) * PB)
                    pe.matmul(ps[:, 2, h * PB:(h + 1) * PB], self.w[:, 0, h, :], self.s_x[:, 0, cols], start=True, stop=True)
                    o1 = ps[:, 2, 256 + h * PB:256 + (h + 1) * PB]
                    pe.matmul(o1, self.w[:, 1, h, :], self.s_x[:, 0, cols], start=True, stop=False)
                    ins = pe.matmul(o1, self.w[:, 2, h, :], self.s_x[:, 1, cols], start=False, stop=True)
                ins.then_inc(self.out_done, 1)
            pe.wait_ge(self.ready, l + 1)
            self.toT.pe(pe, l)

        def act(self, act, l):
            act.wait_ge(self.cw_turned, l + 1)
            nc.scalar.copy(self.cw, ps[:, 7, 0:CT * (CONV + 1)]).then_inc(self.cw_done, 1)
            act.wait_ge(self.dt_abs, l + 1)
            nc.scalar.activation(self.st[:, 0:32], self.st[:, 0:32], ACT.Exp, scale=-1.0)
            nc.scalar.activation(self.a_log, self.a_log, ACT.Exp)
            act.drain()
            nc.scalar.activation(self.st[:, 0:32], self.st[:, 0:32], ACT.Ln, bias=1.0).then_inc(self.dt_log, 1)
            nc.scalar.activation(z_b, z_b, ACT.Silu)
            act.wait_ge(self.convolved, l + 1)
            nc.scalar.activation(self.conv, self.conv, ACT.Silu)
            act.drain()
            act.sem_inc(self.silu_done, 1)
            act.wait_ge(self.turned, l * 2 + 1)
            nc.scalar.copy(self.xs[:, 0, :], ps[:, 0:2, :].rearrange("p a b -> p (a b)"))
            act.wait_ge(self.turned, l * 2 + 2)
            nc.scalar.copy(self.xs[:, 1, :], ps[:, 2:4, :].rearrange("p a b -> p (a b)")).then_inc(self.xs_done, 1)
            with act.Fori(0, self.QUADS) as i:
                n = l * self.QUADS + i
                act.wait_ge(self.seg, n + 1)
                nc.scalar.activation(self.e, self.e, ACT.Exp).then_inc(self.exped, 1)
                act.wait_ge(self.out_done, n + 2)
                nc.scalar.copy(br[:, :, bass.ds(i * 256, 256)], view_bank(2, TT, 256))
            act.drain()
            act.sem_inc(self.copied, 1)
            self.toT.act(act, l)

        def dve(self, dve, l):
            V = nc.vector
            dve.wait_ge(self.par, l * 96 + 96)
            V.tensor_tensor(self.dtv, dt_raw, bc(self.dt_bias.unsqueeze(1), [P, TT, HB]), ALU.add)
            dve.drain()
            sp_ = view(self.st, 0, TT, HB)
            V.scalar_tensor_tensor(out=sp_, in0=self.dtv, scalar=-1.0, in1=self.dtv, op0=ALU.mult, op1=ALU.max).then_inc(self.dt_abs, 1)
            dve.wait_ge(self.cw_done, l + 1)
            carry(dve)
            convolve(dve, self.conv, xbc, lambda j, c: self.cw[:, bass.ds(c + j * CT, 1)], lambda c: self.cw[:, bass.ds(c + CONV * CT, 1)])
            dve.sem_inc(self.convolved, 1)
            dve.wait_ge(self.dt_log, l + 1)
            V.scalar_tensor_tensor(out=self.dtv, in0=self.dtv, scalar=0.0, in1=sp_, op0=ALU.max, op1=ALU.add)
            dve.drain()
            V.scalar_tensor_tensor(out=self.tab[:, 0:2, :], in0=self.dtv, scalar=-1.0, in1=bc(self.a_log.unsqueeze(1), [P, TT, HB]),
                                   op0=ALU.mult, op1=ALU.mult).then_inc(self.decay_done, 1)
            dve.wait_ge(self.cum, l + 1)
            V.tensor_copy(self.tab[:, 2:4, :], view_bank(6, 3, HB)[:, 0:2, :])
            dve.drain()
            V.tensor_tensor(self.tab[:, 4, :], self.tab[:, 2, :], view_bank(6, 3, HB)[:, 2, :], ALU.subtract)
            dve.wait_ge(self.xs_done, l + 1)
            for t in range(TT):
                V.tensor_tensor(self.xdt[:, t, :].rearrange("p (h d) -> p h d", d=PB), self.xs[:, t, :].rearrange("p (h d) -> p h d", d=PB),
                                bc(self.dtv[:, t, :].unsqueeze(2), [P, HB, PB]), ALU.mult)
            dve.wait_ge(self.cb, l + 1)
            for g in range(GB):
                c3 = view_bank(4 + g, 3, P)
                o3 = self.cbm[:, g, :].rearrange("p (b n) -> p b n", b=3)
                V.tensor_tensor(o3[:, 0:3:2, :], c3[:, 0:3:2, :], bc(const("upto").unsqueeze(1), [P, 2, P]), ALU.mult)
                V.tensor_copy(o3[:, 1, :], c3[:, 1, :])
            dve.drain()
            dve.sem_inc(self.table_done, 1)
            with dve.Fori(0, self.QUADS) as i:
                n = l * self.QUADS + i
                dve.wait_ge(self.spread, n + 1)
                for h in range(4):
                    cols = slice(h * P, (h + 1) * P)
                    for b, (bank, f) in enumerate(((0, 2), (1, 4), (1, 3))):
                        ins = V.tensor_scalar(self.e[:, b, h, :], ps[:, bank, cols], self.s_tab[:, f, h:h + 1], 0.0, ALU.subtract, ALU.min)
                ins.then_inc(self.seg, 1)
                dve.wait_ge(self.exped, n + 1)
                V.tensor_tensor(self.w, self.e, bc(self.s_cb.unsqueeze(2), [P, 3, 4, P]), ALU.mult).then_inc(self.weighed, 1)
            dve.wait_ge(self.copied, l + 1)
            sq = view(m3, 0, TT, D)
            for t in range(TT):
                V.tensor_tensor(sq[:, t, :].rearrange("p (h d) -> p h d", d=PB), self.xs[:, t, :].rearrange("p (h d) -> p h d", d=PB),
                                bc(self.d_skip.unsqueeze(2), [P, HB, PB]), ALU.mult)
            dve.drain()
            V.tensor_tensor(br[:], br[:], sq, ALU.add)
            dve.drain()
            V.tensor_tensor(br[:], br[:], z_b, ALU.mult)
            dve.drain()
            V.tensor_tensor(sq, br[:], br[:], ALU.mult)
            dve.drain()
            V.tensor_reduce(self.st[:, 0:4], sq.rearrange("p t (g n) -> p (t g) n", g=GB), AX.X, ALU.add)
            dve.drain()
            V.tensor_scalar(self.st[:, 4:8], self.st[:, 0:4], float(GB) / D, LN_EPS, ALU.mult, ALU.add).then_inc(pow_asked, 1)
            dve.wait_ge(pow_done, power(l, 2))
            groups = br[:].rearrange("p t (g n) -> p (t g) n", g=GB)
            V.tensor_tensor(groups, groups, bc(self.st[:, 8:12].unsqueeze(2), [P, TT * GB, D // GB]), ALU.mult)
            dve.drain()
            V.tensor_tensor(br[:], br[:], bc(self.norm_g.unsqueeze(1), [P, TT, D]), ALU.mult).then_inc(self.ready, 1)
            self.toT.dve(dve, l)

    class OutProduct:

        def __init__(self, q, w):
            self.q, self.w = q, w

        def sp(self, sp, l):
            for c in range(2):
                load_columns(sp, Block(l, 0, self.q + c), self.w(l), c * 512)

        def pe(self, pe, l):
            for c in range(2):
                for t in range(TT):
                    products(pe, ps[:, 2 * t + c, :], brT, t, Block(l, 0, self.q + c)).then_inc(blk, 1)

        def act(self, act, l):
            for c in range(2):
                round_block(act, Block(l, 0, self.q + c))

        def dve(self, dve, l):
            for c in range(2):
                rest_of_block(dve, Block(l, 0, self.q + c))

    class TurnMerged:
        toT = ToFeatures(merged, brT, 4)

        def pe(self, pe, l):
            self.toT.pe(pe, l)

        def act(self, act, l):
            self.toT.act(act, l)

        def dve(self, dve, l):
            self.toT.dve(dve, l)

    def ffn(q, d, w_in, w_out):
        def gate_up(l, u):
            v = layer_of(A[w_in], l).rearrange("(k p) n -> p k n", p=P)
            return v[:, :, bass.ds(u * UF, UF)], v[:, :, bass.ds(u * UF + FF, UF)]

        def down_rows(l, u):
            return layer_of(A[w_out], l)[bass.ds(u * UF, UF), :].rearrange("(k p) n -> p k n", p=P)
        return Gated(UNITS, q, d, gate_up, down_rows)

    ffn1 = ffn(Q_FFN1, 0, "ffn1_w_in", "ffn1_w_out")
    ffn2 = ffn(Q_FFN2, UNITS, "ffn2_w_in", "ffn2_w_out")
    norm1 = Norm(0, 0, 0, FFN_RES, A["ln1_g"], A["ln1_b"])
    norm2 = Norm(1, 3, 5, 1.0, A["ln2_g"], A["ln2_b"])
    norm3 = Norm(2, 4, 6, FFN_RES, A["ln3_g"], A["ln3_b"])
    diff, stick, scan = DiffAttention(), StickBreaking(), Scan()
    merge_a, merge_c, merge_b = Merge(0, Q_OA, 0), Merge(1, Q_OC, 2), Merge(2, Q_OB, 1)
    out_product = OutProduct(Q_MO, lambda l: layer_of(A["w_mix_out"], l))
    turn_x = ToFeatures(x, xT, -1)
    turn_merged = TurnMerged()

    LAYER = [ffn1, norm1, proj_a, diff, merge_a, proj_c, stick, merge_c, proj_b, scan, merge_b,
             turn_merged, out_product, norm2, ffn2, norm3]
    PHASES = len(LAYER)

    L2 = LAYERS
    rows2 = m1[0:72, 0:P]
    cols2 = vecs[:, 0:72]
    mod = view(vecs, 72, 6, KT)
    mod_flat = vecs[:, 72:120]
    scales = view(vecs, 120, 2, KT)
    a_log2, dt_bias2 = vecs[:, 136:144], vecs[:, 144:152]
    out_norm2, q_norm2, k_norm2 = (vecs[:, 152 + HD2 * i:152 + HD2 * (i + 1)] for i in range(3))
    sinks2 = vecs[:, 344:352]
    router_w = view(vecs, 352, KT, ROUTE)
    router_b = vecs[:, 640:676]
    cw2 = vecs[:, 676:676 + CT * CONV]
    trig = view(vecs, 724, 2, TT, HD2 // 2)
    pos_i = ctx.enter_context(nc.sbuf_tensor("pos_i", [P, TT], I32))
    pos_f = vecs[:, 852:854]
    rows_par, cols_par = sem("rows_par"), sem("cols_par")
    gates2 = ln_par

    def load_second(pool):
        r = lambda name: A[name].rearrange("z (k p) -> (z k) p", p=P)
        at = 0
        for name, n in (("c_2", KT), ("b_ada_2", 6 * KT), ("norm_mix_2", KT), ("norm_ffn_2", KT)):
            pool.dma_start(rows2[at:at + n], r(name)).then_inc(rows_par, 16)
            at += n
        for dst, name in ((a_log2, "a_log_2"), (dt_bias2, "dt_bias_2"), (out_norm2, "gdn_out_norm_2"), (q_norm2, "q_norm_2"),
                          (k_norm2, "k_norm_2"), (sinks2, "sinks_2"), (router_b[:, 0:GROUPS], "b_group_2"), (router_b[:, GROUPS:], "b_router_2")):
            pool.dma_start(dst, A[name].partition_broadcast(P)).then_inc(cols_par, 16)
        for dst, name in ((router_w[:, :, 0:GROUPS], "w_group_2"), (router_w[:, :, GROUPS:], "w_router_2")):
            pool.dma_start(dst, A[name].rearrange("z (k p) n -> p (z k) n", p=P)).then_inc(cols_par, 16)
        for t in range(TT):
            pool.dma_start(pos_i[:, t:t + 1], A["positions_2"][:, t * P:(t + 1) * P].rearrange("b p -> p b")).then_inc(cols_par, 16)
        for g in range(2):
            at = (2 + 3 * g) * D
            pool.dma_start(gates2[:, g, :], A["b_ada_2"][:, at:at + D].partition_broadcast(P)).then_inc(cols_par, 16)
    COLS_PAR = 16 * 14

    class Modulation:
        turned, c_done, used = sem("ada_turned"), sem("ada_c"), sem("ada_used")
        diag = view(m1, 1024, 2, 4, P)

        def sp(self, sp, l):
            def block(i, c):
                load_columns(sp, Block(L2, i, Q_ADA + c), A["w_ada_2"].rearrange("z k n -> (z k) n"), i * 1024 + c * 512)
            pairs(sp, 12, block)

        def pe(self, pe, l):
            pe.wait_ge(rows_par, 64)
            carry(pe)
            pe.transpose(ps[:, 7, 0:72], rows2, ident[0:72, 0:72]).then_inc(self.turned, 1)
            pe.wait_ge(self.c_done, 2)
            carry(pe)
            with pe.Fori(0, 2) as i:
                for c in range(6):
                    b = Block(L2, i * 3, Q_ADA + c)
                    pe.wait_ge(self.used, i * 6 + (c + 1))
                    for k in range(KT):
                        if k % 2 == 0:
                            pe.wait_ge(wide_split, b.split(k // 2))
                        ins = three(pe, ps[:, c % 2, :], [h[:, k:k + 1].to_broadcast([P, P]) for h in c_parts], [h[:, k, :] for h in (b.hi, b.lo)],
                                    k == 0, k == KT - 1)
                    ins.then_inc(blk, 2)

        def act(self, act, l):
            act.wait_ge(self.turned, 1)
            nc.scalar.activation(cols2[:, 0:KT], ps[:, 7, 0:KT], ACT.Silu)
            nc.scalar.copy(cols2[:, KT:72], ps[:, 7, KT:72])
            act.drain()
            act.sem_inc(self.c_done, 1)
            with act.Fori(0, 2) as i:
                for c in range(6):
                    round_block(act, Block(L2, i * 3, Q_ADA + c))

        def dve(self, dve, l):
            V = nc.vector
            dve.wait_ge(self.c_done, 1)
            V.tensor_copy(c_parts[0][:], cols2[:, 0:KT])
            dve.drain()
            V.tensor_tensor(c_parts[1][:], cols2[:, 0:KT], c_parts[0][:], ALU.subtract).then_inc(self.c_done, 1)
            dve.wait_ge(cols_par, COLS_PAR)
            carry(dve)

            def use(i, c):
                dve.wait_ge(blk, Block(L2, i * 3, Q_ADA + c).done(1))
                if c < 4:
                    V.tensor_tensor(self.diag[:, c % 2], view_bank(c % 2, 4, P), bc(ident.unsqueeze(1), [P, 4, P]), ALU.mult).then_inc(self.used, 1)
                    dve.drain()
                    V.tensor_reduce(mod_flat[:, bass.ds(i * 24 + c * 4, 4)], self.diag[:, c % 2], AX.X, ALU.add)
                else:
                    gate = gates2[:, bass.ds(i, 1), (c - 4) * 512:(c - 3) * 512]
                    V.tensor_tensor(gate, ps[:, c % 2:c % 2 + 1, :], gate, ALU.add).then_inc(self.used, 1)
            with dve.Fori(0, 2) as i:
                for c in range(6):
                    rest_of_block(dve, Block(L2, i * 3, Q_ADA + c))
                    if c:
                        use(i, c - 1)
                use(i, 5)
            dve.drain()
            V.tensor_tensor(mod_flat, mod_flat, cols2[:, KT:7 * KT], ALU.add)
            dve.drain()
            for g in range(2):
                V.scalar_tensor_tensor(out=scales[:, g, :], in0=mod[:, 1 + 3 * g, :], scalar=1.0, in1=cols2[:, (7 + g) * KT:(8 + g) * KT],
                                       op0=ALU.add, op1=ALU.mult)

    class Modulate:

        h = view(m2, 0, KT, TOK)

        def __init__(self, g, power, turn):
            self.g, self.power, self.turn = g, power, turn

        def add_gated(self, dve, gate):
            for t in range(TT):
                acc = ps[:, 2 * t:2 * t + 2, :].rearrange("p a b -> p (a b)")
                nc.vector.tensor_tensor(merged[:, t, :], gates2[:, gate, :], acc, ALU.mult)
            dve.drain()
            nc.vector.tensor_tensor(x[:], x[:], merged[:], ALU.add)
            dve.drain()

        def dve(self, dve, l):
            V = nc.vector
            if self.g:
                self.add_gated(dve, 0)
            V.tensor_tensor(merged[:], x[:], x[:], ALU.mult)
            dve.drain()
            V.tensor_reduce(small[:, 0:2], merged[:], AX.X, ALU.add)
            dve.drain()
            V.tensor_scalar(small[:, 2:4], small[:, 0:2], 1.0 / D, RMS_EPS, ALU.mult, ALU.add).then_inc(pow_asked, 1)
            dve.wait_ge(pow_done, power(L2, self.power))
            for t in range(TT):
                ins = V.tensor_scalar(merged[:, t, :], x[:, t, :], small[:, 4 + t:5 + t], None, ALU.mult)
            ins.then_inc(normed, 1)
            for kp in range(4):
                k = slice(2 * kp, 2 * kp + 2)
                dve.wait_ge(feat_rounded, turn(L2, self.turn, kp))
                V.tensor_copy(xT[0][:, k, :], self.h[:, k, :])
                dve.drain()
                V.tensor_tensor(xT[1][:, k, :], self.h[:, k, :], xT[0][:, k, :], ALU.subtract)

        def pool(self, pool, l):
            pool.wait_ge(pow_asked, power(L2, self.power))
            nc.gpsimd.tensor_tensor(small[:, 4:6], small[:, 2:4], const("minus_half")[:, 0:2], ALU.pow).then_inc(pow_done, 1)

        def pe(self, pe, l):
            pe.wait_ge(normed, L2 * 3 + self.g + 1)
            for kp in range(4):
                for kk in range(2):
                    for t in range(TT):
                        k, at = 2 * kp + kk, kk * TOK + t * P
                        ins = pe.transpose(ps[:, kp, at:at + P], merged[:, t, k * P:(k + 1) * P], ident)
                ins.then_inc(feat_turned, 1)

        def act(self, act, l):
            for k in range(KT):
                act.wait_ge(feat_turned, turn(L2, self.turn, k // 2))
                ins = nc.scalar.activation(self.h[:, k, :], ps[:, k // 2, (k % 2) * TOK:(k % 2 + 1) * TOK], ACT.Identity,
                                           bias=mod[:, 3 * self.g, k:k + 1], scale=scales[:, self.g, k:k + 1])
                if k % 2:
                    ins.then_inc(feat_rounded, 1)

    z_2 = view(m1, 0, TT, G2W)
    q_s = view(m1, 1024, TT, G2W)
    ab_2 = view(m1, 2048 + CT * (TOK + CONV - 1), TT, 2 * H2)
    kv_s = view(m1, 5200, TT, 2 * KV2 * HD2)
    w_2 = lambda l: A["w_in_2"].rearrange("z k n -> (z k) n")
    proj_2 = Project(Q_P2, 0, [("feat", w_2, W2["qkv"] + c * 512, 512, lambda part, c=c: xbc[:, c * 4 + part * 2:c * 4 + part * 2 + 2, CONV - 1:])
                               for c in range(3)]
                     + [("tok", w_2, W2["z"], 512, lambda part: z_2[:, part:part + 1, :]),
                        ("tok", w_2, W2["ab"], 2 * H2, lambda part: ab_2[:, part:part + 1, :]),
                        ("tok", w_2, W2["sq"], 512, lambda part: q_s[:, part:part + 1, :]),
                        ("tok", w_2, W2["skv"], 256, lambda part: kv_s[:, part:part + 1, :])])

    class DeltaRule:
        par, cw_turned, cw_done, convolved, silu_done = sem("g_par"), sem("g_cw_turned"), sem("g_cw"), sem("g_conv"), sem("g_silu")
        turned, tok_done = sem("g_turned"), sem("g_tok")
        ab_abs, ab_log, decay, cum, cums, exps, table = (sem(f"g_{n}") for n in ("ab_abs", "ab_log", "decay", "cum", "cums", "exps", "table"))
        staged, scaled, split, splitT = sem("g_staged"), sem("g_scaled"), sem("g_split"), sem("g_splitT")
        gram, seg, dec, mats = sem("g_gram"), sem("g_seg"), sem("g_dec"), sem("g_mats")
        level, lt, lt_done, upd, upd_done = sem("g_level"), sem("g_lt"), sem("g_lt_done"), sem("g_upd"), sem("g_upd_done")
        u0, u0_done, state, state_done = sem("g_u0"), sem("g_u0_done"), sem("g_state"), sem("g_state_done")
        vnew, vnew_done, out_done = sem("g_vnew"), sem("g_vnew_done"), sem("g_out")
        copied = sem("g_copied")
        QUADS = H2 // 4
        raw = m1[0:CT * CONV, 5800:5800 + P]
        conv = view(m2, 0, CT, TOK)
        tok = view(m2, 3072, TT, 3 * G2W)
        stage = view(m3, 0, 3, TT, 256)
        kb, vb, kg, qg, kd = (view(m1, 2048 + 512 * i, TT, 256) for i in range(5))
        kT, kbT, qT = (view(m2, 1024 * i, 8, P)[0:HD2] for i in range(3))
        qgT = view(m3, 1536, 4, P)[0:HD2]
        e, mT, aT = (view(m4, 1024 * i, 8, P) for i in range(3))
        T, Tt = (merged[:, i, :].rearrange("p (s n) -> p s n", s=8) for i in range(2))
        LT, LmT = view(xT_work, 0, 8, P), view(xT_work, 1024, 8, P)
        brf = scratch
        vn = view(brf, 0, 8, HD2)
        wT = view(brf, 512, 4, P)[0:HD2]
        st, stn = view(brf, 1024, 4, HD2)[0:HD2], view(brf, 1280, 4, HD2)[0:HD2]
        tab = view(small, 0, 6, TT, H2)
        s_tab = view(vecs, 900, 6, TT, 4)
        sp_ = view(small, 96, TT, H2)
        ss, rs_ = small[:, 112:144], small[:, 144:176]
        gend = view(small, 176, TT, H2)
        anu = small[:, 192:200]

        def load(self, pool, l):
            pool.dma_start(self.raw, A["conv_w_2"].rearrange("z j (c p) -> (z j c) p", p=P)).then_inc(self.par, 16)
            nc.gpsimd.memset(xbc[:, :, 0:CONV - 1], 0.0)

        def pool(self, pool, l):
            pool.wait_ge(pow_asked, power(L2, 1))
            nc.gpsimd.tensor_tensor(self.rs_, self.ss, const("minus_half")[:, 0:32], ALU.pow).then_inc(pow_done, 1)
            pool.wait_ge(self.table, 1)
            with pool.Fori(0, self.QUADS) as i:
                pool.wait_ge(self.out_done, i + 1)
                for j in range(3):
                    nc.gpsimd.tensor_copy(self.stage[:, j], self.tok[:, :, bass.ds(i * 256 + j * G2W, 256)])
                flat = self.tab.rearrange("p f t h -> p (f t) h")
                nc.gpsimd.tensor_copy(self.s_tab.rearrange("p f t h -> p (f t) h"), flat[:, :, bass.ds(i * 4, 4)]).then_inc(self.staged, 1)
            pool.wait_ge(pow_asked, power(L2, 2))
            nc.gpsimd.tensor_tensor(self.rs_[:, 0:16], self.ss[:, 0:16], const("minus_half")[:, 0:16], ALU.pow).then_inc(pow_done, 1)

        def pe(self, pe, l):
            n_par = CT * CONV
            pe.wait_ge(self.par, 16)
            pe.transpose(ps[:, 7, 0:n_par], self.raw, ident[0:n_par, 0:n_par]).then_inc(self.cw_turned, 1)
            pe.wait_ge(self.decay, 1)
            g2 = self.tab[:, 0].rearrange("p t h -> p (t h)")
            pe.matmul(ps[:, 6, 0:16], const("upto"), g2, start=True, stop=True)
            pe.matmul(ps[:, 6, 16:32], const("ones"), g2, start=True, stop=True).then_inc(self.cum, 1)
            pe.wait_ge(self.silu_done, 1)
            for t in range(TT):
                for c in range(CT):
                    ins = pe.transpose(ps[:, 3 * t + c // 4, (c % 4) * P:(c % 4 + 1) * P], self.conv[:, c, t * P:(t + 1) * P], ident)
                ins.then_inc(self.turned, 1)
            pe.wait_ge(self.table, 1)
            with pe.Fori(0, self.QUADS) as i:
                pe.wait_ge(self.scaled, i + 1)
                carry(pe)
                for n, src in enumerate((self.stage[:, 1], self.kb, self.stage[:, 0])):
                    for s in range(8):
                        t, h = divmod(s, 4)
                        ins = pe.transpose(ps[0:HD2, 2 * n + t, h * P:(h + 1) * P], src[:, t, h * HD2:(h + 1) * HD2], ident)
                for h in range(4):
                    ins = pe.transpose(ps[0:HD2, 6, h * P:(h + 1) * P], self.qg[:, 1, h * HD2:(h + 1) * HD2], ident)
                ins.then_inc(self.split, 1)
                pe.wait_ge(self.splitT, i * 2 + 2)
                for s in range(8):
                    t, h = divmod(s, 4)
                    cols = slice(h * P, (h + 1) * P)
                    pe.matmul(ps[:, t, cols], self.s_tab[:, 0, t, h:h + 1].to_broadcast([P, P]), const("upto"), start=True, stop=True)
                    pe.matmul(ps[:, 2 + t, cols], self.kT[:, s, :], self.kbT[:, s, :], start=True, stop=True)
                    ins = pe.matmul(ps[:, 4 + t, cols], self.kT[:, s, :], self.qT[:, s, :], start=True, stop=True)
                ins.then_inc(self.gram, 1)
                for v in range(LEVELS):
                    n = i * LEVELS + v
                    pe.wait_ge(self.level, n + 1)
                    for s in range(8):
                        ins = pe.matmul(ps[:, s // 4, (s % 4) * P:(s % 4 + 1) * P], self.LmT[:, s, :], self.T[:, s, :], start=True, stop=True)
                    ins.then_inc(self.lt, 1)
                    pe.wait_ge(self.lt_done, n * 2 + 2)
                    for s in range(8):
                        cols = slice((s % 4) * P, (s % 4 + 1) * P)
                        pe.matmul(ps[:, 2 + s // 4, cols], self.Tt[:, s, :], self.LT[:, s, :], start=True, stop=True)
                        ins = pe.matmul(ps[:, 4 + s // 4, cols], self.LT[:, s, :], self.Tt[:, s, :], start=True, stop=True)
                    ins.then_inc(self.upd, 1)
                pe.wait_ge(self.upd_done, i + 1)
                for h in range(4):
                    pe.matmul(ps[:, 6, h * HD2:(h + 1) * HD2], self.Tt[:, h, :], self.vb[:, 0, h * HD2:(h + 1) * HD2], start=True, stop=True)
                for h in range(4):
                    ins = pe.matmul(ps[0:HD2, 0, h * P:(h + 1) * P], self.kg[:, 1, h * HD2:(h + 1) * HD2], self.Tt[:, 4 + h, :], start=True, stop=True)
                ins.then_inc(self.u0, 1)
                pe.wait_ge(self.u0_done, i * 2 + 2)
                for h in range(4):
                    ins = pe.matmul(ps[0:HD2, 1, h * HD2:(h + 1) * HD2], self.kd[:, 0, h * HD2:(h + 1) * HD2], self.vn[:, h, :], start=True, stop=True)
                ins.then_inc(self.state, 1)
                pe.wait_ge(self.state_done, i + 1)
                for h in range(4):
                    o = ps[:, 2, h * HD2:(h + 1) * HD2]
                    pe.matmul(o, self.Tt[:, 4 + h, :], self.vb[:, 1, h * HD2:(h + 1) * HD2], start=True, stop=False)
                    ins = pe.matmul(o, self.wT[:, h, :], self.stn[:, h, :], start=False, stop=True)
                ins.then_inc(self.vnew, 1)
                pe.wait_ge(self.vnew_done, i + 1)
                for h in range(4):
                    pe.matmul(ps[:, 7, h * HD2:(h + 1) * HD2], self.aT[:, h, :], self.vn[:, h, :], start=True, stop=True)
                    o = ps[:, 7, 256 + h * HD2:256 + (h + 1) * HD2]
                    pe.matmul(o, self.qgT[:, h, :], self.st[:, h, :], start=True, stop=False)
                    ins = pe.matmul(o, self.aT[:, 4 + h, :], self.vn[:, 4 + h, :], start=False, stop=True)
                ins.then_inc(self.out_done, 1)

        def act(self, act, l):
            act.wait_ge(self.cw_turned, 1)
            nc.scalar.copy(cw2, ps[:, 7, 0:CT * CONV]).then_inc(self.cw_done, 1)
            act.wait_ge(self.ab_abs, 1)
            nc.scalar.activation(self.sp_, self.sp_, ACT.Exp, scale=-1.0)
            nc.scalar.activation(self.anu, a_log2, ACT.Exp)
            act.drain()
            nc.scalar.activation(self.sp_, self.sp_, ACT.Ln, bias=1.0).then_inc(self.ab_log, 1)
            act.wait_ge(self.convolved, 1)
            nc.scalar.activation(self.tab[:, 2], ab_2[:, :, H2:2 * H2], ACT.Sigmoid)
            nc.scalar.activation(z_2, z_2, ACT.Silu)
            nc.scalar.activation(self.conv, self.conv, ACT.Silu)
            act.drain()
            act.sem_inc(self.silu_done, 1)
            for t in range(TT):
                act.wait_ge(self.turned, t + 1)
                ins = nc.scalar.copy(self.tok[:, t, :], ps[:, 3 * t:3 * t + 3, :].rearrange("p a b -> p (a b)"))
            ins.then_inc(self.tok_done, 1)
            act.wait_ge(self.cums, 1)
            nc.scalar.activation(self.tab[:, 3], self.tab[:, 1], ACT.Exp)
            nc.scalar.activation(self.tab[:, 5], self.gend, ACT.Exp).then_inc(self.exps, 1)
            with act.Fori(0, self.QUADS) as i:
                act.wait_ge(self.split, i + 1)
                two = lambda b: ps[0:HD2, b:b + 2, :].rearrange("p a (h n) -> p (a h) n", n=P)
                nc.scalar.copy(self.kT, two(0))
                nc.scalar.copy(self.qgT, ps[0:HD2, 6, :].rearrange("p (h n) -> p h n", n=P)).then_inc(self.splitT, 1)
                act.wait_ge(self.seg, i + 1)
                nc.scalar.activation(self.e, self.e, ACT.Exp).then_inc(self.dec, 1)
                for v in range(LEVELS):
                    n = i * LEVELS + v
                    act.wait_ge(self.lt, n + 1)
                    nc.scalar.copy(self.LT[:, 0:4, :], view_bank(0, 4, P)).then_inc(self.lt_done, 1)
                act.wait_ge(self.u0, i + 1)
                nc.scalar.copy(self.wT, ps[0:HD2, 0, :].rearrange("p (h n) -> p h n", n=P)).then_inc(self.u0_done, 1)
                act.wait_ge(self.out_done, i + 2)
                nc.scalar.copy(br[:, :, bass.ds(i * 256, 256)], view_bank(7, TT, 256))
            act.drain()
            act.sem_inc(self.copied, 1)

        def dve(self, dve, l):
            V = nc.vector
            dve.wait_ge(cols_par, COLS_PAR)
            a = view(small, 200, TT, H2)
            V.tensor_tensor(a, ab_2[:, :, 0:H2], bc(dt_bias2.unsqueeze(1), [P, TT, H2]), ALU.add)
            dve.drain()
            V.scalar_tensor_tensor(out=self.sp_, in0=a, scalar=-1.0, in1=a, op0=ALU.mult, op1=ALU.max).then_inc(self.ab_abs, 1)
            dve.wait_ge(self.ab_log, 1)
            V.scalar_tensor_tensor(out=a, in0=a, scalar=0.0, in1=self.sp_, op0=ALU.max, op1=ALU.add)
            dve.drain()
            V.scalar_tensor_tensor(out=self.tab[:, 0], in0=a, scalar=-1.0, in1=bc(self.anu.unsqueeze(1), [P, TT, H2]), op0=ALU.mult, op1=ALU.mult).then_inc(self.decay, 1)
            dve.wait_ge(self.cw_done, 1)
            convolve(dve, self.conv, xbc, lambda j, c: cw2[:, bass.ds(c + j * CT, 1)])
            dve.sem_inc(self.convolved, 1)
            dve.wait_ge(self.cum, 1)
            G = view_bank(6, 2, TT, H2)
            V.tensor_copy(self.tab[:, 1], G[:, 0])
            dve.drain()
            V.tensor_tensor(self.gend, G[:, 1], self.tab[:, 1], ALU.subtract)
            dve.drain()
            dve.sem_inc(self.cums, 1)
            dve.wait_ge(self.tok_done, 1)
            sq = view(m3, 0, TT, 16, HD2)
            for t in range(TT):
                qk = self.tok[:, t, 0:1024].rearrange("p (h d) -> p h d", d=HD2)
                V.tensor_tensor(sq[:, t], qk, qk, ALU.mult)
            dve.drain()
            V.tensor_reduce(self.ss, sq.rearrange("p t h d -> p (t h) d"), AX.X, ALU.add)
            dve.drain()
            V.tensor_scalar(self.ss, self.ss, RMS_EPS, None, ALU.add).then_inc(pow_asked, 1)
            dve.wait_ge(self.exps, 1)
            V.tensor_tensor(self.tab[:, 4], self.tab[:, 2], self.tab[:, 3], ALU.mult)
            dve.wait_ge(pow_done, power(L2, 1))
            r2 = self.rs_.rearrange("p (t h) -> p t h", t=TT)
            V.tensor_scalar(r2[:, :, 0:H2], r2[:, :, 0:H2], HD2 ** -0.5, None, ALU.mult)
            dve.drain()
            for t in range(TT):
                qk = self.tok[:, t, 0:1024].rearrange("p (h d) -> p h d", d=HD2)
                V.tensor_tensor(qk, qk, bc(r2[:, t, :].unsqueeze(2), [P, 16, HD2]), ALU.mult)
            dve.drain()
            dve.sem_inc(self.table, 1)
            lev = consts[:, CONSTS["level1"][0]:CONSTS["level1"][0] + LEVELS * P].rearrange("p (v n) -> p v n", n=P)
            with dve.Fori(0, self.QUADS) as i:
                dve.wait_ge(self.staged, i + 1)
                heads = lambda ap: ap.rearrange("p t (h d) -> p (t h) d", d=HD2)
                f = lambda n: bc(self.s_tab[:, n].rearrange("p t h -> p (t h)").unsqueeze(2), [P, 8, HD2])
                V.tensor_tensor(heads(self.kb), heads(self.stage[:, 1]), f(2), ALU.mult)
                V.tensor_tensor(heads(self.vb), heads(self.stage[:, 2]), f(2), ALU.mult)
                V.tensor_tensor(heads(self.kg), heads(self.stage[:, 1]), f(4), ALU.mult)
                V.tensor_tensor(heads(self.qg), heads(self.stage[:, 0]), f(3), ALU.mult)
                V.tensor_tensor(heads(self.kd), heads(self.stage[:, 1]), f(5), ALU.mult).then_inc(self.scaled, 1)
                V.tensor_copy(self.T, bc(ident.unsqueeze(1), [P, 8, P]))
                V.tensor_copy(self.Tt, bc(ident.unsqueeze(1), [P, 8, P]))
                dve.wait_ge(self.split, i + 1)
                two = lambda b: ps[0:HD2, b:b + 2, :].rearrange("p a (h n) -> p (a h) n", n=P)
                V.tensor_copy(self.kbT, two(2))
                V.tensor_copy(self.qT, two(4)).then_inc(self.splitT, 1)
                dve.wait_ge(self.gram, i + 1)
                for s in range(8):
                    t, h = divmod(s, 4)
                    ins = V.tensor_scalar(self.e[:, s, :], ps[:, t, h * P:(h + 1) * P], self.s_tab[:, 1, t, h:h + 1], 0.0, ALU.subtract, ALU.min)
                ins.then_inc(self.seg, 1)
                dve.wait_ge(self.dec, i + 1)
                V.tensor_tensor(self.e, self.e, bc(const("upto").unsqueeze(1), [P, 8, P]), ALU.mult)
                dve.drain()
                big = lambda b: ps[:, b:b + 2, :].rearrange("p a (h n) -> p (a h) n", n=P)
                V.tensor_tensor(self.mT, self.e, big(2), ALU.mult)
                V.tensor_tensor(self.aT, self.e, big(4), ALU.mult)
                dve.drain()
                for v in range(LEVELS):
                    n = i * LEVELS + v
                    V.tensor_tensor(self.LmT, self.mT, bc(lev[:, v:v + 1, :], [P, 8, P]), ALU.mult).then_inc(self.level, 1)
                    dve.wait_ge(self.lt, n + 1)
                    V.tensor_copy(self.LT[:, 4:8, :], view_bank(1, 4, P)).then_inc(self.lt_done, 1)
                    dve.wait_ge(self.upd, n + 1)
                    V.tensor_tensor(self.T, self.T, big(2), ALU.subtract)
                    V.tensor_tensor(self.Tt, self.Tt, big(4), ALU.subtract)
                    dve.drain()
                dve.sem_inc(self.upd_done, 1)
                dve.wait_ge(self.u0, i + 1)
                V.tensor_copy(self.vn[:, 0:4, :], ps[:, 6, 0:256].rearrange("p (h n) -> p h n", n=HD2)).then_inc(self.u0_done, 1)
                dve.wait_ge(self.state, i + 1)
                V.tensor_copy(self.st, ps[0:HD2, 1, 0:256].rearrange("p (h n) -> p h n", n=HD2))
                V.tensor_scalar(self.stn, ps[0:HD2, 1, 0:256].rearrange("p (h n) -> p h n", n=HD2), -1.0, None, ALU.mult).then_inc(self.state_done, 1)
                dve.wait_ge(self.vnew, i + 1)
                V.tensor_copy(self.vn[:, 4:8, :], ps[:, 2, 0:256].rearrange("p (h n) -> p h n", n=HD2)).then_inc(self.vnew_done, 1)
            dve.wait_ge(self.copied, 1)
            o = br[:, :, 0:G2W]
            sq = view(m3, 0, TT, G2W)
            V.tensor_tensor(sq, o, o, ALU.mult)
            dve.drain()
            V.tensor_reduce(self.ss[:, 0:16], sq.rearrange("p t (h d) -> p (t h) d", d=HD2), AX.X, ALU.add)
            dve.drain()
            V.tensor_scalar(self.ss[:, 0:16], self.ss[:, 0:16], 1.0 / HD2, RMS_EPS, ALU.mult, ALU.add).then_inc(pow_asked, 1)
            dve.wait_ge(pow_done, power(L2, 2))
            for t in range(TT):
                oh = o[:, t, :].rearrange("p (h d) -> p h d", d=HD2)
                V.tensor_tensor(oh, oh, bc(self.rs_[:, t * H2:(t + 1) * H2].unsqueeze(2), [P, H2, HD2]), ALU.mult)
            dve.drain()
            for t in range(TT):
                oh = o[:, t, :].rearrange("p (h d) -> p h d", d=HD2)
                V.tensor_tensor(oh, oh, bc(out_norm2.unsqueeze(1), [P, H2, HD2]), ALU.mult)
            dve.drain()
            V.tensor_tensor(o, o, z_2, ALU.mult)

    class WindowAttention:
        roped, angles, trig_done = sem("s_roped"), sem("s_angles"), sem("s_trig")
        staged, turned, qT_done, scored, masked, exped = (sem(f"s_{n}") for n in ("staged", "turned", "qT", "scored", "masked", "exped"))
        weighed, w_turned, wT_done, out_done, ready = (sem(f"s_{n}") for n in ("weighed", "w_turned", "wT", "out", "ready"))
        HEADS = H2 + KV2
        qk = view(m2, 0, TT, HEADS, HD2)
        sq = view(m3, 0, TT, HEADS, HD2)
        half = HD2 // 2
        GQ = H2 // KV2
        q, k, v = view(m4, 0, TT, 256), view(m4, 512, TT, HD2), view(m4, 640, TT, HD2)
        qT, kT = view(m4, 768, GQ, TOK)[0:HD2], m4[0:HD2, 1792:1792 + TOK]
        s0, s1 = view(m2, 1280, GQ, P), view(m2, 1792, GQ, TOK)
        wT = view(m2, 2816, 3 * GQ, P)
        ss, rs_ = small[:, 0:20], small[:, 20:40]
        nmx, sums, esink, inv = (view(small, 48 + 8 * i, TT, H2 // KV2) for i in range(4))
        s_sink = small[:, 88:92]
        ang = view(m3, 1280, 2, TT, HD2 // 2)
        turns = view(m3, 1408, 2, TT, HD2 // 2)
        toT = ToFeatures(br, brT, 1)

        def pool(self, pool, l):
            pool.wait_ge(pow_asked, power(L2, 3))
            nc.gpsimd.tensor_tensor(self.rs_, self.ss, const("minus_half")[:, 0:20], ALU.pow).then_inc(pow_done, 1)
            pool.wait_ge(self.roped, 1)
            with pool.Fori(0, KV2) as g:
                pool.wait_ge(self.out_done, g + 1)
                for t in range(TT):
                    nc.gpsimd.tensor_copy(self.q[:, t, :].rearrange("p (h d) -> p h d", d=HD2), self.qk[:, t, bass.ds(g * 4, 4), :])
                nc.gpsimd.tensor_copy(self.k.unsqueeze(2), self.qk[:, :, bass.ds(g + H2, 1), :])
                nc.gpsimd.tensor_copy(self.s_sink, sinks2[:, bass.ds(g * 4, 4)])
                nc.gpsimd.tensor_copy(self.v, kv_s[:, :, bass.ds(g * HD2 + KV2 * HD2, HD2)]).then_inc(self.staged, 1)

        def pe(self, pe, l):
            with pe.Fori(0, KV2) as g:
                pe.wait_ge(self.staged, g + 1)
                carry(pe)
                for h in range(self.GQ):
                    for t in range(TT):
                        at = (h % 2) * TOK + t * P
                        pe.transpose(ps[0:HD2, h // 2, at:at + P], self.q[:, t, h * HD2:(h + 1) * HD2], ident)
                for t in range(TT):
                    ins = pe.transpose(ps[0:HD2, 2, t * P:(t + 1) * P], self.k[:, t, :], ident)
                ins.then_inc(self.turned, 1)
                pe.wait_ge(self.qT_done, g * 2 + 2)
                for h in range(self.GQ):
                    pe.matmul(ps[:, 3, h * P:(h + 1) * P], self.qT[:, h, 0:P], self.kT[:, 0:P], start=True, stop=True)
                    ins = pe.matmul(ps[:, 4 + h // 2, (h % 2) * TOK:(h % 2 + 1) * TOK], self.qT[:, h, P:TOK], self.kT, start=True, stop=True)
                ins.then_inc(self.scored, 1)
                pe.wait_ge(self.weighed, g + 1)
                for h in range(self.GQ):
                    pe.transpose(ps[:, 0, h * P:(h + 1) * P], self.s0[:, h, :], ident)
                    for b in range(2):
                        ins = pe.transpose(ps[:, 1 + b, h * P:(h + 1) * P], self.s1[:, h, b * P:(b + 1) * P], ident)
                ins.then_inc(self.w_turned, 1)
                pe.wait_ge(self.wT_done, g + 1)
                for h in range(self.GQ):
                    pe.matmul(ps[:, 6, h * HD2:(h + 1) * HD2], self.wT[:, h, :], self.v[:, 0, :], start=True, stop=True)
                    o = ps[:, 6, 256 + h * HD2:256 + (h + 1) * HD2]
                    pe.matmul(o, self.wT[:, 4 + h, :], self.v[:, 0, :], start=True, stop=False)
                    ins = pe.matmul(o, self.wT[:, 8 + h, :], self.v[:, 1, :], start=False, stop=True)
                ins.then_inc(self.out_done, 1)
            pe.wait_ge(self.ready, 1)
            self.toT.pe(pe, L2)

        def act(self, act, l):
            act.wait_ge(self.angles, 1)
            nc.scalar.activation(trig, self.ang, ACT.Sin).then_inc(self.trig_done, 1)
            with act.Fori(0, KV2) as g:
                act.wait_ge(self.turned, g + 1)
                nc.scalar.mul(self.qT, ps[0:HD2, 0:2, :].rearrange("p a (h n) -> p (a h) n", n=TOK), HD2 ** -0.5).then_inc(self.qT_done, 1)
                act.wait_ge(self.masked, g + 1)
                for h in range(self.GQ):
                    nc.scalar.activation(self.s0[:, h, :], self.s0[:, h, :], ACT.Exp, bias=self.nmx[:, 0, h:h + 1], accum_out=self.sums[:, 0, h:h + 1])
                    nc.scalar.activation(self.s1[:, h, :], self.s1[:, h, :], ACT.Exp, bias=self.nmx[:, 1, h:h + 1], accum_out=self.sums[:, 1, h:h + 1])
                nc.scalar.activation(self.esink, self.esink, ACT.Exp).then_inc(self.exped, 1)
                act.wait_ge(self.w_turned, g + 1)
                nc.scalar.copy(self.wT, ps[:, 0:3, :].rearrange("p a (h n) -> p (a h) n", n=P)).then_inc(self.wT_done, 1)
                act.wait_ge(self.out_done, g + 2)
                nc.scalar.copy(br[:, :, bass.ds(g * 256 + G2W, 256)], view_bank(6, TT, 256))
            act.drain()
            act.sem_inc(self.ready, 1)
            self.toT.act(act, L2)

        def dve(self, dve, l):
            V = nc.vector
            V.tensor_copy(pos_f, pos_i[:])
            dve.drain()
            for t in range(TT):
                V.tensor_scalar(self.ang[:, 1, t, :], const("inv_freq"), pos_f[:, t:t + 1], None, ALU.mult)
            dve.drain()
            magic = 1.5 * 2.0 ** 23
            a1, a0 = self.ang[:, 1], self.ang[:, 0]
            V.tensor_scalar(self.turns[:, 0], a1, 0.5 / np.pi, 0.25, ALU.mult, ALU.add)
            V.tensor_scalar(self.turns[:, 1], a1, 0.5 / np.pi, None, ALU.mult)
            V.tensor_copy(a0, a1)
            dve.drain()
            V.tensor_scalar(self.turns, self.turns, magic, None, ALU.add)
            dve.drain()
            V.tensor_scalar(self.turns, self.turns, magic, None, ALU.subtract)
            dve.drain()
            rest = 2.0 * np.pi
            flat = lambda ap: ap.rearrange("p a t n -> p (a t n)")
            for bits in (2.0 ** 5, 2.0 ** 17, None):
                part = rest if bits is None else np.floor(rest * bits) / bits
                rest -= part
                V.scalar_tensor_tensor(out=flat(self.ang), in0=flat(self.turns), scalar=-float(part), in1=flat(self.ang), op0=ALU.mult, op1=ALU.add)
                dve.drain()
            V.tensor_scalar(a0, a0, 0.5 * np.pi, None, ALU.add)
            dve.drain()
            V.tensor_scalar(flat(self.ang), flat(self.ang), 3.1415925, -3.1415925, ALU.min, ALU.max).then_inc(self.angles, 1)
            heads = lambda ap: ap.rearrange("p t (h d) -> p t h d", d=HD2)
            qh, kh = heads(q_s), heads(kv_s[:, :, 0:KV2 * HD2])
            V.tensor_tensor(self.sq[:, :, 0:H2, :], qh, qh, ALU.mult)
            V.tensor_tensor(self.sq[:, :, H2:, :], kh, kh, ALU.mult)
            dve.drain()
            V.tensor_reduce(self.ss, self.sq.rearrange("p t h d -> p (t h) d"), AX.X, ALU.add)
            dve.drain()
            V.tensor_scalar(self.ss, self.ss, 1.0 / HD2, RMS_EPS, ALU.mult, ALU.add).then_inc(pow_asked, 1)
            dve.wait_ge(pow_done, power(L2, 3))
            r = self.rs_.rearrange("p (t h) -> p t h", t=TT)
            for t in range(TT):
                V.tensor_tensor(self.qk[:, t, 0:H2, :], qh[:, t], bc(r[:, t, 0:H2].unsqueeze(2), [P, H2, HD2]), ALU.mult)
                V.tensor_tensor(self.qk[:, t, H2:, :], kh[:, t], bc(r[:, t, H2:].unsqueeze(2), [P, KV2, HD2]), ALU.mult)
            dve.drain()
            for t in range(TT):
                V.tensor_tensor(self.qk[:, t, 0:H2, :], self.qk[:, t, 0:H2, :], bc(q_norm2.unsqueeze(1), [P, H2, HD2]), ALU.mult)
                V.tensor_tensor(self.qk[:, t, H2:, :], self.qk[:, t, H2:, :], bc(k_norm2.unsqueeze(1), [P, KV2, HD2]), ALU.mult)
            dve.wait_ge(self.trig_done, 1)
            dve.drain()
            for t in range(TT):
                a, b = self.qk[:, t, :, 0:self.half], self.qk[:, t, :, self.half:]
                cos, sin = (bc(trig[:, c, t, :].unsqueeze(1), [P, self.HEADS, self.half]) for c in range(2))
                ac, bs, bcs, as_ = (view(m3, 320 * i, self.HEADS, self.half) for i in range(4))
                V.tensor_tensor(ac, a, cos, ALU.mult)
                V.tensor_tensor(bs, b, sin, ALU.mult)
                V.tensor_tensor(bcs, b, cos, ALU.mult)
                V.tensor_tensor(as_, a, sin, ALU.mult)
                dve.drain()
                V.tensor_tensor(a, ac, bs, ALU.subtract)
                V.tensor_tensor(b, bcs, as_, ALU.add)
                dve.drain()
            dve.sem_inc(self.roped, 1)
            causal, window = (bc(const(n).unsqueeze(1), [P, self.GQ, P]) for n in ("causal_add", "window_add"))
            with dve.Fori(0, KV2) as g:
                dve.wait_ge(self.turned, g + 1)
                V.tensor_copy(self.kT, ps[0:HD2, 2, 0:TOK]).then_inc(self.qT_done, 1)
                dve.wait_ge(self.scored, g + 1)
                own = ps[:, 4:6, :].rearrange("p a (h n) -> p (a h) n", n=TOK)
                V.tensor_tensor(self.s0, view_bank(3, self.GQ, P), causal, ALU.add)
                V.tensor_tensor(self.s1[:, :, 0:P], own[:, :, 0:P], window, ALU.add)
                V.tensor_tensor(self.s1[:, :, P:TOK], own[:, :, P:TOK], causal, ALU.add)
                dve.drain()
                V.tensor_reduce(self.nmx[:, 0, :], self.s0, AX.X, ALU.max)
                V.tensor_reduce(self.nmx[:, 1, :], self.s1, AX.X, ALU.max)
                dve.drain()
                sk = bc(self.s_sink.unsqueeze(1), [P, TT, self.GQ])
                V.tensor_tensor(self.nmx, self.nmx, sk, ALU.max)
                dve.drain()
                V.tensor_scalar(self.nmx, self.nmx, -1.0, None, ALU.mult)
                dve.drain()
                V.tensor_tensor(self.esink, self.nmx, sk, ALU.add)
                dve.drain()
                dve.sem_inc(self.masked, 1)
                dve.wait_ge(self.exped, g + 1)
                V.tensor_tensor(self.inv, self.sums, self.esink, ALU.add)
                dve.drain()
                V.reciprocal(self.inv, self.inv)
                dve.drain()
                V.tensor_tensor(self.s0, self.s0, bc(self.inv[:, 0, :].unsqueeze(2), [P, self.GQ, P]), ALU.mult)
                V.tensor_tensor(self.s1, self.s1, bc(self.inv[:, 1, :].unsqueeze(2), [P, self.GQ, TOK]), ALU.mult).then_inc(self.weighed, 1)
            self.toT.dve(dve, L2)

    combine = view(vecs, 1000, TT, EXPERTS)

    class Router:
        logits_done, maxed, exped, diffed, exped2 = (sem(f"r_{n}") for n in ("logits", "maxed", "exped", "diffed", "exped2"))
        lg = view(m3, 0, TT, ROUTE)
        sub = view(m3, 80, TT, GROUPS)
        hot = view(m3, 100, TT, GROUPS)
        cnt = view(m3, 120, TT, PER_GROUP)
        prod = view(m3, 160, TT, GROUPS, PER_GROUP)
        ing, hot1, hot2, tmp = (view(m3, 256 + 16 * i, TT, PER_GROUP) for i in range(4))
        gm, gs, m1_, m2_, e2, w1, w2 = (m3[:, 340 + 2 * i:342 + 2 * i] for i in range(7))

        def pe(self, pe, l):
            for t in range(TT):
                for k in range(KT):
                    for j in range(2):
                        stat = xT[j][:, k, t * P:(t + 1) * P].bitcast(F32)
                        ins = pe.matmul(ps[:, 4, t * ROUTE:(t + 1) * ROUTE], stat, router_w[:, k, :], start=(k == 0 and j == 0),
                                        stop=(k == KT - 1 and j == 1))
            ins.then_inc(self.logits_done, 1)

        def act(self, act, l):
            act.wait_ge(self.maxed, 1)
            nc.scalar.activation(self.sub, self.sub, ACT.Exp).then_inc(self.exped, 1)
            act.wait_ge(self.diffed, 1)
            nc.scalar.activation(self.e2, self.e2, ACT.Exp).then_inc(self.exped2, 1)

        def first_of(self, dve, hot, values, top, n):
            V = nc.vector
            V.tensor_tensor(hot, values, bc(top.unsqueeze(2), [P, TT, n]), ALU.is_equal)
            dve.drain()
            for t in range(TT):
                V.tensor_tensor_scan(self.cnt[:, t, 0:n], const("ones")[:, 0:n], hot[:, t, :], 0.0, ALU.mult, ALU.add)
            dve.drain()
            V.scalar_tensor_tensor(out=hot, in0=self.cnt[:, :, 0:n], scalar=1.0, in1=hot, op0=ALU.is_equal, op1=ALU.mult)
            dve.drain()

        def dve(self, dve, l):
            V = nc.vector
            dve.wait_ge(self.logits_done, 1)
            V.tensor_tensor(self.lg, view_bank(4, TT, ROUTE), bc(router_b.unsqueeze(1), [P, TT, ROUTE]), ALU.add)
            dve.drain()
            gl = self.lg[:, :, 0:GROUPS]
            V.tensor_reduce(self.gm, gl, AX.X, ALU.max)
            dve.drain()
            V.tensor_tensor(self.sub, gl, bc(self.gm.unsqueeze(2), [P, TT, GROUPS]), ALU.subtract).then_inc(self.maxed, 1)
            self.first_of(dve, self.hot, gl, self.gm, GROUPS)
            for t in range(TT):
                V.tensor_tensor(self.prod[:, t], self.lg[:, t, GROUPS:].rearrange("p (g e) -> p g e", g=GROUPS),
                                bc(self.hot[:, t, :].unsqueeze(2), [P, GROUPS, PER_GROUP]), ALU.mult)
            dve.drain()
            for t in range(TT):
                V.tensor_reduce(self.ing[:, t, :], self.prod[:, t].rearrange("p g e -> p e g"), AX.X, ALU.add)
            dve.drain()
            V.tensor_reduce(self.m1_, self.ing, AX.X, ALU.max)
            dve.drain()
            self.first_of(dve, self.hot1, self.ing, self.m1_, PER_GROUP)
            V.scalar_tensor_tensor(out=self.tmp, in0=self.hot1, scalar=NEG, in1=self.ing, op0=ALU.mult, op1=ALU.add)
            dve.drain()
            V.tensor_reduce(self.m2_, self.tmp, AX.X, ALU.max)
            dve.drain()
            V.tensor_tensor(self.e2, self.m2_, self.m1_, ALU.subtract).then_inc(self.diffed, 1)
            self.first_of(dve, self.hot2, self.tmp, self.m2_, PER_GROUP)
            dve.wait_ge(self.exped, 1)
            V.tensor_reduce(self.gs, self.sub, AX.X, ALU.add)
            dve.wait_ge(self.exped2, 1)
            V.tensor_scalar(self.w1, self.e2, 1.0, None, ALU.add)
            dve.drain()
            V.tensor_tensor(self.w1, self.w1, self.gs, ALU.mult)
            dve.drain()
            V.reciprocal(self.w1, self.w1)
            dve.drain()
            V.tensor_tensor(self.w2, self.w1, self.e2, ALU.mult)
            dve.drain()
            V.tensor_tensor(self.hot1, self.hot1, bc(self.w1.unsqueeze(2), [P, TT, PER_GROUP]), ALU.mult)
            V.tensor_tensor(self.hot2, self.hot2, bc(self.w2.unsqueeze(2), [P, TT, PER_GROUP]), ALU.mult)
            dve.drain()
            V.tensor_tensor(self.hot1, self.hot1, self.hot2, ALU.add)
            dve.drain()
            for t in range(TT):
                V.tensor_tensor(combine[:, t, :].rearrange("p (g e) -> p g e", g=GROUPS), bc(self.hot1[:, t:t + 1, :], [P, GROUPS, PER_GROUP]),
                                bc(self.hot[:, t, :].unsqueeze(2), [P, GROUPS, PER_GROUP]), ALU.mult)

    def expert_in(l, u):
        return tuple(A[n][0, bass.ds(u, 1)].rearrange("z (k p) n -> p (z k) n", p=P) for n in ("w_gate_2", "w_up_2"))

    def expert_out(l, u):
        return A["w_down_2"][0, bass.ds(u, 1)].rearrange("z (k p) n -> p (z k) n", p=P)

    experts = Gated(EXPERTS, Q_MOE, 0, expert_in, expert_out, weight=lambda t, u: combine[:, t, bass.ds(u, 1)])
    modulation, delta, window, router = Modulation(), DeltaRule(), WindowAttention(), Router()
    mod_mix, mod_ffn = Modulate(0, 0, 0), Modulate(1, 4, 2)
    out_2 = OutProduct(Q_W2, lambda l: A["w_out_2"].rearrange("z k n -> (z k) n"))

    class Last:

        def dve(self, dve, l):
            mod_ffn.add_gated(dve, 1)

    last = Last()
    SECOND = [modulation, mod_mix, proj_2, delta, window, out_2, mod_ffn, router, experts, last]

    in_par = sem("in_par")
    zeroed = sem("zeroed")
    stored = sem("stored")
    block = ctx.enter_context(nc.Block())

    @block.sync
    def _(sp):
        sp.dma_start(consts[:], A["shape_constants"]).then_inc(in_par, 16)
        sp.dma_start(x[:], A["x"].rearrange("b (t p) d -> p (b t) d", p=P)).then_inc(in_par, 16)
        with sp.Fori(0, LAYERS) as l:
            for phase in (ffn1, proj_a, merge_a, proj_c, merge_c, proj_b, merge_b, out_product, ffn2):
                phase.sp(sp, l)
        for phase in (modulation, proj_2, out_2, experts):
            phase.sp(sp, L2)
        sp.wait_ge(phase_left, (LAYERS * PHASES + len(SECOND) + 1) * 4)
        sp.dma_start(out.rearrange("b (t p) d -> p (b t) d", p=P), x[:]).then_inc(stored, 16)
        sp.wait_ge(stored, 16)

    @block.tensor
    def _(pe):
        pe.sem_inc(blk, BLK0)
        pe.sem_inc(dn, DN0)
        pe.sem_inc(hid_turned, 2)
        for s in (diff, stick, scan, delta, window):
            pe.sem_inc(s.out_done, 1)
        pe.wait_ge(in_par, 32)
        pe.wait_ge(zeroed, 1)
        turn_x.pe(pe, 0)
        leave(pe, 0)
        with pe.Fori(0, LAYERS) as l:
            for n, phase in enumerate(LAYER):
                phase.pe(pe, l)
                leave(pe, l * PHASES + n + 1)
        for n, phase in enumerate(SECOND):
            if phase is not last:
                phase.pe(pe, L2)
            leave(pe, LAYERS * PHASES + n + 1)

    @block.scalar
    def _(act):
        act.sem_inc(copied[0], 2)
        turn_x.act(act, 0)
        leave(act, 0)
        with act.Fori(0, LAYERS) as l:
            for n, phase in enumerate(LAYER):
                phase.act(act, l)
                leave(act, l * PHASES + n + 1)
        for n, phase in enumerate(SECOND):
            if phase is not last:
                phase.act(act, L2)
            leave(act, LAYERS * PHASES + n + 1)

    @block.vector
    def _(dve):
        dve.sem_inc(hid_done, 2)
        dve.sem_inc(hidT_done, 2)
        dve.sem_inc(wide_split, WS0)
        dve.sem_inc(down_split, DS0)
        dve.sem_inc(copied[1], 2)
        dve.sem_inc(modulation.used, 2)
        nc.vector.memset(zrow[:], 0.0).then_inc(zeroed, 1)
        turn_x.dve(dve, 0)
        leave(dve, 0)
        with dve.Fori(0, LAYERS) as l:
            for n, phase in enumerate(LAYER):
                phase.dve(dve, l)
                leave(dve, l * PHASES + n + 1)
        for n, phase in enumerate(SECOND):
            phase.dve(dve, L2)
            leave(dve, LAYERS * PHASES + n + 1)

    @block.gpsimd
    def _(pool):
        pool.wait_ge(in_par, 32)
        leave(pool, 0)
        with pool.Fori(0, LAYERS) as l:
            for n, phase in enumerate(LAYER):
                if phase is ffn1:
                    norm1.load(pool, l)
                elif phase is proj_a:
                    norm2.load(pool, l)
                    diff.load(pool, l)
                elif phase is proj_b:
                    scan.load(pool, l)
                elif phase is ffn2:
                    norm3.load(pool, l)
                elif phase in (merge_a, merge_c, merge_b):
                    phase.load(pool, l)
                if phase in (norm1, norm2, norm3, diff, stick, scan):
                    phase.pool(pool, l)
                leave(pool, l * PHASES + n + 1)
        for n, phase in enumerate(SECOND):
            if phase is modulation:
                load_second(pool)
            elif phase is proj_2:
                delta.load(pool, L2)
            if phase in (mod_mix, delta, window, mod_ffn):
                phase.pool(pool, L2)
            leave(pool, LAYERS * PHASES + n + 1)

    ctx.close()


NAMES = ["x", "ffn1_w_in", "ffn1_w_out", "ln1_g", "ln1_b", "w_mix_in", "gate_bias", "diff_lambda", "diff_subln_g",
         "ssm_conv_w", "ssm_conv_b", "ssm_dt_bias", "ssm_A_log", "ssm_D", "ssm_norm_g", "w_branch", "w_mix_out",
         "ln2_g", "ln2_b", "ffn2_w_in", "ffn2_w_out", "ln3_g", "ln3_b", "c_2", "positions_2", "w_ada_2", "b_ada_2",
         "norm_mix_2", "w_in_2", "conv_w_2", "a_log_2", "dt_bias_2", "gdn_out_norm_2", "q_norm_2", "k_norm_2",
         "sinks_2", "w_out_2", "norm_ffn_2", "w_group_2", "b_group_2", "w_router_2", "b_router_2", "w_gate_2",
         "w_up_2", "w_down_2"]


def kernel(**inputs):
    import concourse.bacc as bacc
    from concourse.bass_utils import run_bass_kernel_spmd
    arrays = {n: np.ascontiguousarray(inputs[n]) for n in NAMES}
    arrays["shape_constants"] = SHAPE_CONSTANTS
    nc = bacc.Bacc("TRN2", target_bir_lowering=False, num_devices=1)
    aps = {n: nc.dram_tensor(f"in_{n}", a.shape, mybir.dt.from_np(a.dtype), kind="ExternalInput").ap() for n, a in arrays.items()}
    out = nc.dram_tensor("out", (1, TOK, D), F32, kind="ExternalOutput").ap()
    build(nc, aps, out)
    r = run_bass_kernel_spmd(nc, [{f"in_{n}": a for n, a in arrays.items()}], core_ids=[0])
    return r.results[0]["out"]
```

```python
from contextlib import ExitStack

import numpy as np

import concourse.bass as bass
from concourse import mybir

F32 = mybir.dt.float32
F32R = mybir.dt.float32r
I32 = mybir.dt.int32
ACT = mybir.ActivationFunctionType
ALU = mybir.AluOpType
AX = mybir.AxisListType

P = 128
TT = 2
TOK = P * TT
D = 1024
KT = D // P
LAYERS = 2
FF = 2816
UF = 256
UNITS = FF // UF
ALPHA = (2 * LAYERS) ** 0.25
FFN_RES = 0.5
LN_EPS = 1e-5
RMS_EPS = 1e-6
NEG = -1e30

HA, HDA, ROT_A = 8, 64, 16
HB, PB, GB, NB, CONV = 16, 64, 2, 128, 4
CONV_DIM = HB * PB + 2 * GB * NB
CT = CONV_DIM // P
HC, HDC = 16, 64
C_QA, C_KA, C_VA, C_Z, C_XBC = 0, 1024, 2048, 3072, 4096
C_DT = C_XBC + CONV_DIM
C_QC = C_DT + HB
C_KC, C_VC, C_G = C_QC + 1024, C_QC + 2048, C_QC + 3072

H2, HD2, KV2 = 8, 64, 2
G2W = H2 * HD2
EXPERTS, GROUPS, PER_GROUP = 32, 4, 8
ROUTE = GROUPS + EXPERTS
W2 = dict(qkv=0, z=3 * G2W, ab=4 * G2W, sq=4 * G2W + 2 * H2, skv=5 * G2W + 2 * H2)
LEVELS = 7

Q_FFN1 = 0
Q_A = Q_FFN1 + UNITS
Q_OA = Q_A + 6
Q_C = Q_OA + 4
Q_ADA = Q_C + 6
ADA_C, ADA_B = 8, 4
Q_OC = Q_ADA + ADA_C
Q_B = Q_OC + 4
Q_ADA_B = Q_B + 6
Q_OB = Q_ADA_B + ADA_B
Q_MO = Q_OB + 4
Q_FFN2 = Q_MO + 2
Q_LAYER = Q_FFN2 + UNITS
assert Q_LAYER % 2 == 0
Q_P2 = 0
Q_W2 = Q_P2 + 7
Q_MOE = Q_W2 + 2
D_LAYER = 2 * UNITS
ADA_LAYER = ADA_C + ADA_B
ADA_COLS = 6 * D // (LAYERS * ADA_LAYER)

CONSTS = {}


def shape_constants():
    p = np.arange(P)[:, None]
    j = np.arange(P)[None, :]
    parts = [
        ("ident", p == j),
        ("ones", np.ones((P, P))),
        ("upto", p <= j),
        ("from_", p >= j),
        ("chunk_add", np.where(j // 64 <= p // 64, 0, NEG)),
        ("stick_add", np.concatenate([np.where(p < j, 0, NEG), 0 * (p + j), np.where(p < j, 0, NEG)], 1)),
        ("causal_add", np.where(j <= p, 0, NEG)),
        ("window_add", np.where(j > p, 0, NEG)),
    ]
    for b in [1 << n for n in range(LEVELS)]:
        parts.append((f"level{b}", ((j // b) % 2 == 1) & (p // b == j // b - 1)))
    half = ROT_A // 2
    inv = np.float32(500000.0) ** (-np.arange(half, dtype=np.float32) * np.float32(2.0) / np.float32(ROT_A))
    ang = np.arange(TOK, dtype=np.float32)[:, None] * inv[None, :].astype(np.float32)
    for name, f in (("cos_a", np.cos), ("sin_a", np.sin)):
        t = f(ang.astype(np.float32)).astype(np.float32).reshape(TT, P, half)
        parts.append((name, t.transpose(1, 0, 2).reshape(P, TT * half)))
    h2 = HD2 // 2
    inv2 = np.power(np.float32(10000.0), -np.arange(h2, dtype=np.float32) / np.float32(h2))
    parts.append(("inv_freq", np.broadcast_to(inv2.astype(np.float32), (P, h2))))
    li = [0.8 - 0.6 * np.exp(-0.3 * l) for l in range(LAYERS)]
    parts.append(("lam_init", np.broadcast_to(np.array(li, np.float32), (P, LAYERS))))
    parts.append(("one_minus_lam", np.broadcast_to(1.0 - np.array(li), (P, LAYERS))))
    parts.append(("minus_half", np.full((P, 64), -0.5)))
    at, cols = 0, []
    for name, a in parts:
        a = np.asarray(a, np.float32)
        CONSTS[name] = (at, a.shape[1])
        at += a.shape[1]
        cols.append(a)
    return np.ascontiguousarray(np.concatenate(cols, 1))


SHAPE_CONSTANTS = shape_constants()


def build(nc, A, out, stop=99):
    ctx = ExitStack()

    place = {}

    def sb(name, shape, dt=F32):
        place[name] = nc.sbuf_base
        return ctx.enter_context(nc.sbuf_tensor(name, shape, dt))

    def over(name, shape, other, col=0, dt=F32R):
        return nc.alloc_sbuf_tensor_at(name, shape, dt, offset=place[other] + 4 * col)

    def sem(name):
        return ctx.enter_context(nc.semaphore(name))

    consts = sb("consts", [P, SHAPE_CONSTANTS.shape[1]])
    wide = [sb(f"wide{s}", [P, KT, 512]) for s in range(2)]
    down = [sb(f"down{s}", [P, 2, D]) for s in range(2)]
    x = sb("x", [P, TT, D])
    xT = [sb(f"xT_{part}", [P, KT, TOK], F32R) for part in ("hi", "lo")]
    ln_par = sb("ln_par", [P, 2, D])
    sil = sb("sil", [P, TT, UF])
    hid = sb("hid", [P, TT, UF])
    hidT = [sb(f"hidT_{part}", [P, TT, 2, P], F32R) for part in ("hi", "lo")]
    small = sb("small", [P, 256])
    zrow = sb("zrow", [1, 512])
    merged = sb("merged", [P, TT, D])
    m1 = sb("m1", [P, 6144])
    work = sb("work", [P, 16384])
    vecs = sb("vecs", [P, 1536])
    ps = ctx.enter_context(nc.psum_tensor("ps", [P, 8, 512], F32))

    def const(name, rows=P):
        at, n = CONSTS[name]
        return consts[0:rows, at:at + n]

    ident = const("ident")

    def view(t, at, *dims):
        n = int(np.prod(dims))
        names = " ".join(f"d{i}" for i in range(len(dims)))
        return t[:, at:at + n].rearrange(f"p ({names}) -> p {names}", **{f"d{i}": d for i, d in enumerate(dims)})

    m2, m3, m4 = work[:, 0:6144], work[:, 6144:8192], work[:, 8192:11264]
    br = view(work, 11264, TT, D)
    scratch = work[:, 13312:15360]

    wide_hi, wide_lo = ([over(f"wide_{part}{s}", [P, KT, 512], "work", (2 * i + s) * KT * 512) for s in range(2)] for i, part in enumerate(("hi", "lo")))
    down_hi = [over(f"down_hi{s}", [P, 2, D], "m1", s * 2 * D) for s in range(2)]
    down_lo = [over("down_lo0", [P, 2, D], "m1", 4 * D), over("down_lo1", [P, 2, D], "merged")]
    brT = [over(f"brT_{part}", [P, KT, TOK], "m1", 2048 * (i + 1)) for i, part in enumerate(("hi", "lo"))]
    xT_work = over("xT_work", [P, KT * TOK], "xT_hi", dt=F32)

    def bc(ap, shape):
        return ap.to_broadcast(shape) if not isinstance(shape, int) else ap.to_broadcast([shape])

    wide_full = [sem(f"wide_full{s}") for s in range(2)]
    down_full = [sem(f"down_full{s}") for s in range(2)]
    wide_rounded, down_rounded = sem("wide_rounded"), sem("down_rounded")
    wide_split, down_split = sem("wide_split"), sem("down_split")
    blk = sem("block_done")
    dn = sem("down_done")
    RANGES = ((0, 1), (1, 2), (2, 4), (4, 6), (6, 8))
    NR = len(RANGES)
    BLK0, DN0, WS0, DS0 = 3, 2, NR + 1, 2
    phase_left = sem("phase_left")

    pow_asked, pow_done = sem("pow_asked"), sem("pow_done")
    POW_LAYER = 5
    feat_turned = sem("to_features")
    feat_rounded = sem("feat_rounded")
    TURN_LAYER = 7

    def power(l, nth):
        return l * POW_LAYER + (nth + 1)

    def turn(l, nth, kp):
        return l * (4 * TURN_LAYER) + (4 * (nth + 1) + kp + 1)

    class Block:

        def __init__(self, l, i, c):
            self.number = l * Q_LAYER + i * 2 + c
            self.slot = c % 2
            self.landed = (l * (Q_LAYER // 2) + i + c // 2 + 1) * 32
            self.may_load = self.number * NR + (WS0 - NR)
            self.may_split = self.number * 2 + (BLK0 - 2)
            self.tile, self.hi, self.lo = wide[self.slot], wide_hi[self.slot], wide_lo[self.slot]

        def rounded(self, q):
            return self.number * NR + (q + 1)

        def split(self, q):
            return self.number * NR + (WS0 + q + 1)

        def done(self, t):
            return self.number * 2 + (BLK0 + t + 1)

    class Down:
        def __init__(self, l, i, c):
            self.number = l * D_LAYER + i * 2 + c
            self.slot = c % 2
            self.landed = (l * (D_LAYER // 2) + i + c // 2 + 1) * 16
            self.may_load = self.number + (DS0 - 1)
            self.may_split = self.number + (DN0 - 1)
            self.rounded = self.number + 1
            self.split = self.number + (DS0 + 1)
            self.tile, self.hi, self.lo = down[self.slot], down_hi[self.slot], down_lo[self.slot]

    def steps(eng, n, first, body, last):
        first()
        with eng.Fori(0, (n - 1) // 2) as i:
            body(i, 1)
            body(i, 2)
        if (n - 1) % 2:
            body(0, n - 1)
        last()

    def pairs(eng, n, body):
        with eng.Fori(0, n // 2) as i:
            body(i, 0)
            body(i, 1)
        if n % 2:
            body(0, n - 1)

    carried = sem("waits_carried")

    def carry(eng):
        eng.sem_inc(carried, 1)

    def leave(eng, phase):
        eng.drain()
        eng.sem_inc(phase_left, 1)
        eng.wait_ge(phase_left, phase * 4 + 4)
        carry(eng)

    def load_halves(sp, b, lo, hi, dst):
        sp.wait_ge(wide_split, b.may_load)
        sp.dma_start(dst[0], lo).then_inc(wide_full[b.slot], 16)
        sp.dma_start(dst[1], hi).then_inc(wide_full[b.slot], 16)

    def load_columns(sp, b, w, col, n=512):
        v = w.rearrange("(k p) n -> p k n", p=P)[:, :, bass.ds(col, n)]
        load_halves(sp, b, v[:, 0:4, :], v[:, 4:8, :], (b.tile[:, 0:4, 0:n], b.tile[:, 4:8, 0:n]))

    def layer_of(ap, l):
        names = " ".join("abcd"[:len(ap.shape) - 1])
        return ap[bass.ds(l, 1)].rearrange(f"z {names} -> (z {names.split()[0]}) {' '.join(names.split()[1:])}")

    def round_block(act, b, n=512):
        act.wait_ge(wide_full[b.slot], b.landed)
        act.wait_ge(blk, b.may_split)
        for k0, k1 in RANGES:
            nc.scalar.copy(b.hi[:, k0:k1, 0:n], b.tile[:, k0:k1, 0:n]).then_inc(wide_rounded, 1)

    def rest_of_block(dve, b, n=512):
        for q, (k0, k1) in enumerate(RANGES):
            k = slice(k0, k1)
            dve.wait_ge(wide_rounded, b.rounded(q))
            nc.vector.tensor_tensor(b.lo[:, k, 0:n], b.tile[:, k, 0:n], b.hi[:, k, 0:n], ALU.subtract).then_inc(wide_split, 1)

    def three(pe, out, a, b, start, stop):
        pe.matmul(out, a[0], b[0], start=start, stop=False)
        pe.matmul(out, a[0], b[1], start=False, stop=False)
        return pe.matmul(out, a[1], b[0], start=False, stop=stop)

    def await_parts(pe, b, k):
        for q, (k0, k1) in enumerate(RANGES):
            if k == k0:
                pe.wait_ge(wide_split, b.split(q))

    def products(pe, bank, stat, t, b, n=512, start=True):
        for k in range(KT):
            if t == 0:
                await_parts(pe, b, k)
            last = three(pe, bank[:, 0:n], [s[:, k, t * P:(t + 1) * P] for s in stat], [w[:, k, 0:n] for w in (b.hi, b.lo)],
                         start and k == 0, k == KT - 1)
        return last

    class ToFeatures:

        def __init__(self, src, dst, nth):
            self.src, self.dst, self.nth = src, dst, nth

        def pe(self, pe, l, await_quarter=lambda kp: None):
            for kp in range(4):
                await_quarter(kp)
                for kk in range(2):
                    for t in range(TT):
                        k = 2 * kp + kk
                        at = kk * TOK + t * P
                        ins = pe.transpose(ps[:, kp, at:at + P], self.src[:, t, k * P:(k + 1) * P], ident)
                ins.then_inc(feat_turned, 1)

        def act(self, act, l):
            for kp in range(4):
                act.wait_ge(feat_turned, turn(l, self.nth, kp))
                nc.scalar.copy(self.dst[0][:, 2 * kp:2 * kp + 2, :], view_bank(kp, 2, TOK)).then_inc(feat_rounded, 1)

        def dve(self, dve, l):
            for kp in range(4):
                dve.wait_ge(feat_rounded, turn(l, self.nth, kp))
                k = slice(2 * kp, 2 * kp + 2)
                nc.vector.tensor_tensor(self.dst[1][:, k, :], view_bank(kp, 2, TOK), self.dst[0][:, k, :], ALU.subtract)

    def view_bank(b, *dims):
        names = " ".join(f"d{i}" for i in range(len(dims)))
        n = int(np.prod(dims))
        return ps[:, b, 0:n].rearrange(f"p ({names}) -> p {names}", **{f"d{i}": d for i, d in enumerate(dims)})

    sil_done = sem("sil_done")
    hid_done = sem("hid_done")
    hid_turned = sem("hid_turned")
    hidT_rounded = sem("hidT_rounded")
    hidT_done = sem("hidT_done")
    HALVES_LAYER = 4 * UNITS

    acc_ready = sem("acc_ready")

    class Gated:

        def __init__(self, units, q, d, gate_up, down_rows, weight=None, prepared=False):
            self.units, self.q, self.d, self.prepared = units, q, d, prepared
            self.gate_up, self.down_rows, self.weight = gate_up, down_rows, weight

        def await_sum(self, eng, l, t):
            if t == 0:
                eng.wait_ge(acc_ready, l * 2 + (self.d // UNITS + 1))
            else:
                eng.wait_ge(dn, Down(l, 0, self.d + self.units - 1).number + (DN0 + 1))

        def sp(self, sp, l):
            def unit(i, c):
                b, d = Block(l, i, self.q + c), Down(l, i, self.d + c)
                lo, hi = self.gate_up(l, i * 2 + c)
                load_halves(sp, b, lo, hi, (b.tile[:, :, 0:UF], b.tile[:, :, UF:2 * UF]))
                sp.wait_ge(down_split, d.may_load)
                sp.dma_start(d.tile[:], self.down_rows(l, i * 2 + c)).then_inc(down_full[d.slot], 16)
            pairs(sp, self.units, unit)

        def blocks(self, l, i, c):
            return Block(l, i, self.q + c), Down(l, i, self.d + c), l * HALVES_LAYER + i * 4 + (2 * self.d + c * 2)

        def pe(self, pe, l):
            def gate_up(i, c):
                b, d, n = self.blocks(l, i, c)
                for t in range(TT):
                    pe.wait_ge(hid_done, n + t + 1)
                    products(pe, ps[:, 4 + t, :], xT, t, b).then_inc(blk, 1)

            def turn_hidden(i, c):
                b, d, n = self.blocks(l, i, c)
                for t in range(TT):
                    pe.wait_ge(hid_done, n + t + 3)
                    pe.wait_ge(hidT_done, n + t + 1)
                    for k in range(2):
                        ins = pe.transpose(ps[:, 6 + t, k * P:(k + 1) * P], hid[:, t, k * P:(k + 1) * P], ident)
                    ins.then_inc(hid_turned, 1)

            def down_products(i, c, final=False):
                b, d, n = self.blocks(l, i, c)
                pe.wait_ge(down_split, d.split)
                for t in range(TT):
                    pe.wait_ge(hidT_done, n + t + 3)
                    for half in range(2):
                        cols = slice(half * 512, (half + 1) * 512)
                        for k in range(2):
                            a, w = [h[:, t, k, :] for h in hidT], [h[:, k, cols] for h in (d.hi, d.lo)]
                            for u, v in ((0, 0), (0, 1), (1, 0)):
                                ins = pe.matmul(ps[:, 2 * t + half, :], a[u], w[v], start=False, stop=False, skip_group_check=True)
                    if final and t == 0:
                        ins.then_inc(acc_ready, 1)
                ins.then_inc(dn, 1)

            def first():
                gate_up(0, 0)
                for bank in range(4):
                    pe.matmul(ps[:, bank, :], zrow[0:1, 0:P], zrow[0:1, :], start=True, stop=False, skip_group_check=True)
                turn_hidden(0, 0)

            def unit(i, c):
                gate_up(i, c)
                down_products(i, c - 1)
                turn_hidden(i, c)
            steps(pe, self.units, first, unit, lambda: down_products(0, self.units - 1, True))

        def act(self, act, l):
            def split(i, c):
                b, d, n = self.blocks(l, i, c)
                round_block(act, b)

            def rest(i, c):
                b, d, n = self.blocks(l, i, c)
                for t in range(TT):
                    act.wait_ge(blk, b.done(t))
                    nc.scalar.activation(sil[:, t, :], ps[:, 4 + t, 0:UF], ACT.Silu).then_inc(sil_done, 1)
                act.wait_ge(down_full[d.slot], d.landed)
                act.wait_ge(dn, d.may_split)
                nc.scalar.copy(d.hi[:], d.tile[:]).then_inc(down_rounded, 1)
                for t in range(TT):
                    act.wait_ge(hid_turned, n + t + 3)
                    nc.scalar.copy(hidT[0][:, t], ps[:, 6 + t, 0:UF].rearrange("p (k n) -> p k n", k=2)).then_inc(hidT_rounded, 1)

            def unit(i, c):
                split(i, c)
                rest(i, c - 1)
            steps(act, self.units, lambda: self.prepared or split(0, 0), unit, lambda: rest(0, self.units - 1))

        def dve(self, dve, l):
            def split(i, c):
                b, d, n = self.blocks(l, i, c)
                rest_of_block(dve, b)

            def rest(i, c):
                b, d, n = self.blocks(l, i, c)
                for t in range(TT):
                    dve.wait_ge(sil_done, n + t + 1)
                    dve.wait_ge(hid_turned, n + t + 1)
                    if self.weight is None:
                        nc.vector.tensor_tensor(hid[:, t, :], sil[:, t, :], ps[:, 4 + t, UF:2 * UF], ALU.mult).then_inc(hid_done, 1)
                    else:
                        nc.vector.scalar_tensor_tensor(out=hid[:, t, :], in0=sil[:, t, :], scalar=self.weight(t, i * 2 + c),
                                                       in1=ps[:, 4 + t, UF:2 * UF], op0=ALU.mult, op1=ALU.mult).then_inc(hid_done, 1)
                dve.wait_ge(down_rounded, d.rounded)
                nc.vector.tensor_tensor(d.lo[:], d.tile[:], d.hi[:], ALU.subtract).then_inc(down_split, 1)
                for t in range(TT):
                    dve.wait_ge(hidT_rounded, n + t + 1)
                    nc.vector.tensor_tensor(hidT[1][:, t], ps[:, 6 + t, 0:UF].rearrange("p (k n) -> p k n", k=2), hidT[0][:, t],
                                            ALU.subtract).then_inc(hidT_done, 1)

            def unit(i, c):
                split(i, c)
                rest(i, c - 1)
            steps(dve, self.units, lambda: self.prepared or split(0, 0), unit, lambda: rest(0, self.units - 1))

    norm_par = sem("norm_par")
    ln_scaled, ln_added, ln_mean, ln_squared, ln_done = (sem(f"ln_{n}") for n in ("scaled", "added", "mean", "squared", "done"))

    class Norm:

        def __init__(self, nth, power, turn, source, r, g, b):
            self.nth, self.power, self.source, self.r, self.g, self.b = nth, power, source, r, g, b
            self.toT = ToFeatures(x, xT, turn)

        def load(self, pool, l):
            if self.nth:
                pool.wait_ge(feat_turned, turn(l, {1: 0, 2: 5}[self.nth], 3))
                carry(pool)
            nc.gpsimd.tensor_scalar(x[:], x[:], ALPHA, None, ALU.mult).then_inc(ln_scaled, 1)
            pool.dma_start(ln_par[:, 0, :], self.g[bass.ds(l, 1), :].partition_broadcast(P)).then_inc(norm_par, 16)
            pool.dma_start(ln_par[:, 1, :], self.b[bass.ds(l, 1), :].partition_broadcast(P)).then_inc(norm_par, 16)

        def dve(self, dve, l):
            V, y, n = nc.vector, merged, l * 3 + (self.nth + 1)
            st, mv = view(small, 0, 2, 6), small[:, 24:26]
            dve.wait_ge(ln_scaled, n)
            for t in range(TT):
                self.source.await_sum(dve, l, t)
                acc = ps[:, 2 * t:2 * t + 2, :].rearrange("p a b -> p (a b)")
                ins = V.scalar_tensor_tensor(out=x[:, t, :], in0=acc, scalar=self.r, in1=x[:, t, :], op0=ALU.mult, op1=ALU.add)
                if t == 0:
                    ins.then_inc(ln_added, 1)
            dve.drain()
            for h in range(2):
                V.bn_stats(st[:, h, :], x[:, 1, h * 512:(h + 1) * 512])
            dve.drain()
            V.bn_aggr(mv, st.rearrange("p a b -> p (a b)"))
            dve.wait_ge(norm_par, l * 96 + (self.nth + 1) * 32)
            dve.wait_ge(ln_mean, n)
            V.scalar_tensor_tensor(out=y[:, 0, :], in0=x[:, 0, :], scalar=small[:, 28:29], in1=ln_par[:, 0, :], op0=ALU.add, op1=ALU.mult)
            dve.drain()
            dve.wait_ge(ln_squared, n)
            V.tensor_scalar(small[:, 30:31], small[:, 29:30], 1.0 / D, LN_EPS, ALU.mult, ALU.add)
            V.tensor_scalar(small[:, 31:32], mv[:, 1:2], LN_EPS, None, ALU.add).then_inc(pow_asked, 1)
            V.scalar_tensor_tensor(out=y[:, 1, :], in0=x[:, 1, :], scalar=mv[:, 0:1], in1=ln_par[:, 0, :], op0=ALU.subtract, op1=ALU.mult)
            dve.drain()
            dve.wait_ge(pow_done, power(l, self.power))
            for q in range(4):
                c = slice(q * D // 4, (q + 1) * D // 4)
                for t in range(TT):
                    ins = V.scalar_tensor_tensor(out=x[:, t, c], in0=y[:, t, c], scalar=small[:, 32 + t:33 + t], in1=ln_par[:, 1, c],
                                                 op0=ALU.mult, op1=ALU.add)
                ins.then_inc(ln_done, 1)
            self.toT.dve(dve, l)

        def pool(self, pool, l):
            pool.wait_ge(pow_asked, power(l, self.power))
            nc.gpsimd.tensor_tensor(small[:, 32:34], small[:, 30:32], const("minus_half")[:, 0:2], ALU.pow).then_inc(pow_done, 1)

        def pe(self, pe, l):
            self.toT.pe(pe, l, lambda q: pe.wait_ge(ln_done, l * 12 + (self.nth * 4 + q + 1)))

        def act(self, act, l):
            spare = ps[:, 4:6, :].rearrange("p a b -> p (a b)")
            act.wait_ge(ln_added, l * 3 + (self.nth + 1))
            nc.scalar.activation(spare, x[:, 0, :], ACT.Identity, scale=-1.0 / D, accum_out=small[:, 28:29]).then_inc(ln_mean, 1)
            act.drain()
            nc.scalar.activation(spare, x[:, 0, :], ACT.Square, bias=small[:, 28:29], accum_out=small[:, 29:30]).then_inc(ln_squared, 1)
            self.toT.act(act, l)

    copied = [sem(f"projection_copied{part}") for part in range(2)]
    COPIED_LAYER = 6 + 6 + 6

    class Project:

        def __init__(self, q, before, blocks, merge=None):
            self.q, self.before, self.blocks, self.merge = q, before, blocks, merge

        def sp(self, sp, l):
            for c, (kind, w, col, n, dst) in enumerate(self.blocks):
                load_columns(sp, Block(l, 0, self.q + c), w(l), col, n)

        def pe(self, pe, l):
            for c, (kind, w, col, n, dst) in enumerate(self.blocks):
                b = Block(l, 0, self.q + c)
                for part in range(2):
                    pe.wait_ge(copied[part], l * COPIED_LAYER + (self.before + c + 1))
                    bank = ps[:, 2 * (c % 2) + part, :]
                    if kind == "tok":
                        last = products(pe, bank, xT, part, b, n)
                    else:
                        for f in range(2):
                            at = (2 * part + f) * P
                            for k in range(KT):
                                if part == 0 and f == 0:
                                    await_parts(pe, b, k)
                                last = three(pe, bank[:, f * TOK:(f + 1) * TOK], [h[:, k, at:at + P] for h in (b.hi, b.lo)],
                                             [s[:, k, :] for s in xT], k == 0, k == KT - 1)
                    last.then_inc(blk, 1)

        def copy(self, eng, op, l, part, c):
            kind, w, col, n, dst = self.blocks[c]
            eng.wait_ge(blk, Block(l, 0, self.q + c).done(part))
            bank = 2 * (c % 2) + part
            src = ps[:, bank:bank + 1, 0:n] if kind == "tok" else view_bank(bank, 2, TOK)
            op(dst(part), src).then_inc(copied[part], 1)

        def act(self, act, l):
            for c, (kind, w, col, n, dst) in enumerate(self.blocks):
                if c == 1 and self.merge is not None:
                    act.wait_ge(half_added, self.merge.added(l, 1))
                if c or self.merge is None:
                    round_block(act, Block(l, 0, self.q + c), n)
                if c:
                    self.copy(act, nc.scalar.copy, l, 0, c - 1)
            self.copy(act, nc.scalar.copy, l, 0, len(self.blocks) - 1)

        def dve(self, dve, l):
            for c, (kind, w, col, n, dst) in enumerate(self.blocks):
                if c or self.merge is None:
                    rest_of_block(dve, Block(l, 0, self.q + c), n)
                if c:
                    self.copy(dve, nc.vector.tensor_copy, l, 1, c - 1)
            self.copy(dve, nc.vector.tensor_copy, l, 1, len(self.blocks) - 1)

    w_mix = lambda l: layer_of(A["w_mix_in"], l)

    cols2 = vecs[:, 1360:1432]
    mod_flat = vecs[:, 1300:1348]
    mod = view(vecs, 1300, 6, KT)
    scales = view(vecs, 1432, 2, KT)

    class ModulationPieces:
        rows_par, turned, cols_done = sem("ada_rows"), sem("ada_turned"), sem("ada_cols")
        used = sem("ada_used")
        rows = m1[0:72, 0:P]

        def load(self, act):
            at = 0
            for name, n in (("c_2", KT), ("b_ada_2", 6 * KT), ("norm_mix_2", KT), ("norm_ffn_2", KT)):
                act.dma_start(self.rows[at:at + n], A[name].rearrange("z (k p) -> (z k) p", p=P)).then_inc(self.rows_par, 16)
                at += n

        def turn_pe(self, pe):
            pe.wait_ge(self.rows_par, 64)
            carry(pe)
            pe.transpose(ps[:, 7, 0:72], self.rows, ident[0:72, 0:72]).then_inc(self.turned, 1)

        def turn_act(self, act):
            act.wait_ge(self.turned, 1)
            nc.scalar.activation(cols2[:, 0:KT], ps[:, 7, 0:KT], ACT.Silu)
            nc.scalar.copy(cols2[:, KT:72], ps[:, 7, KT:72])

        def block(self, l, i, c):
            return Block(l, i, Q_ADA + c if c < ADA_C else Q_ADA_B + c - ADA_C)

        def sp(self, sp, l, which):
            w = A["w_ada_2"].rearrange("z k n -> (z k) n")
            for c in which:
                load_columns(sp, self.block(l, 0, c), w, l * (ADA_LAYER * ADA_COLS) + c * ADA_COLS, ADA_COLS)

        def pe(self, pe, l, i, c, bank):
            b = self.block(l, i, c)
            pe.wait_ge(wide_full[b.slot], b.landed)
            pe.wait_ge(self.used, l * ADA_LAYER + i * 2 + (c + 1))
            for k in range(KT):
                ins = pe.matmul(ps[:, bank, 0:ADA_COLS], cols2[:, k:k + 1].to_broadcast([P, P]), b.tile[:, k, 0:ADA_COLS], start=(k == 0), stop=(k == KT - 1))
            ins.then_inc(blk, 2)

        def act(self, act, n):
            act.sem_inc(wide_rounded, NR * n)

        def dve(self, dve, l, i, c, bank, diag):
            tiles = ADA_COLS // P
            dve.wait_ge(blk, self.block(l, i, c).done(1))
            nc.vector.tensor_tensor(diag, view_bank(bank, tiles, P), bc(ident.unsqueeze(1), [P, tiles, P]), ALU.mult).then_inc(self.used, 1)
            dve.drain()
            at = l * (ADA_LAYER * tiles) + i * (2 * tiles) + c * tiles
            nc.vector.tensor_reduce(mod_flat[:, bass.ds(at, tiles)], diag, AX.X, ALU.add).then_inc(wide_split, NR)

    pieces = ModulationPieces()

    qkv_a = view(m1, 0, 3, TT, D)
    proj_a = Project(Q_A, 0, [("tok", w_mix, C_QA + c * 512, 512, lambda part, c=c: qkv_a[:, c // 2, part:part + 1, (c % 2) * 512:(c % 2 + 1) * 512])
                              for c in range(6)])

    class DiffAttention:
        par = sem("a_par")
        lam_sum, lam_exp = sem("a_lam_sum"), sem("a_lam_exp")
        roped = sem("a_roped")
        qk_staged, v_staged = sem("a_qk_staged"), sem("a_v_staged")
        turned, qT_done, kT_done = sem("a_turned"), sem("a_qT"), sem("a_kT")
        scored, masked, exped, mixed = sem("a_scored"), sem("a_masked"), sem("a_exped"), sem("a_mixed")
        w_turned, wT_done = sem("a_w_turned"), sem("a_wT")
        out_done, out_copied = sem("a_out"), sem("a_out_copied")
        ready = sem("a_ready")
        qk = [view(m4, 768 * e, 2, TT, P) for e in range(2)]
        v = [view(m4, 768 * e + 512, TT, P) for e in range(2)]
        qT, kT = ([view(scratch, 1024 * e + 512 * j, 2, TOK)[0:HDA] for e in range(2)] for j in range(2))
        sm = [m2[:, 768 * e:768 * e + 768] for e in range(2)]
        w = [m2[:, 1536 + 384 * e:1920 + 384 * e] for e in range(2)]
        wT = [view(m2, 2304 + 384 * e, 3, P) for e in range(2)]
        st = m2[:, 3072:3136]
        squares = st[:, 0:16]
        sq = [view(m2, 3200 + 256 * e, TT, P) for e in range(2)]
        hs = [m2[:, 3136 + 16 * e:3152 + 16 * e] for e in range(2)]
        subln = vecs[:, 0:2 * HDA]
        lam4 = view(vecs, 128, 4, HDA)
        toT = ToFeatures(br, brT, 1)

        def load(self, pool, l):
            pool.dma_start(self.subln, A["diff_subln_g"][bass.ds(l, 1), :].partition_broadcast(P)).then_inc(self.par, 16)
            pool.dma_start(vecs[:, 128:384], A["diff_lambda"].rearrange("l a d -> l (a d)")[bass.ds(l, 1), :].partition_broadcast(P)).then_inc(self.par, 16)

        def pool(self, pool, l):
            pool.wait_ge(self.roped, l + 1)
            carry(pool)
            with pool.Fori(0, HA // 2) as i:
                n = l * HA + i * 2
                for e in range(2):
                    pool.wait_ge(self.turned, n * 2 + (2 * e + 1))
                    for j in range(2):
                        ins = nc.gpsimd.tensor_copy(self.qk[e][:, j], qkv_a[:, j, :, bass.ds(i * (2 * P) + e * P, P)])
                    ins.then_inc(self.qk_staged, 1)
                for e in range(2):
                    pool.wait_ge(self.out_done, n + (e + 1))
                    nc.gpsimd.tensor_copy(self.v[e], qkv_a[:, 2, :, bass.ds(i * (2 * P) + e * P, P)]).then_inc(self.v_staged, 1)
            pool.wait_ge(pow_asked, power(l, 1))
            nc.gpsimd.tensor_tensor(self.st[:, 32:48], self.st[:, 16:32], const("minus_half")[:, 0:16], ALU.pow).then_inc(pow_done, 1)

        def pe(self, pe, l):
            with pe.Fori(0, HA // 2) as i:
                n = l * HA + i * 2
                for e in range(2):
                    pe.wait_ge(self.qk_staged, n + (e + 1))
                    pe.wait_ge(self.out_copied, n + (e + 1))
                    carry(pe)
                    for j in range(2):
                        for m in range(2):
                            for t in range(TT):
                                ins = pe.transpose(ps[0:HDA, 2 * e + j, m * TOK + t * P:m * TOK + (t + 1) * P],
                                                   self.qk[e][:, j, t, m * HDA:(m + 1) * HDA], ident)
                        ins.then_inc(self.turned, 1)
                for e in range(2):
                    pe.wait_ge(self.qT_done, n + (e + 1))
                    pe.wait_ge(self.kT_done, n + (e + 1))
                    for t in range(TT):
                        keys = (t + 1) * P
                        for m in range(2):
                            ins = pe.matmul(ps[:, 4 + 2 * e + t, m * keys:(m + 1) * keys], self.qT[e][:, m, t * P:(t + 1) * P],
                                            self.kT[e][:, m, 0:keys], start=True, stop=True)
                    ins.then_inc(self.scored, 1)
                for e in range(2):
                    pe.wait_ge(self.mixed, n + (e + 1))
                    for b in range(3):
                        ins = pe.transpose(ps[:, 2 * e, b * P:(b + 1) * P], self.w[e][:, b * P:(b + 1) * P], ident)
                    ins.then_inc(self.w_turned, 1)
                for e in range(2):
                    pe.wait_ge(self.v_staged, n + (e + 1))
                    pe.wait_ge(self.wT_done, n + (e + 1))
                    out = view_bank(2 * e + 1, 2, P)
                    wT, v = self.wT[e], self.v[e]
                    pe.matmul(out[:, 0, :], wT[:, 0, :], v[:, 0, :], start=True, stop=True)
                    pe.matmul(out[:, 1, :], wT[:, 1, :], v[:, 0, :], start=True, stop=False)
                    pe.matmul(out[:, 1, :], wT[:, 2, :], v[:, 1, :], start=False, stop=True).then_inc(self.out_done, 1)
            pe.wait_ge(self.ready, l + 1)
            self.toT.pe(pe, l)

        def act(self, act, l):
            act.wait_ge(self.lam_sum, l + 1)
            nc.scalar.activation(self.st[:, 52:54], self.st[:, 50:52], ACT.Exp).then_inc(self.lam_exp, 1)
            with act.Fori(0, HA // 2) as i:
                n = l * HA + i * 2
                for e in range(2):
                    act.wait_ge(self.turned, n * 2 + (2 * e + 4))
                    nc.scalar.mul(self.qT[e], view_bank(2 * e, 2, TOK)[0:HDA], HDA ** -0.5).then_inc(self.qT_done, 1)
                for e in range(2):
                    act.wait_ge(self.masked, n + (e + 1))
                    at = 0
                    for t in range(TT):
                        keys = (t + 1) * P
                        for m in range(2):
                            c = 2 * t + m
                            ins = nc.scalar.activation(self.sm[e][:, at:at + keys], self.sm[e][:, at:at + keys], ACT.Exp,
                                                       bias=self.hs[e][:, c:c + 1], accum_out=self.hs[e][:, 4 + c:5 + c])
                            at += keys
                    ins.then_inc(self.exped, 1)
                for e in range(2):
                    act.wait_ge(self.w_turned, n + (e + 1))
                    nc.scalar.copy(self.wT[e], view_bank(2 * e, 3, P)).then_inc(self.wT_done, 1)
            self.toT.act(act, l)

        def dve(self, dve, l):
            V, st = nc.vector, self.st
            half = ROT_A // 2
            for t in range(TT):
                maps = qkv_a[:, 0:2, t, :].rearrange("p j (m d) -> p j m d", d=HDA)
                a, b = maps[:, :, :, 0:half], maps[:, :, :, half:ROT_A]
                cos, sin = (bc(const(c)[:, t * half:(t + 1) * half].unsqueeze(1).unsqueeze(1), [P, 2, 16, half]) for c in ("cos_a", "sin_a"))
                ac, bs, bcs, as_ = (view(m3, 256 + 256 * (4 * t + i), 2, 16, half) if 4 * t + i < 7 else view(m2, 4096, 2, 16, half) for i in range(4))
                V.tensor_tensor(ac, a, cos, ALU.mult)
                V.tensor_tensor(bs, b, sin, ALU.mult)
                V.tensor_tensor(bcs, b, cos, ALU.mult)
                V.tensor_tensor(as_, a, sin, ALU.mult)
                dve.drain()
                V.tensor_tensor(a, ac, bs, ALU.subtract)
                V.tensor_tensor(b, bcs, as_, ALU.add)
            dve.drain()
            dve.sem_inc(self.roped, 1)
            dve.wait_ge(self.par, l * 32 + 32)
            pr = view(m3, 0, 2, HDA)
            V.tensor_tensor(pr, self.lam4[:, 0:4:2, :], self.lam4[:, 1:4:2, :], ALU.mult)
            dve.drain()
            V.tensor_reduce(st[:, 50:52], pr, AX.X, ALU.add).then_inc(self.lam_sum, 1)
            V.tensor_copy(st[:, 56:57], const("lam_init")[:, bass.ds(l, 1)])
            V.tensor_copy(st[:, 57:58], const("one_minus_lam")[:, bass.ds(l, 1)])
            dve.drain()
            V.tensor_scalar(self.subln, self.subln, st[:, 57:58], None, ALU.mult)
            dve.wait_ge(self.lam_exp, l + 1)
            V.tensor_tensor(st[:, 54:55], st[:, 53:54], st[:, 52:53], ALU.subtract)
            dve.drain()
            V.tensor_tensor(st[:, 55:56], st[:, 54:55], st[:, 56:57], ALU.subtract)
            mask = const("chunk_add")
            s0, s1 = ([sm[:, a:b].rearrange("p (m k) -> p m k", m=2) for sm in self.sm] for a, b in ((0, 256), (256, 768)))
            with dve.Fori(0, HA // 2) as i:
                n = l * HA + i * 2
                for e in range(2):
                    dve.wait_ge(self.turned, n * 2 + (2 * e + 5))
                    V.tensor_copy(self.kT[e], view_bank(2 * e + 1, 2, TOK)[0:HDA]).then_inc(self.kT_done, 1)
                for e in range(2):
                    dve.wait_ge(self.scored, n + (e + 1))
                    b0, b1 = view_bank(4 + 2 * e, 2, P), view_bank(5 + 2 * e, 2, TOK)
                    V.tensor_tensor(s0[e], b0, bc(mask.unsqueeze(1), [P, 2, P]), ALU.add)
                    V.tensor_copy(s1[e][:, :, 0:P], b1[:, :, 0:P])
                    V.tensor_tensor(s1[e][:, :, P:TOK], b1[:, :, P:TOK], bc(mask.unsqueeze(1), [P, 2, P]), ALU.add)
                    dve.drain()
                    V.tensor_reduce(self.hs[e][:, 0:2], s0[e], AX.X, ALU.max, negate=True)
                    V.tensor_reduce(self.hs[e][:, 2:4], s1[e], AX.X, ALU.max, negate=True).then_inc(self.masked, 1)
                for e in range(2):
                    hs, w = self.hs[e], self.w[e]
                    dve.wait_ge(self.exped, n + (e + 1))
                    V.reciprocal(hs[:, 8:12], hs[:, 4:8])
                    dve.drain()
                    V.tensor_scalar(hs[:, 12:16], hs[:, 8:12], st[:, 55:56], None, ALU.mult)
                    V.tensor_scalar(w[:, 0:P], s0[e][:, 0, :], hs[:, 8:9], None, ALU.mult)
                    V.tensor_scalar(w[:, P:3 * P], s1[e][:, 0, :], hs[:, 10:11], None, ALU.mult)
                    dve.drain()
                    V.scalar_tensor_tensor(out=w[:, 0:P], in0=s0[e][:, 1, :], scalar=hs[:, 13:14], in1=w[:, 0:P], op0=ALU.mult, op1=ALU.add)
                    V.scalar_tensor_tensor(out=w[:, P:3 * P], in0=s1[e][:, 1, :], scalar=hs[:, 15:16], in1=w[:, P:3 * P],
                                           op0=ALU.mult, op1=ALU.add).then_inc(self.mixed, 1)
                for e in range(2):
                    dve.wait_ge(self.out_done, n + (e + 3))
                    V.tensor_copy(br[:, :, bass.ds(i * (2 * P) + e * P, P)], view_bank(2 * e + 1, TT, P))
                    dve.drain()
                    V.tensor_tensor(self.sq[e], view_bank(2 * e + 1, TT, P), br[:, :, bass.ds(i * (2 * P) + e * P, P)], ALU.mult).then_inc(self.out_copied, 1)
                    dve.drain()
                    V.tensor_reduce(self.squares[:, bass.ds(i * 4 + 2 * e, 2)], self.sq[e], AX.X, ALU.add)
            dve.drain()
            V.tensor_scalar(st[:, 16:32], self.squares, 1.0 / P, LN_EPS, ALU.mult, ALU.add).then_inc(pow_asked, 1)
            dve.wait_ge(pow_done, power(l, 1))
            for h in range(HA):
                for t in range(TT):
                    head = br[:, t, h * P:(h + 1) * P]
                    ins = V.scalar_tensor_tensor(out=head, in0=head, scalar=st[:, 32 + 2 * h + t:33 + 2 * h + t], in1=self.subln, op0=ALU.mult, op1=ALU.mult)
            ins.then_inc(self.ready, 1)
            self.toT.dve(dve, l)

    gate_done, half_added = sem("branch_gate"), sem("branch_added")
    gate_par = sem("gate_par")
    gate_row = m1[0:1, 1024:2048]

    class Merge:

        def __init__(self, nth, q, r, after=None):
            self.nth, self.q, self.r = nth, q, r
            self.after = after
            self.gates = view(m1, 0, TT, 512)

        def blocks(self, l):
            return [Block(l, 0, self.q + j) for j in range(4)]

        def added(self, l, half):
            return l * 6 + (self.nth * 2 + half + 1)

        def sp(self, sp, l):
            w = A["w_branch"][bass.ds(l, 1), self.r].rearrange("z k n -> (z k) n")
            for j, b in enumerate(self.blocks(l)):
                if j % 2 == 0:
                    load_columns(sp, b, w, (j // 2) * 512)
                else:
                    load_columns(sp, b, w_mix(l), C_G + self.r * D + (j // 2) * 512)

        def load(self, pool, l):
            row = A["gate_bias"][bass.ds(l, 1), self.r, :]
            pool.dma_start(gate_row, row).then_inc(gate_par, 16)

        def pe(self, pe, l):
            for j, b in enumerate(self.blocks(l)):
                for t in range(TT):
                    bank = ps[:, 2 * j + t, :]
                    if j % 2 == 0:
                        products(pe, bank, brT, t, b).then_inc(blk, 1)
                    else:
                        if j == 1 and t == 0:
                            pe.wait_ge(gate_par, l * 48 + (self.nth + 1) * 16)
                            carry(pe)
                        pe.matmul(bank, const("ones", 1), gate_row[:, (j // 2) * 512:(j // 2 + 1) * 512], start=True, stop=False)
                        products(pe, bank, xT, t, b, start=False).then_inc(blk, 1)

        def act(self, act, l):
            blocks = self.blocks(l)
            for b in blocks:
                round_block(act, b)
            for c in range(2):
                if c == 1:
                    if self.after is not None:
                        round_block(act, Block(l, 0, self.after))
                    act.wait_ge(half_added, self.added(l, 0))
                for t in range(TT):
                    act.wait_ge(blk, blocks[2 * c + 1].done(t))
                    nc.scalar.activation(self.gates[:, t, :], ps[:, 4 * c + 2 + t, :], ACT.Sigmoid).then_inc(gate_done, 1)

        def dve(self, dve, l):
            blocks = self.blocks(l)
            for b in blocks:
                rest_of_block(dve, b)
            for c in range(2):
                if c == 1 and self.after is not None:
                    rest_of_block(dve, Block(l, 0, self.after))
                cols = slice(c * 512, (c + 1) * 512)
                for t in range(TT):
                    dve.wait_ge(blk, blocks[2 * c].done(t))
                    dve.wait_ge(gate_done, l * 12 + (self.nth * 4 + 2 * c + t + 1))
                    dst = merged[:, t, cols] if self.nth == 0 else self.gates[:, t, :]
                    ins = nc.vector.tensor_tensor(dst, self.gates[:, t, :], ps[:, 4 * c + t, :], ALU.mult)
                if self.nth:
                    dve.drain()
                    ins = nc.vector.tensor_tensor(merged[:, :, cols], merged[:, :, cols], self.gates, ALU.add)
                ins.then_inc(half_added, 1)

    qk_c = view(m1, 0, 16, TOK)
    v_c = view(m1, 4096, TT, D)
    proj_c = Project(Q_C, 6, [("feat", w_mix, C_QC + c * 512, 512, lambda part, c=c: qk_c[:, c * 4 + part * 2:c * 4 + part * 2 + 2, :])
                              for c in range(4)]
                     + [("tok", w_mix, C_VC + c * 512, 512, lambda part, c=c: v_c[:, part:part + 1, c * 512:(c + 1) * 512]) for c in range(2)])

    class StickBreaking:
        qk_staged, v_staged = sem("c_qk_staged"), sem("c_v_staged")
        scored, absed, logged = sem("c_scored"), sem("c_abs"), sem("c_log")
        stay, summed, shifted, weighed = sem("c_stay"), sem("c_summed"), sem("c_shifted"), sem("c_weighed")
        out_done, ready = sem("c_out"), sem("c_ready")
        qk = [view(m4, 768 * g, 2, TOK) for g in range(2)]
        v = [view(m4, 768 * g + 512, TT, P) for g in range(2)]
        diag = view(work, 9728, 2, ADA_COLS // P, P)
        z, ab, lg, sp_, a = ([view(work, 3840 * g + 768 * j, 2, 384) for g in range(2)] for j in range(5))
        toT = ToFeatures(br, brT, 2)

        def pool(self, pool, l):
            with pool.Fori(0, HC // 4) as i:
                n = l * (HC // 2) + i * 2
                for g in range(2):
                    pool.wait_ge(self.scored, n + (g + 1))
                    nc.gpsimd.tensor_copy(self.qk[g][:, 0:1, :], qk_c[:, bass.ds(i * 2 + g, 1), :])
                    nc.gpsimd.tensor_copy(self.qk[g][:, 1:2, :], qk_c[:, bass.ds(i * 2 + (g + 8), 1), :]).then_inc(self.qk_staged, 1)
                for g in range(2):
                    pool.wait_ge(self.out_done, n + (g + 1))
                    nc.gpsimd.tensor_copy(self.v[g], v_c[:, :, bass.ds(i * (2 * P) + g * P, P)]).then_inc(self.v_staged, 1)

        def pe(self, pe, l):
            with pe.Fori(0, HC // 4) as i:
                n = l * (HC // 2) + i * 2
                for g in range(2):
                    pe.wait_ge(self.qk_staged, n + (g + 1))
                    q, k = self.qk[g][:, 0, :], self.qk[g][:, 1, :]
                    for e in range(2):
                        rows, bank = slice(e * HDC, (e + 1) * HDC), ps[:, 4 * g + e, :]
                        pe.matmul(bank[:, 0:TOK], k[rows, 0:P], q[rows], start=True, stop=True)
                        ins = pe.matmul(bank[:, TOK:384], k[rows, P:TOK], q[rows, P:TOK], start=True, stop=True)
                    ins.then_inc(self.scored, 1)
                pieces.pe(pe, l, i, 0, 3)
                for g in range(2):
                    pe.wait_ge(self.stay, n + (g + 1))
                    for e in range(2):
                        bank = ps[:, 4 * g + e, :]
                        pe.matmul(bank[:, 0:384], const("from_"), self.sp_[g][:, e, :], start=True, stop=False)
                        ins = pe.matmul(bank[:, P:TOK], const("ones"), self.sp_[g][:, e, TOK:384], start=False, stop=True)
                    ins.then_inc(self.summed, 1)
                pieces.pe(pe, l, i, 1, 7)
                for g in range(2):
                    pe.wait_ge(self.v_staged, n + (g + 1))
                    pe.wait_ge(self.weighed, n + (g + 1))
                    for e in range(2):
                        cols = slice(e * HDC, (e + 1) * HDC)
                        a, v = self.a[g][:, e, :], self.v[g]
                        o0, o1 = ps[:, 4 * g + 2, e * HDC:(e + 1) * HDC], ps[:, 4 * g + 2, P + e * HDC:P + (e + 1) * HDC]
                        pe.matmul(o0, a[:, 0:P], v[:, 0, cols], start=True, stop=True)
                        pe.matmul(o1, a[:, P:TOK], v[:, 0, cols], start=True, stop=False)
                        ins = pe.matmul(o1, a[:, TOK:384], v[:, 1, cols], start=False, stop=True)
                    ins.then_inc(self.out_done, 1)
            pe.wait_ge(self.ready, l + 1)
            self.toT.pe(pe, l)

        def act(self, act, l):
            with act.Fori(0, HC // 4) as i:
                n = l * (HC // 2) + i * 2
                for g in range(2):
                    act.wait_ge(self.absed, n + (g + 1))
                    nc.scalar.activation(self.lg[g], self.ab[g], ACT.Exp, scale=-1.0)
                act.drain()
                for g in range(2):
                    nc.scalar.activation(self.lg[g], self.lg[g], ACT.Ln, bias=1.0).then_inc(self.logged, 1)
                for g in range(2):
                    act.wait_ge(self.shifted, n + (g + 1))
                    nc.scalar.activation(self.a[g], self.a[g], ACT.Exp).then_inc(self.weighed, 1)
                for g in range(2):
                    act.wait_ge(self.out_done, n + (g + 3))
                    nc.scalar.copy(br[:, :, bass.ds(i * (2 * P) + g * P, P)], view_bank(4 * g + 2, TT, P))
                pieces.act(act, 2)
            act.drain()
            act.sem_inc(self.ready, 1)
            self.toT.act(act, l)

        def dve(self, dve, l):
            V = nc.vector
            with dve.Fori(0, HC // 4) as i:
                n = l * (HC // 2) + i * 2
                for g in range(2):
                    z = self.z[g]
                    dve.wait_ge(self.scored, n + (g + 3))
                    V.scalar_tensor_tensor(out=z, in0=ps[:, 4 * g:4 * g + 2, 0:384], scalar=HDC ** -0.5,
                                           in1=bc(const("stick_add").unsqueeze(1), [P, 2, 384]), op0=ALU.mult, op1=ALU.add)
                    dve.drain()
                    V.scalar_tensor_tensor(out=self.ab[g], in0=z, scalar=-1.0, in1=z, op0=ALU.mult, op1=ALU.max).then_inc(self.absed, 1)
                for g in range(2):
                    dve.wait_ge(self.logged, n + (g + 1))
                    V.scalar_tensor_tensor(out=self.sp_[g], in0=self.z[g], scalar=0.0, in1=self.lg[g], op0=ALU.max, op1=ALU.add).then_inc(self.stay, 1)
                pieces.dve(dve, l, i, 0, 3, self.diag[:, 0])
                for g in range(2):
                    dve.wait_ge(self.summed, n + (g + 1))
                    V.tensor_tensor(self.a[g], self.z[g], ps[:, 4 * g:4 * g + 2, 0:384], ALU.subtract).then_inc(self.shifted, 1)
                pieces.dve(dve, l, i, 1, 7, self.diag[:, 1])
            self.toT.dve(dve, l)

    z_b = view(m1, 0, TT, D)
    xbc = view(m1, 2048, CT, TOK + CONV - 1)
    dt_raw = view(m1, 2048 + CT * (TOK + CONV - 1), TT, HB)
    proj_b = Project(Q_B, 12, [("tok", w_mix, C_Z + c * 512, 512, lambda part, c=c: z_b[:, part:part + 1, c * 512:(c + 1) * 512]) for c in range(2)]
                     + [("feat", w_mix, C_XBC + c * 512, 512, lambda part, c=c: xbc[:, c * 4 + part * 2:c * 4 + part * 2 + 2, CONV - 1:]) for c in range(3)]
                     + [("tok", w_mix, C_DT, HB, lambda part: dt_raw[:, part:part + 1, :])])

    CONV_GROUPS = 3

    class Convolve:
        first, added, done = sem("conv_first"), sem("conv_added"), sem("conv_done")

        def __init__(self, src, dst, taps, bias):
            self.src, self.dst, self.taps, self.bias = src, dst, taps, bias

        def tap(self, j, c):
            return self.taps[:, j * CT + c:j * CT + c + 1]

        def group(self, g):
            return range(g * CT // CONV_GROUPS, (g + 1) * CT // CONV_GROUPS)

        def act_first(self):
            for g in range(CONV_GROUPS):
                for c in self.group(g):
                    ins = nc.scalar.activation(self.dst[:, c, :], self.src[:, c, 0:TOK], ACT.Identity, scale=self.tap(0, c),
                                               bias=self.tap(CONV, c) if self.bias else 0.0)
                ins.then_inc(self.first, 1)

        def dve(self, dve, l):
            for g in range(CONV_GROUPS):
                dve.wait_ge(self.first, l * CONV_GROUPS + (g + 1))
                for j in range(1, CONV):
                    for c in self.group(g):
                        nc.vector.scalar_tensor_tensor(out=self.dst[:, c, :], in0=self.src[:, c, j:j + TOK], scalar=self.tap(j, c),
                                                       in1=self.dst[:, c, :], op0=ALU.mult, op1=ALU.add)
                    dve.drain()
                dve.sem_inc(self.added, 1)

        def act_silu(self, act, l):
            for g in range(CONV_GROUPS):
                act.wait_ge(self.added, l * CONV_GROUPS + (g + 1))
                cs = slice(self.group(g)[0], self.group(g)[-1] + 1)
                nc.scalar.activation(self.dst[:, cs, :], self.dst[:, cs, :], ACT.Silu).then_inc(self.done, 1)

    class Scan:
        par, pad, cw_turned, cw_done = sem("b_par"), sem("b_pad"), sem("b_cw_turned"), sem("b_cw")
        dt_abs, dt_log, decay_done = sem("b_dt_abs"), sem("b_dt_log"), sem("b_decay")
        cum, turned, xs_done, cb = sem("b_cum"), sem("b_turned"), sem("b_xs"), sem("b_cb")
        table_done, spread, seg = sem("b_table"), sem("b_spread"), sem("b_seg")
        exped, weighed, out_done = sem("b_exped"), sem("b_weighed"), sem("b_out")
        ready = sem("b_ready")
        QUADS = HB // 4
        norm_g = vecs[:, 0:D]
        dt_bias, a_log, d_skip = (vecs[:, D + HB * i:D + HB * (i + 1)] for i in range(3))
        cw = vecs[:, 1100:1100 + CT * (CONV + 1)]
        raw = m1[0:CT * (CONV + 1), 5800:5800 + P]
        conv = view(m2, 0, CT, TOK)
        convolve = Convolve(xbc, conv, cw, True)
        xs = view(m2, 3072, TT, D)
        cbm = view(m2, 5120, GB, 3 * P)
        xdt = view(m3, 0, TT, D)
        dtv = view(small, 0, TT, HB)
        tab = view(small, 64, 5, HB)
        st = small[:, 144:208]
        sums = view(small, 208, TT, GB, 2)
        sq = view(m1, 2048, TT, 256)
        diag = view(m1, 5200, 2, ADA_COLS // P, P)
        e, w = ([view(at[0], at[1] + 1536 * n, 3, 4, P) for at in ((m4, 0), (work, 0))] for n in range(2))
        toT = ToFeatures(br, brT, 3)

        def load(self, pool, l):
            pool.dma_start(self.norm_g, A["ssm_norm_g"][bass.ds(l, 1), :].partition_broadcast(P)).then_inc(self.par, 16)
            for dst, name in ((self.dt_bias, "ssm_dt_bias"), (self.a_log, "ssm_A_log"), (self.d_skip, "ssm_D")):
                pool.dma_start(dst, A[name][bass.ds(l, 1), :].partition_broadcast(P)).then_inc(self.par, 16)
            taps = CT * CONV
            pool.dma_start(self.raw[0:taps], layer_of(A["ssm_conv_w"], l).rearrange("j (c p) -> (j c) p", p=P)).then_inc(self.par, 16)
            pool.dma_start(self.raw[taps:taps + CT], A["ssm_conv_b"][bass.ds(l, 1), :].rearrange("z (c p) -> (z c) p", p=P)).then_inc(self.par, 16)
            nc.gpsimd.memset(xbc[:, :, 0:CONV - 1], 0.0)

        def pool(self, pool, l):
            pool.wait_ge(pow_asked, power(l, 2))
            nc.gpsimd.tensor_tensor(self.st[:, 8:12], self.st[:, 4:8], const("minus_half")[:, 0:4], ALU.pow).then_inc(pow_done, 1)

        def pe(self, pe, l):
            n_par = CT * (CONV + 1)
            pe.wait_ge(self.par, l * 96 + 96)
            carry(pe)
            pe.transpose(ps[:, 7, 0:n_par], self.raw, ident[0:n_par, 0:n_par]).then_inc(self.cw_turned, 1)
            for c in range(2):
                pieces.pe(pe, l, 0, ADA_C + c, 4 + c)
            pe.wait_ge(self.decay_done, l + 1)
            d = self.tab[:, 0:2, :].rearrange("p t h -> p (t h)")
            pe.matmul(ps[:, 6, 0:2 * HB], const("upto"), d, start=True, stop=True)
            pe.matmul(ps[:, 6, 2 * HB:3 * HB], const("ones"), self.tab[:, 0, :], start=True, stop=True).then_inc(self.cum, 1)
            for t in range(TT):
                for c in range(8):
                    if t == 0 and c % 4 == 0:
                        pe.wait_ge(self.convolve.done, l * CONV_GROUPS + (c // 4 + 1))
                    ins = pe.transpose(ps[:, 2 * t + c // 4, (c % 4) * P:(c % 4 + 1) * P], self.conv[:, c, t * P:(t + 1) * P], ident)
                ins.then_inc(self.turned, 1)
            pe.wait_ge(self.convolve.done, l * CONV_GROUPS + CONV_GROUPS)
            pe.wait_ge(pieces.used, l * ADA_LAYER + (ADA_C + 4))
            for g in range(GB):
                b_, c_ = self.conv[:, 8 + g, :], self.conv[:, 10 + g, :]
                pe.matmul(ps[:, 4 + g, 0:TOK], b_[:, 0:P], c_, start=True, stop=True)
                ins = pe.matmul(ps[:, 4 + g, TOK:384], b_[:, P:TOK], c_[:, P:TOK], start=True, stop=True)
            ins.then_inc(self.cb, 1)
            pe.wait_ge(self.table_done, l + 1)
            carry(pe)

            def spread(q):
                for t in range(TT):
                    for h in range(4):
                        ins = pe.matmul(ps[:, 3 * (q % 2) + t, h * P:(h + 1) * P], self.tab[:, t, 4 * q + h:4 * q + h + 1].to_broadcast([P, P]), const("upto"),
                                        start=True, stop=True)
                ins.then_inc(self.spread, 1)

            def outputs(q):
                pe.wait_ge(self.weighed, l * self.QUADS + (q + 1))
                w = self.w[q % 2]
                for h in range(4):
                    cols = slice((4 * q + h) * PB, (4 * q + h + 1) * PB)
                    o0, o1 = (ps[:, 3 * (q % 2) + 2, 256 * t + h * PB:256 * t + (h + 1) * PB] for t in range(TT))
                    pe.matmul(o0, w[:, 0, h, :], self.xdt[:, 0, cols], start=True, stop=True)
                    pe.matmul(o1, w[:, 1, h, :], self.xdt[:, 0, cols], start=True, stop=False)
                    ins = pe.matmul(o1, w[:, 2, h, :], self.xdt[:, 1, cols], start=False, stop=True)
                ins.then_inc(self.out_done, 1)
            spread(0)
            spread(1)
            for q in range(self.QUADS):
                if q + 2 < self.QUADS:
                    pe.wait_ge(self.seg, l * self.QUADS + (q + 1))
                    spread(q + 2)
                if q < 2:
                    pieces.pe(pe, l, 0, ADA_C + 2 + q, 6 + q)
                outputs(q)
            pe.wait_ge(self.ready, l + 1)
            self.toT.pe(pe, l)

        def act(self, act, l):
            act.wait_ge(self.cw_turned, l + 1)
            nc.scalar.copy(self.cw, ps[:, 7, 0:CT * (CONV + 1)]).then_inc(self.cw_done, 1)
            act.drain()
            self.convolve.act_first()
            act.wait_ge(self.dt_abs, l + 1)
            nc.scalar.activation(self.st[:, 0:32], self.st[:, 0:32], ACT.Exp, scale=-1.0)
            nc.scalar.activation(self.a_log, self.a_log, ACT.Exp)
            act.drain()
            nc.scalar.activation(self.st[:, 0:32], self.st[:, 0:32], ACT.Ln, bias=1.0).then_inc(self.dt_log, 1)
            nc.scalar.activation(z_b, z_b, ACT.Silu)
            self.convolve.act_silu(act, l)
            act.wait_ge(self.turned, l * 2 + 1)
            nc.scalar.copy(self.xs[:, 0, :], ps[:, 0:2, :].rearrange("p a b -> p (a b)"))
            act.wait_ge(self.turned, l * 2 + 2)
            nc.scalar.copy(self.xs[:, 1, :], ps[:, 2:4, :].rearrange("p a b -> p (a b)")).then_inc(self.xs_done, 1)
            for q in range(self.QUADS):
                act.wait_ge(self.seg, l * self.QUADS + (q + 1))
                nc.scalar.activation(self.e[q % 2], self.e[q % 2], ACT.Exp).then_inc(self.exped, 1)
            pieces.act(act, ADA_B)
            self.toT.act(act, l)

        def dve(self, dve, l):
            V = nc.vector
            dve.wait_ge(self.par, l * 96 + 96)
            V.tensor_tensor(self.dtv, dt_raw, bc(self.dt_bias.unsqueeze(1), [P, TT, HB]), ALU.add)
            dve.drain()
            sp_ = view(self.st, 0, TT, HB)
            V.scalar_tensor_tensor(out=sp_, in0=self.dtv, scalar=-1.0, in1=self.dtv, op0=ALU.mult, op1=ALU.max).then_inc(self.dt_abs, 1)
            dve.wait_ge(self.cw_done, l + 1)
            carry(dve)
            self.convolve.dve(dve, l)
            dve.wait_ge(self.dt_log, l + 1)
            V.scalar_tensor_tensor(out=self.dtv, in0=self.dtv, scalar=0.0, in1=sp_, op0=ALU.max, op1=ALU.add)
            dve.drain()
            V.scalar_tensor_tensor(out=self.tab[:, 0:2, :], in0=self.dtv, scalar=-1.0, in1=bc(self.a_log.unsqueeze(1), [P, TT, HB]),
                                   op0=ALU.mult, op1=ALU.mult).then_inc(self.decay_done, 1)
            dve.wait_ge(self.cum, l + 1)
            V.tensor_copy(self.tab[:, 2:4, :], view_bank(6, 3, HB)[:, 0:2, :])
            dve.drain()
            V.tensor_tensor(self.tab[:, 4, :], self.tab[:, 2, :], view_bank(6, 3, HB)[:, 2, :], ALU.subtract)
            for c in range(2):
                pieces.dve(dve, l, 0, ADA_C + c, 4 + c, self.diag[:, c])
            dve.wait_ge(self.xs_done, l + 1)
            for t in range(TT):
                V.tensor_tensor(self.xdt[:, t, :].rearrange("p (h d) -> p h d", d=PB), self.xs[:, t, :].rearrange("p (h d) -> p h d", d=PB),
                                bc(self.dtv[:, t, :].unsqueeze(2), [P, HB, PB]), ALU.mult)
            dve.wait_ge(self.cb, l + 1)
            for g in range(GB):
                c3 = view_bank(4 + g, 3, P)
                o3 = self.cbm[:, g, :].rearrange("p (b n) -> p b n", b=3)
                V.tensor_tensor(o3[:, 0:3:2, :], c3[:, 0:3:2, :], bc(const("upto").unsqueeze(1), [P, 2, P]), ALU.mult)
                V.tensor_copy(o3[:, 1, :], c3[:, 1, :])
            dve.drain()
            dve.sem_inc(self.table_done, 1)

            def exponents(q):
                dve.wait_ge(self.spread, l * self.QUADS + (q + 1))
                for h in range(4):
                    cols = slice(h * P, (h + 1) * P)
                    for b, (t, f) in enumerate(((0, 2), (1, 4), (1, 3))):
                        ins = V.tensor_scalar(self.e[q % 2][:, b, h, :], ps[:, 3 * (q % 2) + t, cols], self.tab[:, f, 4 * q + h:4 * q + h + 1], 0.0, ALU.subtract, ALU.min)
                ins.then_inc(self.seg, 1)

            def weights(q):
                dve.wait_ge(self.exped, l * self.QUADS + (q + 1))
                c_b = self.cbm[:, q // 2, :].rearrange("p (b n) -> p b n", b=3)
                V.tensor_tensor(self.w[q % 2], self.e[q % 2], bc(c_b.unsqueeze(2), [P, 3, 4, P]), ALU.mult).then_inc(self.weighed, 1)

            def finish(q):
                dve.wait_ge(self.out_done, l * self.QUADS + (q + 1))
                cols = slice(q * 256, (q + 1) * 256)
                V.tensor_tensor(br[:, :, cols], view_bank(3 * (q % 2) + 2, TT, 256), self.xs[:, :, cols], ALU.add)
                dve.drain()
                V.tensor_tensor(br[:, :, cols], br[:, :, cols], z_b[:, :, cols], ALU.mult)
                dve.drain()
                V.tensor_tensor(self.sq, br[:, :, cols], br[:, :, cols], ALU.mult)
                dve.drain()
                V.tensor_reduce(self.sums[:, :, q // 2, q % 2], self.sq, AX.X, ALU.add)
            exponents(0)
            exponents(1)
            for t in range(TT):
                heads = self.xs[:, t, :].rearrange("p (h d) -> p h d", d=PB)
                V.tensor_tensor(heads, heads, bc(self.d_skip.unsqueeze(2), [P, HB, PB]), ALU.mult)
            for q in range(self.QUADS):
                weights(q)
                dve.drain()
                if q + 2 < self.QUADS:
                    exponents(q + 2)
                if q < 2:
                    pieces.dve(dve, l, 0, ADA_C + 2 + q, 6 + q, self.diag[:, q])
                if q:
                    finish(q - 1)
            finish(self.QUADS - 1)
            dve.drain()
            V.tensor_reduce(self.st[:, 0:4], self.sums.rearrange("p t g k -> p (t g) k"), AX.X, ALU.add)
            dve.drain()
            V.tensor_scalar(self.st[:, 4:8], self.st[:, 0:4], float(GB) / D, LN_EPS, ALU.mult, ALU.add).then_inc(pow_asked, 1)
            dve.wait_ge(pow_done, power(l, 2))
            for t in range(TT):
                for g in range(GB):
                    part = slice(g * D // GB, (g + 1) * D // GB)
                    ins = V.scalar_tensor_tensor(out=br[:, t, part], in0=br[:, t, part], scalar=self.st[:, 8 + t * GB + g:9 + t * GB + g],
                                                 in1=self.norm_g[:, part], op0=ALU.mult, op1=ALU.mult)
            ins.then_inc(self.ready, 1)
            self.toT.dve(dve, l)

    class OutProduct:

        def __init__(self, q, w):
            self.q, self.w = q, w

        def await_sum(self, eng, l, t):
            eng.wait_ge(blk, Block(l, 0, self.q + 1).done(t))

        def sp(self, sp, l):
            for c in range(2):
                load_columns(sp, Block(l, 0, self.q + c), self.w(l), c * 512)

        def pe(self, pe, l):
            for c in range(2):
                for t in range(TT):
                    products(pe, ps[:, 2 * t + c, :], brT, t, Block(l, 0, self.q + c)).then_inc(blk, 1)

        def act(self, act, l):
            for c in range(2):
                round_block(act, Block(l, 0, self.q + c))

        def dve(self, dve, l):
            for c in range(2):
                rest_of_block(dve, Block(l, 0, self.q + c))

    class TurnMerged:
        toT = ToFeatures(merged, brT, 4)

        def pe(self, pe, l):
            self.toT.pe(pe, l, lambda kp: pe.wait_ge(half_added, merge_b.added(l, kp // 2)))

        def act(self, act, l):
            self.toT.act(act, l)

        def dve(self, dve, l):
            self.toT.dve(dve, l)

    def ffn(q, d, w_in, w_out):
        def gate_up(l, u):
            v = layer_of(A[w_in], l).rearrange("(k p) n -> p k n", p=P)
            return v[:, :, bass.ds(u * UF, UF)], v[:, :, bass.ds(u * UF + FF, UF)]

        def down_rows(l, u):
            return layer_of(A[w_out], l)[bass.ds(u * UF, UF), :].rearrange("(k p) n -> p k n", p=P)
        return Gated(UNITS, q, d, gate_up, down_rows)

    ffn1 = ffn(Q_FFN1, 0, "ffn1_w_in", "ffn1_w_out")
    ffn2 = ffn(Q_FFN2, UNITS, "ffn2_w_in", "ffn2_w_out")
    out_product = OutProduct(Q_MO, lambda l: layer_of(A["w_mix_out"], l))
    norm1 = Norm(0, 0, 0, ffn1, FFN_RES, A["ln1_g"], A["ln1_b"])
    norm2 = Norm(1, 3, 5, out_product, 1.0, A["ln2_g"], A["ln2_b"])
    norm3 = Norm(2, 4, 6, ffn2, FFN_RES, A["ln3_g"], A["ln3_b"])
    diff, stick, scan = DiffAttention(), StickBreaking(), Scan()
    merge_a, merge_c, merge_b = Merge(0, Q_OA, 0, Q_C), Merge(1, Q_OC, 2, Q_B), Merge(2, Q_OB, 1)
    proj_c.merge, proj_b.merge = merge_a, merge_c
    turn_x = ToFeatures(x, xT, -1)
    turn_merged = TurnMerged()

    LAYER = [(ffn1, norm1, proj_a), (diff,), (merge_a, proj_c), (stick,), (merge_c, proj_b), (scan,),
             (merge_b, turn_merged, out_product, norm2, ffn2, norm3)]
    PHASES = len(LAYER)

    L2 = LAYERS
    a_log2, dt_bias2 = vecs[:, 136:144], vecs[:, 144:152]
    out_norm2, q_norm2, k_norm2 = (vecs[:, 152 + HD2 * i:152 + HD2 * (i + 1)] for i in range(3))
    sinks2 = vecs[:, 344:352]
    router_w = view(vecs, 352, KT, ROUTE)
    router_b = vecs[:, 640:676]
    cw2 = vecs[:, 676:676 + CT * CONV]
    trig = view(vecs, 724, 2, TT, HD2 // 2)
    pos_i = ctx.enter_context(nc.sbuf_tensor("pos_i", [P, TT], I32))
    pos_f = vecs[:, 852:854]
    cols_par = sem("cols_par")
    gates2 = ln_par

    def load_second(pool):
        for dst, name in ((a_log2, "a_log_2"), (dt_bias2, "dt_bias_2"), (out_norm2, "gdn_out_norm_2"), (q_norm2, "q_norm_2"),
                          (k_norm2, "k_norm_2"), (sinks2, "sinks_2"), (router_b[:, 0:GROUPS], "b_group_2"), (router_b[:, GROUPS:], "b_router_2")):
            pool.dma_start(dst, A[name].partition_broadcast(P)).then_inc(cols_par, 16)
        for dst, name in ((router_w[:, :, 0:GROUPS], "w_group_2"), (router_w[:, :, GROUPS:], "w_router_2")):
            pool.dma_start(dst, A[name].rearrange("z (k p) n -> p (z k) n", p=P)).then_inc(cols_par, 16)
        for t in range(TT):
            pool.dma_start(pos_i[:, t:t + 1], A["positions_2"][:, t * P:(t + 1) * P].rearrange("b p -> p b")).then_inc(cols_par, 16)
    COLS_PAR = 16 * 12

    class Modulation:
        done, spread = sem("mod_done"), sem("mod_spread")

        def pe(self, pe, l):
            pe.wait_ge(self.done, 1)
            for g in range(2):
                for k in range(KT):
                    ins = pe.matmul(ps[:, 2 * g + k // 4, (k % 4) * P:(k % 4 + 1) * P], mod[:, 2 + 3 * g, k:k + 1].to_broadcast([P, P]), ident,
                                    start=True, stop=True)
            ins.then_inc(self.spread, 1)

        def act(self, act, l):
            act.wait_ge(self.spread, 1)
            for g in range(2):
                nc.scalar.copy(gates2[:, g, :], ps[:, 2 * g:2 * g + 2, :].rearrange("p a b -> p (a b)"))

        def dve(self, dve, l):
            V = nc.vector
            V.tensor_tensor(mod_flat, mod_flat, cols2[:, KT:7 * KT], ALU.add)
            dve.drain()
            dve.sem_inc(self.done, 1)
            for g in range(2):
                V.scalar_tensor_tensor(out=scales[:, g, :], in0=mod[:, 1 + 3 * g, :], scalar=1.0, in1=cols2[:, (7 + g) * KT:(8 + g) * KT],
                                       op0=ALU.add, op1=ALU.mult)

    class Modulate:

        added, squared, normed = sem("mod_added"), sem("mod_squared"), sem("mod_normed")
        h = view(m2, 0, KT, TOK)

        def __init__(self, g, power, turn):
            self.g, self.power, self.turn = g, power, turn

        def add_gated(self, dve, gate):
            for t in range(TT):
                acc = ps[:, 2 * t:2 * t + 2, :].rearrange("p a b -> p (a b)")
                nc.vector.tensor_tensor(merged[:, t, :], gates2[:, gate, :], acc, ALU.mult)
            dve.drain()
            nc.vector.tensor_tensor(x[:], x[:], merged[:], ALU.add)
            dve.drain()

        def dve(self, dve, l):
            V = nc.vector
            if self.g:
                self.add_gated(dve, 0)
            if self.g:
                dve.sem_inc(self.added, 1)
            dve.wait_ge(self.squared, self.g + 1)
            V.tensor_scalar(small[:, 2:4], small[:, 0:2], 1.0 / D, RMS_EPS, ALU.mult, ALU.add).then_inc(pow_asked, 1)
            dve.wait_ge(pow_done, power(L2, self.power))
            for q in range(4):
                c = slice(q * D // 4, (q + 1) * D // 4)
                for t in range(TT):
                    ins = V.tensor_scalar(merged[:, t, c], x[:, t, c], small[:, 4 + t:5 + t], None, ALU.mult)
                ins.then_inc(self.normed, 1)
            for kp in range(4):
                k = slice(2 * kp, 2 * kp + 2)
                dve.wait_ge(feat_rounded, turn(L2, self.turn, kp))
                V.tensor_copy(xT[0][:, k, :], self.h[:, k, :])
                dve.drain()
                V.tensor_tensor(xT[1][:, k, :], self.h[:, k, :], xT[0][:, k, :], ALU.subtract)

        def pool(self, pool, l):
            pool.wait_ge(pow_asked, power(L2, self.power))
            nc.gpsimd.tensor_tensor(small[:, 4:6], small[:, 2:4], const("minus_half")[:, 0:2], ALU.pow).then_inc(pow_done, 1)

        def pe(self, pe, l):
            for kp in range(4):
                pe.wait_ge(self.normed, self.g * 4 + kp + 1)
                for kk in range(2):
                    for t in range(TT):
                        k, at = 2 * kp + kk, kk * TOK + t * P
                        ins = pe.transpose(ps[:, kp, at:at + P], merged[:, t, k * P:(k + 1) * P], ident)
                ins.then_inc(feat_turned, 1)

        def act(self, act, l):
            if self.g:
                act.wait_ge(self.added, 1)
            for t in range(TT):
                ins = nc.scalar.activation(self.h.rearrange("p k n -> p (k n)")[:, t * D:(t + 1) * D], x[:, t, :], ACT.Square, accum_out=small[:, t:t + 1])
            ins.then_inc(self.squared, 1)
            for k in range(KT):
                act.wait_ge(feat_turned, turn(L2, self.turn, k // 2))
                ins = nc.scalar.activation(self.h[:, k, :], ps[:, k // 2, (k % 2) * TOK:(k % 2 + 1) * TOK], ACT.Identity,
                                           bias=mod[:, 3 * self.g, k:k + 1], scale=scales[:, self.g, k:k + 1])
                if k % 2:
                    ins.then_inc(feat_rounded, 1)

    z_2 = view(m1, 0, TT, G2W)
    q_s = view(m1, 1024, TT, G2W)
    ab_2 = view(m1, 2048 + CT * (TOK + CONV - 1), TT, 2 * H2)
    kv_s = view(m1, 5200, TT, 2 * KV2 * HD2)
    w_2 = lambda l: A["w_in_2"].rearrange("z k n -> (z k) n")
    proj_2 = Project(Q_P2, 0, [("feat", w_2, W2["qkv"] + c * 512, 512, lambda part, c=c: xbc[:, c * 4 + part * 2:c * 4 + part * 2 + 2, CONV - 1:])
                               for c in range(3)]
                     + [("tok", w_2, W2["z"], 512, lambda part: z_2[:, part:part + 1, :]),
                        ("tok", w_2, W2["ab"], 2 * H2, lambda part: ab_2[:, part:part + 1, :]),
                        ("tok", w_2, W2["sq"], 512, lambda part: q_s[:, part:part + 1, :]),
                        ("tok", w_2, W2["skv"], 256, lambda part: kv_s[:, part:part + 1, :])])

    class DeltaRule:
        par, cw_turned, cw_done = sem("g_par"), sem("g_cw_turned"), sem("g_cw")
        turned, tok_done = sem("g_turned"), sem("g_tok")
        ab_abs, ab_log, decay, cum, cums, exps = (sem(f"g_{n}") for n in ("ab_abs", "ab_log", "decay", "cum", "cums", "exps"))
        unit, scaled, scaled2, split, splitT = (sem(f"g_{n}") for n in ("unit", "scaled", "scaled2", "split", "splitT"))
        gram, seg, dec, mats = sem("g_gram"), sem("g_seg"), sem("g_dec"), sem("g_mats")
        level, lt, upd = sem("g_level"), sem("g_lt"), sem("g_upd")
        lt0_done, lt1_done = sem("g_lt0_done"), sem("g_lt1_done")
        u0, u0_done, wT_done, state, state_done = (sem(f"g_{n}") for n in ("u0", "u0_done", "wT_done", "state", "state_done"))
        vnew, vnew_done, out_done = sem("g_vnew"), sem("g_vnew_done"), sem("g_out")
        copied = sem("g_copied")
        raw = m1[0:CT * CONV, 5800:5800 + P]
        conv = view(work, 0, CT, TOK)
        convolve = Convolve(xbc, conv, cw2, False)
        tok = view(work, 3072, TT, 3 * G2W)
        q_, k_, v_ = tok[:, :, 0:G2W], tok[:, :, G2W:2 * G2W], tok[:, :, 2 * G2W:]
        vb, kd, kg = (view(m1, 2048 + 1024 * n, TT, G2W) for n in range(3))
        kb, qg = (view(work, 1024 * n, TT, G2W) for n in range(2))
        kT, kbT, qT = ([view(work, 6144 + 3072 * e + 1024 * n, 8, P)[0:HD2] for e in range(2)] for n in range(3))
        e, mT, aT = ([view(work, 2048 * n + 1024 * e, 8, P) for e in range(2)] for n in range(3))
        LT = e
        LmT = [view(work, 6144 + 1024 * e, 8, P) for e in range(2)]
        T = [merged[:, e, :].rearrange("p (s n) -> p s n", n=P) for e in range(2)]
        Tt = [view(xT_work, D * e, 8, P) for e in range(2)]
        st, stn = ([view(work, 8192 + 512 * e + 256 * n, 4, HD2)[0:HD2] for e in range(2)] for n in range(2))
        vn = [view(scratch, 512 * e, 8, HD2) for e in range(2)]
        wT = [view(scratch, 1024 + 512 * e, 4, P)[0:HD2] for e in range(2)]
        qgT = [view(work, 15360 + 512 * e, 4, P)[0:HD2] for e in range(2)]
        tab = view(small, 0, 6, TT, H2)
        sp_ = view(small, 96, TT, H2)
        ss, rs_ = small[:, 112:144], small[:, 144:176]
        gend = view(small, 176, TT, H2)
        anu = small[:, 192:200]

        def multiples(self, eng, which):
            for dst, src, f in which:
                for t in range(TT):
                    heads = [ap[:, t, :].rearrange("p (h d) -> p h d", d=HD2) for ap in (dst, src)]
                    eng.tensor_tensor(heads[0], heads[1], bc(self.tab[:, f, t, :].unsqueeze(2), [P, H2, HD2]), ALU.mult)

        def load(self, pool, l):
            pool.dma_start(self.raw, A["conv_w_2"].rearrange("z j (c p) -> (z j c) p", p=P)).then_inc(self.par, 16)
            nc.gpsimd.memset(xbc[:, :, 0:CONV - 1], 0.0)

        def pool(self, pool, l):
            pool.wait_ge(pow_asked, power(L2, 1))
            nc.gpsimd.tensor_tensor(self.rs_, self.ss, const("minus_half")[:, 0:32], ALU.pow).then_inc(pow_done, 1)
            pool.wait_ge(self.unit, 1)
            self.multiples(nc.gpsimd, ((self.vb, self.v_, 2), (self.kg, self.k_, 4), (self.kd, self.k_, 5)))
            pool.drain()
            pool.sem_inc(self.scaled2, 1)
            pool.wait_ge(pow_asked, power(L2, 2))
            nc.gpsimd.tensor_tensor(self.rs_[:, 0:16], self.ss[:, 0:16], const("minus_half")[:, 0:16], ALU.pow).then_inc(pow_done, 1)

        def pe(self, pe, l):
            n_par = CT * CONV
            pe.wait_ge(self.par, 16)
            pe.transpose(ps[:, 7, 0:n_par], self.raw, ident[0:n_par, 0:n_par]).then_inc(self.cw_turned, 1)
            pe.wait_ge(self.decay, 1)
            g2 = self.tab[:, 0].rearrange("p t h -> p (t h)")
            pe.matmul(ps[:, 6, 0:16], const("upto"), g2, start=True, stop=True)
            pe.matmul(ps[:, 6, 16:32], const("ones"), g2, start=True, stop=True).then_inc(self.cum, 1)
            for t in range(TT):
                for c in range(CT):
                    if t == 0 and c % 4 == 0:
                        pe.wait_ge(self.convolve.done, L2 * CONV_GROUPS + c // 4 + 1)
                    ins = pe.transpose(ps[:, 3 * t + c // 4, (c % 4) * P:(c % 4 + 1) * P], self.conv[:, c, t * P:(t + 1) * P], ident)
                ins.then_inc(self.turned, 1)
            head = lambda ap, t, e, h: ap[:, t, (4 * e + h) * HD2:(4 * e + h + 1) * HD2]
            heads = [(t, h) for t in range(TT) for h in range(4)]
            for e in range(2):
                pe.wait_ge(self.scaled, 1)
                if e:
                    pe.wait_ge(self.splitT, 2)
                for n, src in enumerate((self.k_, self.kb, self.q_)):
                    for t, h in heads:
                        pe.transpose(ps[0:HD2, 2 * n + t, h * P:(h + 1) * P], head(src, t, e, h), ident)
                for h in range(4):
                    ins = pe.transpose(ps[0:HD2, 6, h * P:(h + 1) * P], head(self.qg, 1, e, h), ident)
                ins.then_inc(self.split, 1)
            for e in range(2):
                pe.wait_ge(self.splitT, 4)
                if e:
                    pe.wait_ge(self.mats, 1)
                for t, h in heads:
                    s, cols = 4 * t + h, slice(h * P, (h + 1) * P)
                    pe.matmul(ps[:, t, cols], self.tab[:, 0, t, 4 * e + h:4 * e + h + 1].to_broadcast([P, P]), const("upto"), start=True, stop=True)
                    pe.matmul(ps[:, 2 + t, cols], self.kT[e][:, s, :], self.kbT[e][:, s, :], start=True, stop=True)
                    ins = pe.matmul(ps[:, 4 + t, cols], self.kT[e][:, s, :], self.qT[e][:, s, :], start=True, stop=True)
                ins.then_inc(self.gram, 1)
            pe.wait_ge(self.mats, 2)
            carry(pe)

            def l_times_t(e, stat):
                for t, h in heads:
                    s = 4 * t + h
                    ins = pe.matmul(ps[:, 4 * e + t, h * P:(h + 1) * P], self.LmT[e][:, s, :], stat(s), start=True, stop=True)
                ins.then_inc(self.lt, 1)

            def update(e, both):
                for t, h in heads:
                    s, cols = 4 * t + h, slice(h * P, (h + 1) * P)
                    if both:
                        pe.matmul(ps[:, 4 * e + 2 + t, cols], self.Tt[e][:, s, :], self.LT[e][:, s, :], start=True, stop=True)
                    ins = pe.matmul(ps[:, 4 * e + t, cols], self.LT[e][:, s, :], self.Tt[e][:, s, :], start=True, stop=True)
                ins.then_inc(self.upd, 1)
            for e in range(2):
                pe.wait_ge(self.level, e + 1)
                l_times_t(e, lambda s: ident)
            with pe.Fori(0, LEVELS - 2) as v:
                for e in range(2):
                    pe.wait_ge(self.level, v * 2 + (e + 3))
                    l_times_t(e, lambda s: self.T[e][:, s, :])
                for e in range(2):
                    pe.wait_ge(self.lt0_done, v * 2 + (e + 1))
                    pe.wait_ge(self.lt1_done, v * 2 + (e + 1))
                    update(e, True)
            for e in range(2):
                pe.wait_ge(self.level, LEVELS * 2 + e - 1)
                l_times_t(e, lambda s: self.T[e][:, s, :])
            for e in range(2):
                pe.wait_ge(self.lt0_done, LEVELS * 2 + e - 3)
                pe.wait_ge(self.lt1_done, LEVELS * 2 + e - 3)
                update(e, False)
            cols = lambda h: slice(h * HD2, (h + 1) * HD2)
            for e in range(2):
                pe.wait_ge(self.level, LEVELS * 2 + e + 1)
                pe.wait_ge(self.scaled2, 1)
                for h in range(4):
                    pe.matmul(ps[:, 4 * e, cols(h)], self.Tt[e][:, h, :], head(self.vb, 0, e, h), start=True, stop=True)
                    ins = pe.matmul(ps[0:HD2, 4 * e + 1, h * P:(h + 1) * P], head(self.kg, 1, e, h), self.Tt[e][:, 4 + h, :], start=True, stop=True)
                ins.then_inc(self.u0, 1)
            for e in range(2):
                pe.wait_ge(self.u0_done, e + 1)
                for h in range(4):
                    ins = pe.matmul(ps[0:HD2, 4 * e + 2, cols(h)], head(self.kd, 0, e, h), self.vn[e][:, h, :], start=True, stop=True)
                ins.then_inc(self.state, 1)
            for e in range(2):
                pe.wait_ge(self.wT_done, e + 1)
                pe.wait_ge(self.state_done, e + 1)
                for h in range(4):
                    o = ps[:, 4 * e + 3, cols(h)]
                    pe.matmul(o, self.Tt[e][:, 4 + h, :], head(self.vb, 1, e, h), start=True, stop=False)
                    ins = pe.matmul(o, self.wT[e][:, h, :], self.stn[e][:, h, :], start=False, stop=True)
                ins.then_inc(self.vnew, 1)
            for e in range(2):
                pe.wait_ge(self.vnew_done, e + 1)
                for h in range(4):
                    pe.matmul(ps[:, 4 * e, cols(h)], self.aT[e][:, h, :], self.vn[e][:, h, :], start=True, stop=True)
                    o = ps[:, 4 * e, cols(4 + h)]
                    pe.matmul(o, self.qgT[e][:, h, :], self.st[e][:, h, :], start=True, stop=False)
                    ins = pe.matmul(o, self.aT[e][:, 4 + h, :], self.vn[e][:, 4 + h, :], start=False, stop=True)
                ins.then_inc(self.out_done, 1)

        def act(self, act, l):
            act.wait_ge(self.cw_turned, 1)
            nc.scalar.copy(cw2, ps[:, 7, 0:CT * CONV]).then_inc(self.cw_done, 1)
            act.drain()
            self.convolve.act_first()
            act.wait_ge(self.ab_abs, 1)
            nc.scalar.activation(self.sp_, self.sp_, ACT.Exp, scale=-1.0)
            nc.scalar.activation(self.anu, a_log2, ACT.Exp)
            act.drain()
            nc.scalar.activation(self.sp_, self.sp_, ACT.Ln, bias=1.0).then_inc(self.ab_log, 1)
            nc.scalar.activation(self.tab[:, 2], ab_2[:, :, H2:2 * H2], ACT.Sigmoid)
            nc.scalar.activation(z_2, z_2, ACT.Silu)
            self.convolve.act_silu(act, L2)
            for t in range(TT):
                act.wait_ge(self.turned, t + 1)
                ins = nc.scalar.copy(self.tok[:, t, :], ps[:, 3 * t:3 * t + 3, :].rearrange("p a b -> p (a b)"))
            ins.then_inc(self.tok_done, 1)
            act.wait_ge(self.cums, 1)
            nc.scalar.activation(self.tab[:, 3], self.tab[:, 1], ACT.Exp)
            nc.scalar.activation(self.tab[:, 5], self.gend, ACT.Exp).then_inc(self.exps, 1)
            for e in range(2):
                act.wait_ge(self.split, e + 1)
                nc.scalar.copy(self.kT[e], ps[0:HD2, 0:2, :].rearrange("p a (h n) -> p (a h) n", n=P))
                nc.scalar.copy(self.qgT[e], view_bank(6, 4, P)[0:HD2]).then_inc(self.splitT, 1)
            for e in range(2):
                act.wait_ge(self.seg, e + 1)
                nc.scalar.activation(self.e[e], self.e[e], ACT.Exp).then_inc(self.dec, 1)
            window.trig(act)
            with act.Fori(0, LEVELS - 1) as v:
                for e in range(2):
                    act.wait_ge(self.lt, v * 2 + (e + 3))
                    nc.scalar.copy(self.LT[e][:, 0:4, :], view_bank(4 * e, 4, P)).then_inc(self.lt0_done, 1)
            for e in range(2):
                act.wait_ge(self.u0, e + 1)
                nc.scalar.copy(self.wT[e], view_bank(4 * e + 1, 4, P)[0:HD2]).then_inc(self.wT_done, 1)
            for e in range(2):
                act.wait_ge(self.out_done, e + 1)
                nc.scalar.copy(br[:, :, 256 * e:256 * (e + 1)], view_bank(4 * e, TT, 256))
            act.drain()
            act.sem_inc(self.copied, 1)

        def dve(self, dve, l):
            V = nc.vector
            dve.wait_ge(cols_par, COLS_PAR)
            a = view(small, 200, TT, H2)
            V.tensor_tensor(a, ab_2[:, :, 0:H2], bc(dt_bias2.unsqueeze(1), [P, TT, H2]), ALU.add)
            dve.drain()
            V.scalar_tensor_tensor(out=self.sp_, in0=a, scalar=-1.0, in1=a, op0=ALU.mult, op1=ALU.max).then_inc(self.ab_abs, 1)
            window.angles(dve)
            dve.wait_ge(self.cw_done, 1)
            self.convolve.dve(dve, L2)
            dve.wait_ge(self.ab_log, 1)
            V.scalar_tensor_tensor(out=a, in0=a, scalar=0.0, in1=self.sp_, op0=ALU.max, op1=ALU.add)
            dve.drain()
            V.scalar_tensor_tensor(out=self.tab[:, 0], in0=a, scalar=-1.0, in1=bc(self.anu.unsqueeze(1), [P, TT, H2]), op0=ALU.mult, op1=ALU.mult).then_inc(self.decay, 1)
            dve.wait_ge(self.cum, 1)
            G = view_bank(6, 2, TT, H2)
            V.tensor_copy(self.tab[:, 1], G[:, 0])
            dve.drain()
            V.tensor_tensor(self.gend, G[:, 1], self.tab[:, 1], ALU.subtract)
            dve.drain()
            dve.sem_inc(self.cums, 1)
            dve.wait_ge(self.tok_done, 1)
            sq = view(m3, 0, TT, 16, HD2)
            for t in range(TT):
                qk = self.tok[:, t, 0:1024].rearrange("p (h d) -> p h d", d=HD2)
                V.tensor_tensor(sq[:, t], qk, qk, ALU.mult)
            dve.drain()
            V.tensor_reduce(self.ss, sq.rearrange("p t h d -> p (t h) d"), AX.X, ALU.add)
            dve.drain()
            V.tensor_scalar(self.ss, self.ss, RMS_EPS, None, ALU.add).then_inc(pow_asked, 1)
            dve.wait_ge(self.exps, 1)
            V.tensor_tensor(self.tab[:, 4], self.tab[:, 2], self.tab[:, 3], ALU.mult)
            dve.wait_ge(pow_done, power(L2, 1))
            r2 = self.rs_.rearrange("p (t h) -> p t h", t=TT)
            V.tensor_scalar(r2[:, :, 0:H2], r2[:, :, 0:H2], HD2 ** -0.5, None, ALU.mult)
            dve.drain()
            for t in range(TT):
                qk = self.tok[:, t, 0:1024].rearrange("p (h d) -> p h d", d=HD2)
                V.tensor_tensor(qk, qk, bc(r2[:, t, :].unsqueeze(2), [P, 16, HD2]), ALU.mult)
            dve.drain()
            dve.sem_inc(self.unit, 1)
            self.multiples(V, ((self.kb, self.k_, 2), (self.qg, self.q_, 3)))
            dve.drain()
            dve.sem_inc(self.scaled, 1)
            big = lambda b: ps[:, b:b + 2, :].rearrange("p a (h n) -> p (a h) n", n=P)
            for e in range(2):
                dve.wait_ge(self.split, e + 1)
                V.tensor_copy(self.kbT[e], big(2)[0:HD2])
                V.tensor_copy(self.qT[e], big(4)[0:HD2]).then_inc(self.splitT, 1)
            lev = consts[:, CONSTS["level1"][0]:CONSTS["level1"][0] + LEVELS * P].rearrange("p (v n) -> p v n", n=P)
            dve.wait_ge(self.scaled2, 1)
            for e in range(2):
                dve.wait_ge(self.gram, e + 1)
                for s in range(8):
                    t, h = divmod(s, 4)
                    ins = V.tensor_scalar(self.e[e][:, s, :], ps[:, t, h * P:(h + 1) * P], self.tab[:, 1, t, 4 * e + h:4 * e + h + 1], 0.0, ALU.subtract, ALU.min)
                ins.then_inc(self.seg, 1)
                dve.wait_ge(self.dec, e + 1)
                V.tensor_tensor(self.e[e], self.e[e], bc(const("upto").unsqueeze(1), [P, 8, P]), ALU.mult)
                dve.drain()
                V.tensor_tensor(self.mT[e], self.e[e], big(2), ALU.mult)
                V.tensor_tensor(self.aT[e], self.e[e], big(4), ALU.mult).then_inc(self.mats, 1)
            dve.drain()
            for e in range(2):
                V.tensor_tensor(self.LmT[e], self.mT[e], bc(lev[:, 0:1, :], [P, 8, P]), ALU.mult).then_inc(self.level, 1)
            eye = bc(ident.unsqueeze(1), [P, 8, P])

            def copy_lt(e):
                V.tensor_copy(self.LT[e][:, 4:8, :], view_bank(4 * e + 1, 4, P)).then_inc(self.lt1_done, 1)

            def next_level(e, mask):
                V.tensor_tensor(self.LmT[e], self.mT[e], bc(mask, [P, 8, P]), ALU.mult)
                dve.drain()
                dve.sem_inc(self.level, 1)
            for e in range(2):
                dve.wait_ge(self.lt, e + 1)
                V.tensor_tensor(self.T[e], eye, big(4 * e), ALU.subtract)
                V.tensor_tensor(self.Tt[e], eye, self.LmT[e], ALU.subtract)
                dve.drain()
                next_level(e, lev[:, 1:2, :])
            with dve.Fori(0, LEVELS - 2) as v:
                for e in range(2):
                    dve.wait_ge(self.lt, v * 2 + (e + 3))
                    copy_lt(e)
                for e in range(2):
                    dve.wait_ge(self.upd, v * 2 + (e + 1))
                    V.tensor_tensor(self.T[e], self.T[e], big(4 * e + 2), ALU.subtract)
                    V.tensor_tensor(self.Tt[e], self.Tt[e], big(4 * e), ALU.subtract)
                    next_level(e, lev[:, bass.ds(v + 2, 1), :])
            for e in range(2):
                dve.wait_ge(self.lt, LEVELS * 2 + e - 1)
                copy_lt(e)
            for e in range(2):
                dve.wait_ge(self.upd, LEVELS * 2 + e - 3)
                V.tensor_tensor(self.Tt[e], self.Tt[e], big(4 * e), ALU.subtract)
                dve.drain()
                dve.sem_inc(self.level, 1)
            for e in range(2):
                dve.wait_ge(self.u0, e + 1)
                V.tensor_copy(self.vn[e][:, 0:4, :], ps[:, 4 * e, 0:256].rearrange("p (h n) -> p h n", n=HD2)).then_inc(self.u0_done, 1)
            for e in range(2):
                dve.wait_ge(self.state, e + 1)
                s = ps[0:HD2, 4 * e + 2, 0:256].rearrange("p (h n) -> p h n", n=HD2)
                V.tensor_copy(self.st[e], s)
                V.tensor_scalar(self.stn[e], s, -1.0, None, ALU.mult).then_inc(self.state_done, 1)
            for e in range(2):
                dve.wait_ge(self.vnew, e + 1)
                V.tensor_copy(self.vn[e][:, 4:8, :], ps[:, 4 * e + 3, 0:256].rearrange("p (h n) -> p h n", n=HD2)).then_inc(self.vnew_done, 1)
            dve.wait_ge(self.copied, 1)
            o = br[:, :, 0:G2W]
            sq = view(m3, 0, TT, G2W)
            V.tensor_tensor(sq, o, o, ALU.mult)
            dve.drain()
            V.tensor_reduce(self.ss[:, 0:16], sq.rearrange("p t (h d) -> p (t h) d", d=HD2), AX.X, ALU.add)
            dve.drain()
            V.tensor_scalar(self.ss[:, 0:16], self.ss[:, 0:16], 1.0 / HD2, RMS_EPS, ALU.mult, ALU.add).then_inc(pow_asked, 1)
            dve.wait_ge(pow_done, power(L2, 2))
            for t in range(TT):
                oh = o[:, t, :].rearrange("p (h d) -> p h d", d=HD2)
                V.tensor_tensor(oh, oh, bc(self.rs_[:, t * H2:(t + 1) * H2].unsqueeze(2), [P, H2, HD2]), ALU.mult)
            dve.drain()
            for t in range(TT):
                oh = o[:, t, :].rearrange("p (h d) -> p h d", d=HD2)
                V.tensor_tensor(oh, oh, bc(out_norm2.unsqueeze(1), [P, H2, HD2]), ALU.mult)
            dve.drain()
            V.tensor_tensor(o, o, z_2, ALU.mult)

    class WindowAttention:
        roped, angles_done, trig_done = sem("s_roped"), sem("s_angles"), sem("s_trig")
        turned, qT_done, kT_done, scored, masked, exped = (sem(f"s_{n}") for n in ("turned", "qT", "kT", "scored", "masked", "exped"))
        weighed, w_turned, wT_done, out_done, ready = (sem(f"s_{n}") for n in ("weighed", "w_turned", "wT", "out", "ready"))
        HEADS = H2 + KV2
        qk = view(m2, 0, TT, HEADS, HD2)
        sq = view(m3, 0, TT, HEADS, HD2)
        half = HD2 // 2
        GQ = H2 // KV2
        s0 = [view(work, 1280 + 1536 * g, H2 // KV2, P) for g in range(2)]
        s1 = [view(work, 1792 + 1536 * g, H2 // KV2, TOK) for g in range(2)]
        wT = [view(work, 4352 + 1536 * g, 3 * (H2 // KV2), P) for g in range(2)]
        qT = [view(m4, 1280 * g, H2 // KV2, TOK)[0:HD2] for g in range(2)]
        kT = [m4[0:HD2, 1280 * g + 1024:1280 * (g + 1)] for g in range(2)]
        bank = (5, 0)
        ss, rs_ = small[:, 0:20], small[:, 20:40]
        nmx, sums, esink, inv = ([view(small, 48 + 8 * (2 * i + g), TT, H2 // KV2) for g in range(2)] for i in range(4))
        ang, turns = (view(sil[:, i, :], 0, 2, TT, HD2 // 2) for i in range(2))
        toT = ToFeatures(br, brT, 1)

        def pool(self, pool, l):
            pool.wait_ge(pow_asked, power(L2, 3))
            nc.gpsimd.tensor_tensor(self.rs_, self.ss, const("minus_half")[:, 0:20], ALU.pow).then_inc(pow_done, 1)

        def pe(self, pe, l):
            pe.wait_ge(self.roped, 1)
            carry(pe)
            for g in range(KV2):
                for h in range(self.GQ):
                    for t in range(TT):
                        at = (h % 2) * TOK + t * P
                        pe.transpose(ps[0:HD2, 2 * g + h // 2, at:at + P], self.qk[:, t, g * self.GQ + h, :], ident)
                for t in range(TT):
                    ins = pe.transpose(ps[0:HD2, 4 + g, t * P:(t + 1) * P], self.qk[:, t, H2 + g, :], ident)
                ins.then_inc(self.turned, 1)
            for g in range(KV2):
                b = self.bank[g]
                pe.wait_ge(self.qT_done, g + 1)
                pe.wait_ge(self.kT_done, KV2)
                for h in range(self.GQ):
                    pe.matmul(ps[:, b, h * P:(h + 1) * P], self.qT[g][:, h, 0:P], self.kT[g][:, 0:P], start=True, stop=True)
                    ins = pe.matmul(ps[:, b + 1 + h // 2, (h % 2) * TOK:(h % 2 + 1) * TOK], self.qT[g][:, h, P:TOK], self.kT[g], start=True, stop=True)
                ins.then_inc(self.scored, 1)
            for g in range(KV2):
                b = self.bank[g]
                pe.wait_ge(self.weighed, g + 1)
                for h in range(self.GQ):
                    pe.transpose(ps[:, b, h * P:(h + 1) * P], self.s0[g][:, h, :], ident)
                    for n in range(2):
                        ins = pe.transpose(ps[:, b + 1 + n, h * P:(h + 1) * P], self.s1[g][:, h, n * P:(n + 1) * P], ident)
                ins.then_inc(self.w_turned, 1)
            for g in range(KV2):
                wT, v = self.wT[g], kv_s[:, :, (KV2 + g) * HD2:(KV2 + g + 1) * HD2]
                pe.wait_ge(self.wT_done, g + 1)
                for h in range(self.GQ):
                    o0, o1 = (ps[:, 3 + g, 256 * t + h * HD2:256 * t + (h + 1) * HD2] for t in range(TT))
                    pe.matmul(o0, wT[:, h, :], v[:, 0, :], start=True, stop=True)
                    pe.matmul(o1, wT[:, 4 + h, :], v[:, 0, :], start=True, stop=False)
                    ins = pe.matmul(o1, wT[:, 8 + h, :], v[:, 1, :], start=False, stop=True)
                ins.then_inc(self.out_done, 1)
            pe.wait_ge(self.ready, 1)
            self.toT.pe(pe, L2)

        def trig(self, act):
            act.wait_ge(self.angles_done, 1)
            nc.scalar.activation(trig, self.ang, ACT.Sin).then_inc(self.trig_done, 1)

        def act(self, act, l):
            for g in range(KV2):
                act.wait_ge(self.turned, g + 1)
                nc.scalar.mul(self.qT[g], ps[0:HD2, 2 * g:2 * g + 2, :].rearrange("p a (h n) -> p (a h) n", n=TOK), HD2 ** -0.5).then_inc(self.qT_done, 1)
            for g in range(KV2):
                act.wait_ge(self.masked, g + 1)
                for h in range(self.GQ):
                    for t, s in enumerate((self.s0[g], self.s1[g])):
                        nc.scalar.activation(s[:, h, :], s[:, h, :], ACT.Exp, bias=self.nmx[g][:, t, h:h + 1], accum_out=self.sums[g][:, t, h:h + 1])
                nc.scalar.activation(self.esink[g], self.esink[g], ACT.Exp).then_inc(self.exped, 1)
            for g in range(KV2):
                act.wait_ge(self.w_turned, g + 1)
                nc.scalar.copy(self.wT[g], ps[:, self.bank[g]:self.bank[g] + 3, :].rearrange("p a (h n) -> p (a h) n", n=P)).then_inc(self.wT_done, 1)
            for g in range(KV2):
                act.wait_ge(self.out_done, g + 1)
                nc.scalar.copy(br[:, :, G2W + 256 * g:G2W + 256 * (g + 1)], view_bank(3 + g, TT, 256))
            act.drain()
            act.sem_inc(self.ready, 1)
            self.toT.act(act, L2)

        def angles(self, dve):
            V = nc.vector
            dve.wait_ge(cols_par, COLS_PAR)
            V.tensor_copy(pos_f, pos_i[:])
            dve.drain()
            for t in range(TT):
                V.tensor_scalar(self.ang[:, 1, t, :], const("inv_freq"), pos_f[:, t:t + 1], None, ALU.mult)
            dve.drain()
            magic = 1.5 * 2.0 ** 23
            a1, a0 = self.ang[:, 1], self.ang[:, 0]
            V.tensor_scalar(self.turns[:, 0], a1, 0.5 / np.pi, 0.25, ALU.mult, ALU.add)
            V.tensor_scalar(self.turns[:, 1], a1, 0.5 / np.pi, None, ALU.mult)
            V.tensor_copy(a0, a1)
            dve.drain()
            V.tensor_scalar(self.turns, self.turns, magic, None, ALU.add)
            dve.drain()
            V.tensor_scalar(self.turns, self.turns, magic, None, ALU.subtract)
            dve.drain()
            rest = 2.0 * np.pi
            flat = lambda ap: ap.rearrange("p a t n -> p (a t n)")
            for bits in (2.0 ** 5, 2.0 ** 17, None):
                part = rest if bits is None else np.floor(rest * bits) / bits
                rest -= part
                V.scalar_tensor_tensor(out=flat(self.ang), in0=flat(self.turns), scalar=-float(part), in1=flat(self.ang), op0=ALU.mult, op1=ALU.add)
                dve.drain()
            V.tensor_scalar(a0, a0, 0.5 * np.pi, None, ALU.add)
            dve.drain()
            V.tensor_scalar(flat(self.ang), flat(self.ang), 3.1415925, -3.1415925, ALU.min, ALU.max).then_inc(self.angles_done, 1)

        def dve(self, dve, l):
            V = nc.vector
            heads = lambda ap: ap.rearrange("p t (h d) -> p t h d", d=HD2)
            qh, kh = heads(q_s), heads(kv_s[:, :, 0:KV2 * HD2])
            V.tensor_tensor(self.sq[:, :, 0:H2, :], qh, qh, ALU.mult)
            V.tensor_tensor(self.sq[:, :, H2:, :], kh, kh, ALU.mult)
            dve.drain()
            V.tensor_reduce(self.ss, self.sq.rearrange("p t h d -> p (t h) d"), AX.X, ALU.add)
            dve.drain()
            V.tensor_scalar(self.ss, self.ss, 1.0 / HD2, RMS_EPS, ALU.mult, ALU.add).then_inc(pow_asked, 1)
            dve.wait_ge(pow_done, power(L2, 3))
            r = self.rs_.rearrange("p (t h) -> p t h", t=TT)
            for t in range(TT):
                V.tensor_tensor(self.qk[:, t, 0:H2, :], qh[:, t], bc(r[:, t, 0:H2].unsqueeze(2), [P, H2, HD2]), ALU.mult)
                V.tensor_tensor(self.qk[:, t, H2:, :], kh[:, t], bc(r[:, t, H2:].unsqueeze(2), [P, KV2, HD2]), ALU.mult)
            dve.drain()
            for t in range(TT):
                V.tensor_tensor(self.qk[:, t, 0:H2, :], self.qk[:, t, 0:H2, :], bc(q_norm2.unsqueeze(1), [P, H2, HD2]), ALU.mult)
                V.tensor_tensor(self.qk[:, t, H2:, :], self.qk[:, t, H2:, :], bc(k_norm2.unsqueeze(1), [P, KV2, HD2]), ALU.mult)
            dve.wait_ge(self.trig_done, 1)
            dve.drain()
            for t in range(TT):
                a, b = self.qk[:, t, :, 0:self.half], self.qk[:, t, :, self.half:]
                cos, sin = (bc(trig[:, c, t, :].unsqueeze(1), [P, self.HEADS, self.half]) for c in range(2))
                ac, bs, bcs, as_ = (view(m3, 320 * i, self.HEADS, self.half) for i in range(4))
                V.tensor_tensor(ac, a, cos, ALU.mult)
                V.tensor_tensor(bs, b, sin, ALU.mult)
                V.tensor_tensor(bcs, b, cos, ALU.mult)
                V.tensor_tensor(as_, a, sin, ALU.mult)
                dve.drain()
                V.tensor_tensor(a, ac, bs, ALU.subtract)
                V.tensor_tensor(b, bcs, as_, ALU.add)
                dve.drain()
            dve.sem_inc(self.roped, 1)
            causal, window = (bc(const(n).unsqueeze(1), [P, self.GQ, P]) for n in ("causal_add", "window_add"))
            for g in range(KV2):
                dve.wait_ge(self.turned, g + 1)
                V.tensor_copy(self.kT[g], ps[0:HD2, 4 + g, 0:TOK]).then_inc(self.kT_done, 1)
            for g in range(KV2):
                s0, s1, nmx = self.s0[g], self.s1[g], self.nmx[g]
                dve.wait_ge(self.scored, g + 1)
                own = ps[:, self.bank[g] + 1:self.bank[g] + 3, :].rearrange("p a (h n) -> p (a h) n", n=TOK)
                V.tensor_tensor(s0, view_bank(self.bank[g], self.GQ, P), causal, ALU.add)
                V.tensor_tensor(s1[:, :, 0:P], own[:, :, 0:P], window, ALU.add)
                V.tensor_tensor(s1[:, :, P:TOK], own[:, :, P:TOK], causal, ALU.add)
                dve.drain()
                V.tensor_reduce(nmx[:, 0, :], s0, AX.X, ALU.max)
                V.tensor_reduce(nmx[:, 1, :], s1, AX.X, ALU.max)
                dve.drain()
                sink = bc(sinks2[:, self.GQ * g:self.GQ * (g + 1)].unsqueeze(1), [P, TT, self.GQ])
                V.tensor_tensor(nmx, nmx, sink, ALU.max)
                dve.drain()
                V.tensor_scalar(nmx, nmx, -1.0, None, ALU.mult)
                dve.drain()
                V.tensor_tensor(self.esink[g], nmx, sink, ALU.add)
                dve.drain()
                dve.sem_inc(self.masked, 1)
            for g in range(KV2):
                inv = self.inv[g]
                dve.wait_ge(self.exped, g + 1)
                V.tensor_tensor(inv, self.sums[g], self.esink[g], ALU.add)
                dve.drain()
                V.reciprocal(inv, inv)
                dve.drain()
                V.tensor_tensor(self.s0[g], self.s0[g], bc(inv[:, 0, :].unsqueeze(2), [P, self.GQ, P]), ALU.mult)
                V.tensor_tensor(self.s1[g], self.s1[g], bc(inv[:, 1, :].unsqueeze(2), [P, self.GQ, TOK]), ALU.mult).then_inc(self.weighed, 1)
            self.toT.dve(dve, L2)

    combine = view(vecs, 1000, TT, EXPERTS)

    class Router:
        logits_done, maxed, exped, diffed, exped2, combined = (sem(f"r_{n}") for n in ("logits", "maxed", "exped", "diffed", "exped2", "combined"))
        lg = view(m2, 0, TT, ROUTE)
        sub = view(m2, 80, TT, GROUPS)
        hot = view(m2, 100, TT, GROUPS)
        cnt = view(m2, 120, TT, PER_GROUP)
        prod = view(m2, 160, TT, GROUPS, PER_GROUP)
        ing, hot1, hot2, tmp = (view(m2, 256 + 16 * i, TT, PER_GROUP) for i in range(4))
        gm, gs, m1_, m2_, e2, w1, w2 = (m2[:, 340 + 2 * i:342 + 2 * i] for i in range(7))

        def pe(self, pe, l):
            for t in range(TT):
                for k in range(KT):
                    for j in range(2):
                        stat = xT[j][:, k, t * P:(t + 1) * P].bitcast(F32)
                        ins = pe.matmul(ps[:, 4, t * ROUTE:(t + 1) * ROUTE], stat, router_w[:, k, :], start=(k == 0 and j == 0),
                                        stop=(k == KT - 1 and j == 1))
            ins.then_inc(self.logits_done, 1)

        def act(self, act, l):
            round_block(act, Block(l, 0, Q_MOE))
            act.wait_ge(self.maxed, 1)
            nc.scalar.activation(self.sub, self.sub, ACT.Exp).then_inc(self.exped, 1)
            act.wait_ge(self.diffed, 1)
            nc.scalar.activation(self.e2, self.e2, ACT.Exp).then_inc(self.exped2, 1)
            act.wait_ge(self.combined, 1)

        def first_of(self, dve, hot, values, top, n):
            V = nc.vector
            V.tensor_tensor(hot, values, bc(top.unsqueeze(2), [P, TT, n]), ALU.is_equal)
            dve.drain()
            for t in range(TT):
                V.tensor_tensor_scan(self.cnt[:, t, 0:n], const("ones")[:, 0:n], hot[:, t, :], 0.0, ALU.mult, ALU.add)
            dve.drain()
            V.scalar_tensor_tensor(out=hot, in0=self.cnt[:, :, 0:n], scalar=1.0, in1=hot, op0=ALU.is_equal, op1=ALU.mult)
            dve.drain()

        def dve(self, dve, l):
            V = nc.vector
            dve.wait_ge(self.logits_done, 1)
            V.tensor_tensor(self.lg, view_bank(4, TT, ROUTE), bc(router_b.unsqueeze(1), [P, TT, ROUTE]), ALU.add)
            rest_of_block(dve, Block(l, 0, Q_MOE))
            dve.drain()
            gl = self.lg[:, :, 0:GROUPS]
            V.tensor_reduce(self.gm, gl, AX.X, ALU.max)
            dve.drain()
            V.tensor_tensor(self.sub, gl, bc(self.gm.unsqueeze(2), [P, TT, GROUPS]), ALU.subtract).then_inc(self.maxed, 1)
            self.first_of(dve, self.hot, gl, self.gm, GROUPS)
            for t in range(TT):
                V.tensor_tensor(self.prod[:, t], self.lg[:, t, GROUPS:].rearrange("p (g e) -> p g e", g=GROUPS),
                                bc(self.hot[:, t, :].unsqueeze(2), [P, GROUPS, PER_GROUP]), ALU.mult)
            dve.drain()
            for t in range(TT):
                V.tensor_reduce(self.ing[:, t, :], self.prod[:, t].rearrange("p g e -> p e g"), AX.X, ALU.add)
            dve.drain()
            V.tensor_reduce(self.m1_, self.ing, AX.X, ALU.max)
            dve.drain()
            self.first_of(dve, self.hot1, self.ing, self.m1_, PER_GROUP)
            V.scalar_tensor_tensor(out=self.tmp, in0=self.hot1, scalar=NEG, in1=self.ing, op0=ALU.mult, op1=ALU.add)
            dve.drain()
            V.tensor_reduce(self.m2_, self.tmp, AX.X, ALU.max)
            dve.drain()
            V.tensor_tensor(self.e2, self.m2_, self.m1_, ALU.subtract).then_inc(self.diffed, 1)
            self.first_of(dve, self.hot2, self.tmp, self.m2_, PER_GROUP)
            dve.wait_ge(self.exped, 1)
            V.tensor_reduce(self.gs, self.sub, AX.X, ALU.add)
            dve.wait_ge(self.exped2, 1)
            V.tensor_scalar(self.w1, self.e2, 1.0, None, ALU.add)
            dve.drain()
            V.tensor_tensor(self.w1, self.w1, self.gs, ALU.mult)
            dve.drain()
            V.reciprocal(self.w1, self.w1)
            dve.drain()
            V.tensor_tensor(self.w2, self.w1, self.e2, ALU.mult)
            dve.drain()
            V.tensor_tensor(self.hot1, self.hot1, bc(self.w1.unsqueeze(2), [P, TT, PER_GROUP]), ALU.mult)
            V.tensor_tensor(self.hot2, self.hot2, bc(self.w2.unsqueeze(2), [P, TT, PER_GROUP]), ALU.mult)
            dve.drain()
            V.tensor_tensor(self.hot1, self.hot1, self.hot2, ALU.add)
            dve.drain()
            for t in range(TT):
                ins = V.tensor_tensor(combine[:, t, :].rearrange("p (g e) -> p g e", g=GROUPS), bc(self.hot1[:, t:t + 1, :], [P, GROUPS, PER_GROUP]),
                                bc(self.hot[:, t, :].unsqueeze(2), [P, GROUPS, PER_GROUP]), ALU.mult)
            ins.then_inc(self.combined, 1)

    def expert_in(l, u):
        return tuple(A[n][0, bass.ds(u, 1)].rearrange("z (k p) n -> p (z k) n", p=P) for n in ("w_gate_2", "w_up_2"))

    def expert_out(l, u):
        return A["w_down_2"][0, bass.ds(u, 1)].rearrange("z (k p) n -> p (z k) n", p=P)

    experts = Gated(EXPERTS, Q_MOE, 0, expert_in, expert_out, weight=lambda t, u: combine[:, t, bass.ds(u, 1)], prepared=True)
    modulation, delta, window, router = Modulation(), DeltaRule(), WindowAttention(), Router()
    mod_mix, mod_ffn = Modulate(0, 0, 0), Modulate(1, 4, 2)
    out_2 = OutProduct(Q_W2, lambda l: A["w_out_2"].rearrange("z k n -> (z k) n"))

    class Last:

        def dve(self, dve, l):
            mod_ffn.add_gated(dve, 1)

    last = Last()
    SECOND = [(modulation,), (mod_mix,), (proj_2,), (delta,), (window,), (out_2,), (mod_ffn,), (router, experts), (last,)]

    in_par, consts_par = sem("in_par"), sem("consts_par")
    assert CONSTS["ident"] == (0, P)
    zeroed = sem("zeroed")
    stored = sem("stored")
    block = ctx.enter_context(nc.Block())

    @block.sync
    def _(sp):
        sp.dma_start(ident, A["shape_constants"][:, 0:P]).then_inc(in_par, 16)
        sp.dma_start(x[:], A["x"].rearrange("b (t p) d -> p (b t) d", p=P)).then_inc(in_par, 16)
        with sp.Fori(0, LAYERS) as l:
            for phase in (ffn1, proj_a, merge_a, proj_c):
                phase.sp(sp, l)
            pieces.sp(sp, l, range(ADA_C))
            for phase in (merge_c, proj_b):
                phase.sp(sp, l)
            pieces.sp(sp, l, range(ADA_C, ADA_LAYER))
            for phase in (merge_b, out_product, ffn2):
                phase.sp(sp, l)
        for phase in (proj_2, out_2, experts):
            phase.sp(sp, L2)
        sp.wait_ge(phase_left, (LAYERS * PHASES + len(SECOND) + 1) * 4)
        sp.dma_start(out.rearrange("b (t p) d -> p (b t) d", p=P), x[:]).then_inc(stored, 16)
        sp.wait_ge(stored, 16)

    @block.tensor
    def _(pe):
        pe.sem_inc(blk, BLK0)
        pe.sem_inc(dn, DN0)
        pe.sem_inc(hid_turned, 2)
        for s in (diff.out_done, stick.out_done, stick.scored):
            pe.sem_inc(s, 2)
        pe.sem_inc(diff.turned, 3)
        pe.wait_ge(in_par, 32)
        pe.wait_ge(zeroed, 1)
        turn_x.pe(pe, 0)
        pieces.turn_pe(pe)
        leave(pe, 0)
        with pe.Fori(0, LAYERS) as l:
            for n, phase in enumerate(LAYER):
                for step in phase:
                    step.pe(pe, l)
                leave(pe, l * PHASES + n + 1)
        for n, phase in enumerate(SECOND):
            for step in phase:
                if step is not last:
                    step.pe(pe, L2)
            leave(pe, LAYERS * PHASES + n + 1)

    @block.scalar
    def _(act):
        pieces.load(act)
        act.sem_inc(copied[0], 2)
        turn_x.act(act, 0)
        pieces.turn_act(act)
        leave(act, 0)
        with act.Fori(0, LAYERS) as l:
            for n, phase in enumerate(LAYER):
                for step in phase:
                    step.act(act, l)
                leave(act, l * PHASES + n + 1)
        for n, phase in enumerate(SECOND):
            for step in phase:
                if step is not last:
                    step.act(act, L2)
            leave(act, LAYERS * PHASES + n + 1)

    @block.vector
    def _(dve):
        dve.sem_inc(hid_done, 2)
        dve.sem_inc(hidT_done, 2)
        dve.sem_inc(wide_split, WS0)
        dve.sem_inc(down_split, DS0)
        dve.sem_inc(copied[1], 2)
        dve.sem_inc(diff.out_copied, 2)
        dve.sem_inc(pieces.used, 2)
        nc.vector.memset(zrow[:], 0.0).then_inc(zeroed, 1)
        turn_x.dve(dve, 0)
        leave(dve, 0)
        with dve.Fori(0, LAYERS) as l:
            for n, phase in enumerate(LAYER):
                for step in phase:
                    step.dve(dve, l)
                leave(dve, l * PHASES + n + 1)
        for n, phase in enumerate(SECOND):
            for step in phase:
                step.dve(dve, L2)
            leave(dve, LAYERS * PHASES + n + 1)

    @block.gpsimd
    def _(pool):
        pool.wait_ge(in_par, 32)
        leave(pool, 0)
        pool.dma_start(consts[:, P:], A["shape_constants"][:, P:]).then_inc(consts_par, 16)
        pool.wait_ge(consts_par, 16)
        carry(pool)
        with pool.Fori(0, LAYERS) as l:
            for n, phase in enumerate(LAYER):
                for step in phase:
                    if step is ffn1:
                        norm1.load(pool, l)
                    elif step is proj_a:
                        norm2.load(pool, l)
                        diff.load(pool, l)
                    elif step is proj_b:
                        pool.wait_ge(half_added, merge_c.added(l, 1))
                        carry(pool)
                        scan.load(pool, l)
                    elif step is ffn2:
                        norm3.load(pool, l)
                    elif step in (merge_a, merge_c, merge_b):
                        step.load(pool, l)
                    if step in (norm1, norm2, norm3, diff, stick, scan):
                        step.pool(pool, l)
                leave(pool, l * PHASES + n + 1)
        for n, phase in enumerate(SECOND):
            for step in phase:
                if step is proj_2:
                    load_second(pool)
                    delta.load(pool, L2)
                if step in (mod_mix, delta, window, mod_ffn):
                    step.pool(pool, L2)
            leave(pool, LAYERS * PHASES + n + 1)

    ctx.close()


NAMES = ["x", "ffn1_w_in", "ffn1_w_out", "ln1_g", "ln1_b", "w_mix_in", "gate_bias", "diff_lambda", "diff_subln_g",
         "ssm_conv_w", "ssm_conv_b", "ssm_dt_bias", "ssm_A_log", "ssm_D", "ssm_norm_g", "w_branch", "w_mix_out",
         "ln2_g", "ln2_b", "ffn2_w_in", "ffn2_w_out", "ln3_g", "ln3_b", "c_2", "positions_2", "w_ada_2", "b_ada_2",
         "norm_mix_2", "w_in_2", "conv_w_2", "a_log_2", "dt_bias_2", "gdn_out_norm_2", "q_norm_2", "k_norm_2",
         "sinks_2", "w_out_2", "norm_ffn_2", "w_group_2", "b_group_2", "w_router_2", "b_router_2", "w_gate_2",
         "w_up_2", "w_down_2"]


def kernel(**inputs):
    import concourse.bacc as bacc
    from concourse.bass_utils import run_bass_kernel_spmd
    arrays = {n: np.ascontiguousarray(inputs[n]) for n in NAMES}
    arrays["shape_constants"] = SHAPE_CONSTANTS
    nc = bacc.Bacc("TRN2", target_bir_lowering=False, num_devices=1)
    aps = {n: nc.dram_tensor(f"in_{n}", a.shape, mybir.dt.from_np(a.dtype), kind="ExternalInput").ap() for n, a in arrays.items()}
    out = nc.dram_tensor("out", (1, TOK, D), F32, kind="ExternalOutput").ap()
    build(nc, aps, out)
    r = run_bass_kernel_spmd(nc, [{f"in_{n}": a for n, a in arrays.items()}], core_ids=[0])
    return r.results[0]["out"]
```
